# Optimizing a Trainium2 kernel written in Bass

```python
import jax
import jax.numpy as jnp
from jax import lax
import numpy as np
import math
import jax, jax.numpy as jnp

D_MODEL = 2048
BATCH = 1
SEQ = 256
DEPTH = 1

MEM_LEN = 256
N_BRANCH = 4
MIX_WIDTH = D_MODEL // 4

NSA_HEAD_DIM = 64
NSA_HEADS = MIX_WIDTH // NSA_HEAD_DIM
NSA_KV_GROUPS = 2
NSA_GQA = NSA_HEADS // NSA_KV_GROUPS
NSA_N_BRANCH = 3
NSA_CMP_LEN = 32
NSA_CMP_STRIDE = 16
NSA_SEL_BLOCK = 64
NSA_N_SEL = 16
NSA_WINDOW = 512
NSA_Q_BLOCK = 128
NSA_FORCE_SCORE = 1e6

HGRN_HEAD_DIM = 128
HGRN_HEADS = MIX_WIDTH // HGRN_HEAD_DIM
HGRN_CHUNK = 64
HGRN_F_MIN = 1e-6

POOL_WINDOWS = (2, 4, 8, 16)
POOL_GROUPS = 4
POOL_GROUP_DIM = MIX_WIDTH // POOL_GROUPS

SG_CHUNK = 128
SG_HEADS = 4
SG_HEAD_DIM = MIX_WIDTH // SG_HEADS

X_HEADS = 4
X_HEAD_DIM = 128
X_WIDTH = X_HEADS * X_HEAD_DIM

D_FF = 5632
CONV_WIDTH = 3

LN_EPS = 1e-5
NEG_INF = -1e30
DEEPNORM_ALPHA = (2 * DEPTH) ** 0.25
DEEPNORM_BETA = (8 * DEPTH) ** -0.25

IN_SPLITS = (
    MIX_WIDTH,
    NSA_N_BRANCH * 2 * NSA_KV_GROUPS * NSA_HEAD_DIM,
    NSA_HEADS * NSA_N_BRANCH,
    4 * MIX_WIDTH,
    MIX_WIDTH,
    2 * MIX_WIDTH,
    N_BRANCH * D_MODEL,
)
W_IN_COLS = sum(IN_SPLITS)


def layer_norm(x, g, b):
    xf = x.astype(jnp.float32)
    mu = jnp.mean(xf, -1, keepdims=True)
    var = jnp.mean(jnp.square(xf - mu), -1, keepdims=True)
    y = (xf - mu) * lax.rsqrt(var + LN_EPS) * g.astype(jnp.float32) + b.astype(jnp.float32)
    return y.astype(x.dtype)

def rms_norm(x, g):
    xf = x.astype(jnp.float32)
    y = xf * lax.rsqrt(jnp.mean(jnp.square(xf), -1, keepdims=True) + LN_EPS) * g.astype(jnp.float32)
    return y.astype(x.dtype)

def alibi_slopes(n_heads):
    return jnp.asarray(2.0 ** (-8.0 * np.arange(1, n_heads + 1) / n_heads), dtype=jnp.float32)

def masked_softmax(s, mask, axis=-1):
    p = jax.nn.softmax(jnp.where(mask, s, NEG_INF), axis=axis)
    return jnp.where(mask, p, 0.0)

def cmp_to_sel_matrix(n_cmp, n_blk):
    c0 = np.arange(n_cmp)[:, None] * NSA_CMP_STRIDE
    s0 = np.arange(n_blk)[None, :] * NSA_SEL_BLOCK
    ov = np.clip(np.minimum(c0 + NSA_CMP_LEN, s0 + NSA_SEL_BLOCK) - np.maximum(c0, s0), 0, None)
    return jnp.asarray(ov / NSA_CMP_LEN, dtype=jnp.float32)

def nsa_mixer(q, kv, gate_logits, cmp_pos, cmp_w):
    B, S, _ = q.shape
    G, J, dh, T = NSA_KV_GROUPS, NSA_GQA, NSA_HEAD_DIM, NSA_Q_BLOCK
    f32 = jnp.float32
    q = q.reshape(B, S, G, J, dh) * dh ** -0.5
    kv = kv.reshape(B, S, NSA_N_BRANCH, 2, G, dh)
    gates = jax.nn.sigmoid(gate_logits.reshape(B, S, G, J, NSA_N_BRANCH))
    slopes = alibi_slopes(NSA_HEADS).reshape(G, J)

    n_cmp = (S - NSA_CMP_LEN) // NSA_CMP_STRIDE + 1
    blk = np.arange(n_cmp)[:, None] * NSA_CMP_STRIDE + np.arange(NSA_CMP_LEN)[None, :]

    def compress(t, pos, w):
        tb = t[:, blk] + pos[None, None, :, None, :]
        return jnp.einsum('bclgd,lde->bcge', tb, w)

    k_cmp = compress(kv[:, :, 0, 0], cmp_pos[0], cmp_w[0])
    v_cmp = compress(kv[:, :, 0, 1], cmp_pos[1], cmp_w[1])
    cmp_end = jnp.arange(n_cmp) * NSA_CMP_STRIDE + (NSA_CMP_LEN - 1)

    n_blk = S // NSA_SEL_BLOCK
    n_sel = min(NSA_N_SEL, n_blk)
    sel_map = cmp_to_sel_matrix(n_cmp, n_blk)

    def to_blocks(t):
        return t.reshape(B, n_blk, NSA_SEL_BLOCK, G, dh).transpose(0, 1, 3, 2, 4)

    k_slc = to_blocks(kv[:, :, 1, 0])
    v_slc = to_blocks(kv[:, :, 1, 1])
    blk_ids = jnp.arange(n_blk)
    in_blk = jnp.arange(NSA_SEL_BLOCK)
    b_idx = jnp.arange(B)[:, None, None, None]
    g_idx = jnp.arange(G)[None, None, :, None]

    pad = jnp.zeros((B, NSA_WINDOW, G, dh), kv.dtype)
    k_win = jnp.concatenate([pad, kv[:, :, 2, 0]], axis=1)
    v_win = jnp.concatenate([pad, kv[:, :, 2, 1]], axis=1)

    def query_block(qb):
        q0 = qb * T
        t = q0 + jnp.arange(T)
        qt = lax.dynamic_slice_in_dim(q, q0, T, axis=1)
        gt = lax.dynamic_slice_in_dim(gates, q0, T, axis=1)
        sl = slopes[None, None, :, :, None]

        dist_c = (t[:, None] - cmp_end[None, :]).astype(f32)
        mask_c = (dist_c >= 0)[None, :, None, None, :]
        s_c = jnp.einsum('btgjd,bcgd->btgjc', qt, k_cmp).astype(f32) - sl * dist_c[None, :, None, None, :]
        p_c = masked_softmax(s_c, mask_c)
        o_c = jnp.einsum('btgjc,bcgd->btgjd', p_c.astype(v_cmp.dtype), v_cmp)

        imp = jnp.einsum('btgjc,cn->btgn', p_c, sel_map)
        cur = (t // NSA_SEL_BLOCK)[:, None]
        forced = (blk_ids[None] == 0) | (blk_ids[None] == cur) | (blk_ids[None] == cur - 1)
        future = blk_ids[None] * NSA_SEL_BLOCK > t[:, None]
        imp = jnp.where(forced[None, :, None], NSA_FORCE_SCORE,
                        jnp.where(future[None, :, None], NEG_INF, imp))
        _, idx = lax.top_k(imp, n_sel)
        k_s = k_slc[b_idx, idx, g_idx]
        v_s = v_slc[b_idx, idx, g_idx]
        pos_s = idx[..., None] * NSA_SEL_BLOCK + in_blk
        dist_s = (t[None, :, None, None, None] - pos_s).astype(f32)[:, :, :, None]
        mask_s = dist_s >= 0
        s_s = (jnp.einsum('btgjd,btgnkd->btgjnk', qt, k_s).astype(f32)
               - slopes[None, None, :, :, None, None] * dist_s)
        p_s = masked_softmax(s_s, mask_s, axis=(-2, -1))
        o_s = jnp.einsum('btgjnk,btgnkd->btgjd', p_s.astype(v_s.dtype), v_s)

        k_w = lax.dynamic_slice_in_dim(k_win, q0, T + NSA_WINDOW, axis=1)
        v_w = lax.dynamic_slice_in_dim(v_win, q0, T + NSA_WINDOW, axis=1)
        pos_w = q0 - NSA_WINDOW + jnp.arange(T + NSA_WINDOW)
        dist_w = t[:, None] - pos_w[None, :]
        mask_w = ((pos_w[None] >= 0) & (dist_w >= 0) & (dist_w < NSA_WINDOW))[None, :, None, None, :]
        s_w = (jnp.einsum('btgjd,bsgd->btgjs', qt, k_w).astype(f32)
               - sl * dist_w.astype(f32)[None, :, None, None, :])
        p_w = masked_softmax(s_w, mask_w)
        o_w = jnp.einsum('btgjs,bsgd->btgjd', p_w.astype(v_w.dtype), v_w)

        o = gt[..., 0:1] * o_c + gt[..., 1:2] * o_s + gt[..., 2:3] * o_w
        return o.reshape(B, T, NSA_HEADS * dh)

    out = lax.map(query_block, jnp.arange(S // T))
    return out.transpose(1, 0, 2, 3).reshape(B, S, NSA_HEADS * dh)

def hgrn2_mixer(q, f_logit, i, g, lb, norm_g):
    B, S, _ = q.shape
    H, dk, C = HGRN_HEADS, HGRN_HEAD_DIM, HGRN_CHUNK
    n = S // C
    f32 = jnp.float32
    lbh = lb.reshape(H, dk).astype(f32)
    z = f_logit.reshape(B, S, H, dk).astype(f32)
    f = jnp.maximum(lbh + (1.0 - lbh) * jax.nn.sigmoid(z), HGRN_F_MIN)
    log_f = jnp.log(f)
    k = 1.0 - f

    def to_chunks(a):
        return a.reshape(B, n, C, H, dk).transpose(1, 0, 3, 2, 4)

    xs = (to_chunks(q.astype(f32)), to_chunks(k), to_chunks(i.astype(f32)), to_chunks(log_f))
    causal = jnp.tril(jnp.ones((C, C), dtype=bool))[:, :, None]

    def step(state, inp):
        qq, kk, vv, ll = inp
        b = jnp.cumsum(ll, axis=2)
        o_inter = jnp.einsum('bhtk,bhkv->bhtv', qq * jnp.exp(b), state)
        decay = jnp.exp(jnp.where(causal, b[:, :, :, None, :] - b[:, :, None, :, :], NEG_INF))
        a = jnp.einsum('bhtk,bhtsk,bhsk->bhts', qq, decay, kk)
        o = o_inter + jnp.einsum('bhts,bhsv->bhtv', a, vv)
        b_last = b[:, :, -1:, :]
        state = (jnp.exp(b_last[:, :, 0, :, None]) * state
                 + jnp.einsum('bhsk,bhsv->bhkv', kk * jnp.exp(b_last - b), vv))
        return state, o

    s0 = jnp.zeros((B, H, dk, dk), f32)
    _, o = lax.scan(step, s0, xs)
    o = o.transpose(1, 0, 3, 2, 4).reshape(B, S, H, dk)
    o = rms_norm(o, norm_g.reshape(H, dk)).reshape(B, S, H * dk)
    return (o * jax.nn.silu(g.astype(f32))).astype(q.dtype)

def pool_mixer(c, w, scale):
    B, S, _ = c.shape
    cf = c.astype(jnp.float32).reshape(B, S, POOL_GROUPS, POOL_GROUP_DIM)
    cs = jnp.concatenate([jnp.zeros((B, 1, POOL_GROUPS, POOL_GROUP_DIM), jnp.float32),
                          jnp.cumsum(cf, axis=1)], axis=1)
    t = jnp.arange(S)
    outs = []
    for gi, win in enumerate(POOL_WINDOWS):
        lo = jnp.maximum(t + 1 - win, 0)
        cnt = jnp.minimum(t + 1, win).astype(jnp.float32)
        mean = (cs[:, 1:, gi] - cs[:, lo, gi]) / cnt[None, :, None]
        outs.append(mean - cf[:, :, gi])
    p = jnp.stack(outs, axis=2)
    y = jnp.einsum('bsgc,gcd->bsgd', p, w.astype(jnp.float32)).reshape(B, S, MIX_WIDTH)
    return (y * scale.astype(jnp.float32)).astype(c.dtype)

def sgu_mixer(u, v, ln_g, ln_b, ws, bs):
    B, S, _ = u.shape
    n = S // SG_CHUNK
    v = layer_norm(jax.nn.gelu(v), ln_g, ln_b).reshape(B, n, SG_CHUNK, SG_HEADS, SG_HEAD_DIM)
    mask = jnp.tril(jnp.ones((SG_CHUNK, SG_CHUNK), dtype=bool))
    wm = jnp.where(mask, ws, 0.0)
    vs = jnp.einsum('gqp,bnpgc->bnqgc', wm, v) + bs.T[None, None, :, :, None]
    return jax.nn.gelu(u) * vs.reshape(B, S, MIX_WIDTH)

def cross_attention(x, mem_n, wq, wk, wv, wo):
    B, S, _ = x.shape
    M = mem_n.shape[1]
    q = (x @ wq).reshape(B, S, X_HEADS, X_HEAD_DIM)
    k = (mem_n @ wk).reshape(B, M, X_HEADS, X_HEAD_DIM)
    v = (mem_n @ wv).reshape(B, M, X_HEADS, X_HEAD_DIM)
    s = jnp.einsum('bshd,bmhd->bhsm', q, k).astype(jnp.float32) * X_HEAD_DIM ** -0.5
    p = jax.nn.softmax(s, axis=-1).astype(v.dtype)
    o = jnp.einsum('bhsm,bmhd->bshd', p, v).reshape(B, S, X_WIDTH)
    return o @ wo

def conv_ffn(x, w_in, conv_w, conv_b, w_out):
    h = x @ w_in
    gate, up = jnp.split(h, 2, axis=-1)
    gate = lax.conv_general_dilated(
        gate, conv_w[:, None, :], window_strides=(1,), padding=((CONV_WIDTH - 1, 0),),
        dimension_numbers=('NWC', 'WIO', 'NWC'), feature_group_count=D_FF) + conv_b
    return (jax.nn.silu(gate) * up) @ w_out

def first_inputs(seed: int = 0) -> dict:
    key = jax.random.key(seed)
    ks = iter(jax.random.split(key, 32))
    L, D = DEPTH, D_MODEL
    f32 = jnp.float32

    def nrm(shape, scale):
        return jax.random.normal(next(ks), shape, f32) * scale

    def gain(shape):
        return 1.0 + nrm(shape, 0.05)

    def bias(shape):
        return nrm(shape, 0.02)

    beta = DEEPNORM_BETA
    return {
        'x': nrm((BATCH, SEQ, D), 1.0),
        'mem': nrm((BATCH, MEM_LEN, D), 1.0),
        'w_in': nrm((L, D, W_IN_COLS), D ** -0.5),
        'nsa_cmp_pos': nrm((L, 2, NSA_CMP_LEN, NSA_HEAD_DIM), 0.1),
        'nsa_cmp_w': nrm((L, 2, NSA_CMP_LEN, NSA_HEAD_DIM, NSA_HEAD_DIM), (NSA_CMP_LEN * NSA_HEAD_DIM) ** -0.5),
        'hgrn_lb_logits': nrm((L, MIX_WIDTH), 1.0),
        'hgrn_norm_g': gain((L, MIX_WIDTH)),
        'pool_w': nrm((L, POOL_GROUPS, POOL_GROUP_DIM, POOL_GROUP_DIM), POOL_GROUP_DIM ** -0.5),
        'pool_scale': gain((L, MIX_WIDTH)),
        'sg_ln_g': gain((L, MIX_WIDTH)),
        'sg_ln_b': bias((L, MIX_WIDTH)),
        'sg_w': nrm((L, SG_HEADS, SG_CHUNK, SG_CHUNK), SG_CHUNK ** -0.5),
        'sg_b': gain((L, SG_HEADS, SG_CHUNK)),
        'w_branch': nrm((L, N_BRANCH, MIX_WIDTH, D), MIX_WIDTH ** -0.5),
        'w_mix_out': nrm((L, D, D), beta * D ** -0.5),
        'ln_mix_g': gain((L, D)),
        'ln_mix_b': bias((L, D)),
        'mem_ln_g': gain((D,)),
        'mem_ln_b': bias((D,)),
        'xattn_q': nrm((L, D, X_WIDTH), D ** -0.5),
        'xattn_k': nrm((L, D, X_WIDTH), D ** -0.5),
        'xattn_v': nrm((L, D, X_WIDTH), beta * D ** -0.5),
        'xattn_o': nrm((L, X_WIDTH, D), beta * X_WIDTH ** -0.5),
        'ln_x_g': gain((L, D)),
        'ln_x_b': bias((L, D)),
        'ffn_in': nrm((L, D, 2 * D_FF), D ** -0.5),
        'ffn_conv_w': nrm((L, CONV_WIDTH, D_FF), CONV_WIDTH ** -0.5),
        'ffn_conv_b': bias((L, D_FF)),
        'ffn_out': nrm((L, D_FF, D), beta * D_FF ** -0.5),
        'ln_ffn_g': gain((L, D)),
        'ln_ffn_b': bias((L, D)),
    }

def first_block(x, mem, w_in, nsa_cmp_pos, nsa_cmp_w, hgrn_lb_logits, hgrn_norm_g, pool_w, pool_scale,
              sg_ln_g, sg_ln_b, sg_w, sg_b, w_branch, w_mix_out, ln_mix_g, ln_mix_b, mem_ln_g, mem_ln_b,
              xattn_q, xattn_k, xattn_v, xattn_o, ln_x_g, ln_x_b, ffn_in, ffn_conv_w, ffn_conv_b, ffn_out,
              ln_ffn_g, ln_ffn_b):
    B, S, D = x.shape
    mem_n = layer_norm(mem, mem_ln_g, mem_ln_b)
    sm = jax.nn.softmax(hgrn_lb_logits.astype(jnp.float32), axis=0)
    lower_bounds = jnp.cumsum(sm, axis=0) - sm[0]
    split_at = [int(v) for v in np.cumsum(IN_SPLITS)[:-1]]

    for l in range(DEPTH):
        h = x @ w_in[l]
        a_q, a_kv, a_g, b_in, c_in, d_in, merge = jnp.split(h, split_at, axis=-1)
        o_a = nsa_mixer(a_q, a_kv, a_g, nsa_cmp_pos[l], nsa_cmp_w[l])
        b_q, b_f, b_i, b_g = jnp.split(b_in, 4, axis=-1)
        o_b = hgrn2_mixer(b_q, b_f, b_i, b_g, lower_bounds[l], hgrn_norm_g[l])
        o_c = pool_mixer(c_in, pool_w[l], pool_scale[l])
        d_u, d_v = jnp.split(d_in, 2, axis=-1)
        o_d = sgu_mixer(d_u, d_v, sg_ln_g[l], sg_ln_b[l], sg_w[l], sg_b[l])
        branches = jnp.stack([o_a, o_b, o_c, o_d], axis=2)
        gates = jax.nn.sigmoid(merge.reshape(B, S, N_BRANCH, D))
        y = jnp.einsum('bsnw,nwd->bsnd', branches, w_branch[l])
        mixed = jnp.sum(gates * y, axis=2) @ w_mix_out[l]
        x = layer_norm(DEEPNORM_ALPHA * x + mixed, ln_mix_g[l], ln_mix_b[l])

        xa = cross_attention(x, mem_n, xattn_q[l], xattn_k[l], xattn_v[l], xattn_o[l])
        x = layer_norm(DEEPNORM_ALPHA * x + xa, ln_x_g[l], ln_x_b[l])

        ff = conv_ffn(x, ffn_in[l], ffn_conv_w[l], ffn_conv_b[l], ffn_out[l])
        x = layer_norm(DEEPNORM_ALPHA * x + ff, ln_ffn_g[l], ln_ffn_b[l])
    return x


N_MEM = 256
MLSTM_WIDTH = D_MODEL // 2
MLSTM_HEADS = 4
MLSTM_HEAD_DIM = MLSTM_WIDTH // MLSTM_HEADS
MLSTM_CHUNK = 64
CONV_WIDTH_2 = 4
ATTN_WIDTH = D_MODEL - MLSTM_WIDTH
ATTN_HEAD_DIM = 128
ATTN_HEADS = ATTN_WIDTH // ATTN_HEAD_DIM
DILATED_PATTERNS = ((128, 1), (512, 4), (2048, 16))
ATTN_BLOCK = 128
REL_BUCKETS = 32
REL_MAX_DISTANCE = 2048
XATTN_HEADS = 4
XATTN_HEAD_DIM = D_MODEL // XATTN_HEADS
FFN_HIDDEN = -(-8 * D_MODEL // (3 * 256)) * 256
DEEPNORM_ALPHA_2 = (2 * DEPTH) ** 0.25
DEEPNORM_BETA_2 = (8 * DEPTH) ** -0.25
IN_SPLITS_2 = (MLSTM_WIDTH, MLSTM_WIDTH, MLSTM_WIDTH, MLSTM_WIDTH, MLSTM_HEADS, MLSTM_HEADS,
             ATTN_WIDTH, ATTN_WIDTH, ATTN_WIDTH)
IN_WIDTH = sum(IN_SPLITS_2)


def split_columns(a, sizes):
    bounds = np.cumsum(sizes)[:-1].tolist()
    return jnp.split(a, bounds, axis=-1)

def layer_norm_2(x, g, b):
    xf = x.astype(jnp.float32)
    mu = xf.mean(-1, keepdims=True)
    var = jnp.square(xf - mu).mean(-1, keepdims=True)
    return ((xf - mu) * lax.rsqrt(var + LN_EPS) * g + b).astype(x.dtype)

def causal_depthwise_conv(x, w, b):
    c = x.shape[-1]
    y = lax.conv_general_dilated(x, w[:, None, :].astype(x.dtype), window_strides=(1,),
                                 padding=[(CONV_WIDTH_2 - 1, 0)],
                                 dimension_numbers=('NWC', 'WIO', 'NWC'),
                                 feature_group_count=c)
    return y + b

def mlstm_chunk_step(carry, xs):
    c_state, n_state, m_state = carry
    q, k, v, log_i, log_f = xs
    L = q.shape[2]
    causal = jnp.tril(jnp.ones((L, L), dtype=bool))
    b = jnp.cumsum(log_f, axis=-1)
    d_log = jnp.where(causal, b[..., :, None] - b[..., None, :] + log_i[..., None, :], -jnp.inf)
    inter = b + m_state[..., None]
    m_row = jnp.maximum(inter, d_log.max(-1))
    s_w = jnp.exp(d_log - m_row[..., None]) * jnp.einsum('bhsd,bhrd->bhsr', q, k)
    w_inter = jnp.exp(inter - m_row)
    num = jnp.einsum('bhsr,bhre->bhse', s_w, v) + w_inter[..., None] * jnp.einsum('bhsd,bhde->bhse', q, c_state)
    den = s_w.sum(-1) + w_inter * jnp.einsum('bhsd,bhd->bhs', q, n_state)
    h = num / jnp.maximum(jnp.abs(den), jnp.exp(-m_row))[..., None]
    b_last = b[..., -1]
    g = b_last[..., None] - b + log_i
    m_new = jnp.maximum(b_last + m_state, g.max(-1))
    wk = jnp.exp(g - m_new[..., None])
    decay = jnp.exp(b_last + m_state - m_new)
    c_new = decay[..., None, None] * c_state + jnp.einsum('bhr,bhrd,bhre->bhde', wk, k, v)
    n_new = decay[..., None] * n_state + jnp.einsum('bhr,bhrd->bhd', wk, k)
    return (c_new, n_new, m_new), h

def mlstm_mixer(q_pre, k_pre, v_pre, o_pre, i_pre, f_pre, conv_w, conv_b, gate_b, mh_g):
    B, S, _ = q_pre.shape
    H, dh = MLSTM_HEADS, MLSTM_HEAD_DIM
    qk = jax.nn.silu(causal_depthwise_conv(jnp.concatenate([q_pre, k_pre], -1), conv_w, conv_b))
    q, k = jnp.split(qk, 2, axis=-1)
    heads = lambda a: a.reshape(B, S, H, dh).transpose(0, 2, 1, 3).astype(jnp.float32)
    q, k, v = heads(q), heads(k) * (dh ** -0.5), heads(v_pre)
    gates = (jnp.concatenate([i_pre, f_pre], -1) + gate_b).astype(jnp.float32)
    log_i = gates[..., :H].transpose(0, 2, 1)
    log_f = jax.nn.log_sigmoid(gates[..., H:]).transpose(0, 2, 1)
    nc = S // MLSTM_CHUNK
    chunks = lambda a: jnp.moveaxis(a.reshape(a.shape[:2] + (nc, MLSTM_CHUNK) + a.shape[3:]), 2, 0)
    init = (jnp.zeros((B, H, dh, dh), jnp.float32), jnp.zeros((B, H, dh), jnp.float32),
            jnp.zeros((B, H), jnp.float32))
    _, h = lax.scan(mlstm_chunk_step, init,
                    (chunks(q), chunks(k), chunks(v), chunks(log_i), chunks(log_f)))
    h = jnp.moveaxis(h, 0, 2).reshape(B, H, S, dh)
    mu = h.mean(-1, keepdims=True)
    var = jnp.square(h - mu).mean(-1, keepdims=True)
    hn = ((h - mu) * lax.rsqrt(var + LN_EPS)).transpose(0, 2, 1, 3).reshape(B, S, MLSTM_WIDTH) * mh_g
    return (jax.nn.sigmoid(o_pre.astype(jnp.float32)) * hn).astype(q_pre.dtype)

def t5_bucket(dist):
    exact = REL_BUCKETS // 2
    d = jnp.maximum(dist, 1).astype(jnp.float32)
    log_bucket = exact + (jnp.log(d / exact) / math.log(REL_MAX_DISTANCE / exact)
                          * (REL_BUCKETS - exact)).astype(jnp.int32)
    return jnp.where(dist < exact, dist, jnp.minimum(log_bucket, REL_BUCKETS - 1))

def dilated_pattern(q, k, v, rel_bias, window, dil):
    B, H, S, dh = q.shape
    L = S // dil
    nb = -(-L // ATTN_BLOCK)
    pad = nb * ATTN_BLOCK - L
    reach = window // dil

    def to_blocks(a):
        a = a.reshape(B, H, L, dil, dh).transpose(0, 1, 3, 2, 4)
        a = jnp.pad(a, ((0, 0), (0, 0), (0, 0), (0, pad), (0, 0)))
        return a.reshape(B, H, dil, nb, ATTN_BLOCK, dh)

    def with_prev(a):
        prev = jnp.concatenate([jnp.zeros_like(a[:, :, :, :1]), a[:, :, :, :-1]], axis=3)
        return jnp.concatenate([prev, a], axis=4)

    qb = to_blocks(q)
    kc, vc = with_prev(to_blocks(k)), with_prev(to_blocks(v))
    qi = jnp.arange(ATTN_BLOCK)[:, None]
    kj = jnp.arange(2 * ATTN_BLOCK)[None, :]
    delta = qi + ATTN_BLOCK - kj
    blk = jnp.arange(nb)[:, None, None]
    valid = (delta >= 0) & (delta <= reach) & (blk * ATTN_BLOCK + kj - ATTN_BLOCK >= 0)
    bias = rel_bias[t5_bucket(jnp.maximum(delta, 0) * dil)].transpose(2, 0, 1).astype(jnp.float32)
    s = jnp.einsum('bhrnqd,bhrnkd->bhrnqk', qb, kc) * (dh ** -0.5) + bias[:, None, None]
    s = jnp.where(valid, s, -jnp.inf)
    lse = jax.nn.logsumexp(s, axis=-1)
    p = jnp.exp(s - lse[..., None])
    o = jnp.einsum('bhrnqk,bhrnkd->bhrnqd', p, vc)
    o = o.reshape(B, H, dil, nb * ATTN_BLOCK, dh)[:, :, :, :L].transpose(0, 1, 3, 2, 4).reshape(B, H, S, dh)
    lse = lse.reshape(B, H, dil, nb * ATTN_BLOCK)[:, :, :, :L].transpose(0, 1, 3, 2).reshape(B, H, S)
    return o, lse

def dilated_attention(q_pre, k_pre, v_pre, rel_bias):
    B, S, _ = q_pre.shape
    heads = lambda a: a.reshape(B, S, ATTN_HEADS, ATTN_HEAD_DIM).transpose(0, 2, 1, 3).astype(jnp.float32)
    q, k, v = heads(q_pre), heads(k_pre), heads(v_pre)
    outs, lses = [], []
    for window, dil in DILATED_PATTERNS:
        o, lse = dilated_pattern(q, k, v, rel_bias, window, dil)
        outs.append(o)
        lses.append(lse)
    w = jax.nn.softmax(jnp.stack(lses, 0), axis=0)
    o = jnp.einsum('pbhs,pbhsd->bhsd', w, jnp.stack(outs, 0))
    return o.transpose(0, 2, 1, 3).reshape(B, S, ATTN_WIDTH).astype(q_pre.dtype)

def memory_cross_attention(x, mem, wq, wk, wv, wo):
    B, S, _ = x.shape
    M = mem.shape[1]
    q = (x @ wq).reshape(B, S, XATTN_HEADS, XATTN_HEAD_DIM)
    k = (mem @ wk).reshape(B, M, XATTN_HEADS, XATTN_HEAD_DIM)
    v = (mem @ wv).reshape(B, M, XATTN_HEADS, XATTN_HEAD_DIM)
    s = jnp.einsum('bshd,bmhd->bhsm', q, k).astype(jnp.float32) * (XATTN_HEAD_DIM ** -0.5)
    p = jax.nn.softmax(s, axis=-1)
    o = jnp.einsum('bhsm,bmhd->bshd', p, v.astype(jnp.float32)).reshape(B, S, D_MODEL).astype(x.dtype)
    return o @ wo

def swiglu_ffn(x, w1, w3, w2):
    return (jax.nn.silu(x @ w1) * (x @ w3)) @ w2

def second_inputs(seed: int = 0) -> dict:
    key = jax.random.key(seed)
    ks = jax.random.split(key, 24)
    nrm = lambda k, shape, scale: jax.random.normal(k, shape, jnp.float32) * scale
    beta = DEEPNORM_BETA_2
    col_scales = (1.0, 1.0, beta, 1.0, 1.0, 1.0, 1.0, 1.0, beta)
    col_scale = jnp.concatenate([jnp.full((n,), s, jnp.float32) for n, s in zip(IN_SPLITS_2, col_scales)])
    x = nrm(ks[0], (BATCH, SEQ, D_MODEL), 1.0)
    mem = nrm(ks[1], (BATCH, N_MEM, D_MODEL), 1.0)
    w_in = nrm(ks[2], (DEPTH, D_MODEL, IN_WIDTH), D_MODEL ** -0.5) * col_scale
    forget_init = jnp.tile(jnp.linspace(3.0, 6.0, MLSTM_HEADS, dtype=jnp.float32)[None], (DEPTH, 1))
    gate_b = jnp.concatenate([nrm(ks[3], (DEPTH, MLSTM_HEADS), 0.1),
                              forget_init + nrm(ks[4], (DEPTH, MLSTM_HEADS), 0.1)], axis=-1)
    conv_w = nrm(ks[5], (DEPTH, CONV_WIDTH_2, 2 * MLSTM_WIDTH), CONV_WIDTH_2 ** -0.5)
    conv_b = nrm(ks[6], (DEPTH, 2 * MLSTM_WIDTH), 0.02)
    mh_g = 1.0 + nrm(ks[7], (DEPTH, MLSTM_WIDTH), 0.02)
    rel_bias = nrm(ks[8], (REL_BUCKETS, ATTN_HEADS), 0.5)
    w_out = nrm(ks[9], (DEPTH, D_MODEL, D_MODEL), D_MODEL ** -0.5) * beta
    xq = nrm(ks[10], (DEPTH, D_MODEL, D_MODEL), D_MODEL ** -0.5)
    xk = nrm(ks[11], (DEPTH, D_MODEL, D_MODEL), D_MODEL ** -0.5)
    xv = nrm(ks[12], (DEPTH, D_MODEL, D_MODEL), D_MODEL ** -0.5) * beta
    xo = nrm(ks[13], (DEPTH, D_MODEL, D_MODEL), D_MODEL ** -0.5) * beta
    w1 = nrm(ks[14], (DEPTH, D_MODEL, FFN_HIDDEN), D_MODEL ** -0.5)
    w3 = nrm(ks[15], (DEPTH, D_MODEL, FFN_HIDDEN), D_MODEL ** -0.5)
    w2 = nrm(ks[16], (DEPTH, FFN_HIDDEN, D_MODEL), FFN_HIDDEN ** -0.5) * beta
    ln_g = 1.0 + nrm(ks[17], (DEPTH, 3, D_MODEL), 0.02)
    ln_b = nrm(ks[18], (DEPTH, 3, D_MODEL), 0.02)
    return {"x": x, "mem": mem, "w_in": w_in, "gate_b": gate_b, "conv_w": conv_w, "conv_b": conv_b,
            "mh_g": mh_g, "rel_bias": rel_bias, "w_out": w_out, "xq": xq, "xk": xk, "xv": xv,
            "xo": xo, "w1": w1, "w3": w3, "w2": w2, "ln_g": ln_g, "ln_b": ln_b}

def second_block(x, mem, w_in, gate_b, conv_w, conv_b, mh_g, rel_bias, w_out, xq, xk, xv, xo,
              w1, w3, w2, ln_g, ln_b):
    for l in range(DEPTH):
        proj = x @ w_in[l]
        q_m, k_m, v_m, o_m, i_m, f_m, q_a, k_a, v_a = split_columns(proj, IN_SPLITS_2)
        y_m = mlstm_mixer(q_m, k_m, v_m, o_m, i_m, f_m, conv_w[l], conv_b[l], gate_b[l], mh_g[l])
        y_a = dilated_attention(q_a, k_a, v_a, rel_bias)
        y = jnp.concatenate([y_m, y_a], axis=-1) @ w_out[l]
        x = layer_norm_2(DEEPNORM_ALPHA_2 * x + y, ln_g[l, 0], ln_b[l, 0])
        y = memory_cross_attention(x, mem, xq[l], xk[l], xv[l], xo[l])
        x = layer_norm_2(DEEPNORM_ALPHA_2 * x + y, ln_g[l, 1], ln_b[l, 1])
        y = swiglu_ffn(x, w1[l], w3[l], w2[l])
        x = layer_norm_2(DEEPNORM_ALPHA_2 * x + y, ln_g[l, 2], ln_b[l, 2])
    return x


def setup_inputs(seed=0):
    out = dict(first_inputs(seed))
    for name, value in second_inputs(seed + 1).items():
        if name != "x":
            out[name + "_2"] = value
    return out


def reference(
    x, mem, w_in, nsa_cmp_pos, nsa_cmp_w, hgrn_lb_logits, hgrn_norm_g, pool_w, pool_scale,
    sg_ln_g, sg_ln_b, sg_w, sg_b, w_branch, w_mix_out, ln_mix_g, ln_mix_b, mem_ln_g, mem_ln_b,
    xattn_q, xattn_k, xattn_v, xattn_o, ln_x_g, ln_x_b, ffn_in, ffn_conv_w, ffn_conv_b, ffn_out,
    ln_ffn_g, ln_ffn_b, mem_2, w_in_2, gate_b_2, conv_w_2, conv_b_2, mh_g_2, rel_bias_2,
    w_out_2, xq_2, xk_2, xv_2, xo_2, w1_2, w3_2, w2_2, ln_g_2, ln_b_2,
):
    x = first_block(
        x, mem, w_in, nsa_cmp_pos, nsa_cmp_w, hgrn_lb_logits, hgrn_norm_g, pool_w, pool_scale,
        sg_ln_g, sg_ln_b, sg_w, sg_b, w_branch, w_mix_out, ln_mix_g, ln_mix_b, mem_ln_g,
        mem_ln_b, xattn_q, xattn_k, xattn_v, xattn_o, ln_x_g, ln_x_b, ffn_in, ffn_conv_w,
        ffn_conv_b, ffn_out, ln_ffn_g, ln_ffn_b,
    )
    return second_block(
        x, mem_2, w_in_2, gate_b_2, conv_w_2, conv_b_2, mh_g_2, rel_bias_2, w_out_2, xq_2, xk_2,
        xv_2, xo_2, w1_2, w3_2, w2_2, ln_g_2, ln_b_2,
    )


_drawn_inputs = setup_inputs


def setup_inputs(seed=0):
    import zlib

    import numpy as np

    out = dict(_drawn_inputs(seed))
    spreads = {}
    factors = {'nsa_cmp_pos': 2.89,
     'hgrn_norm_g': 6.471,
     'pool_scale': 4.862,
     'sg_ln_g': 8.0,
     'sg_ln_b': 8.0,
     'sg_b': 5.568,
     'mem_ln_g': 8.0,
     'mem_ln_b': 7.231,
     'ffn_conv_b': 8.0,
     'conv_b_2': 8.0,
     'mh_g_2': 8.0,
     'rel_bias_2': 3.138}
    for name, (base, spread) in spreads.items():
        noise = np.random.default_rng([zlib.crc32(name.encode()), seed]).standard_normal(out[name].shape)
        drawn = base * np.exp(spread * noise) if base else spread * noise
        out[name] = jnp.asarray(drawn.astype(out[name].dtype))
    for name, factor in factors.items():
        out[name] = (out[name] * factor).astype(out[name].dtype)
    return out
```

```python
from contextlib import ExitStack, contextmanager

import numpy as np
import concourse.bass as bass
from concourse import mybir

F32 = mybir.dt.float32
F32R = mybir.dt.float32r
ALU = mybir.AluOpType
ACT = mybir.ActivationFunctionType
AX = mybir.AxisListType.X

P = 128
T = 256
NT = T // P
D = 2048
DC = D // P
CB = 4
UNIT = CB * P
SLOTS = 4
NB = D // UNIT
FF = 5632
FC = FF // P
FB = FF // UNIT
ALPHA = 2.0 ** 0.25
EPS = 1e-5
NEG = -1e30
FAR = 1e35
MIX = 512
C_Q, C_KV, C_HG, C_POOL, C_SG, C_MERGE = 0, 512, 1304, 3352, 3864, 4888
C2_GATE, C2_DQ = 4096, 4104
NCMP = 15
REL = 32
SKEW = 384

STAGES = [("nsa_q", 4), ("nsa_kv", 8), ("hgrn", 16), ("pool", 4), ("sgu", 8), ("merge", 80),
          ("mix_out", 16), ("xmem", 8), ("xq", 4), ("xo", 4), ("ffn_in", 8 * FB), ("ffn_out", 4 * FB),
          ("gates2", 4), ("mlstm", 32), ("dilated", 24), ("out2", 16), ("x2", 48), ("xo2", 16),
          ("ffn2_in", 8 * FB), ("ffn2_out", 4 * FB)]
BASE, _n = {}, 0
for _name, _u in STAGES:
    BASE[_name] = _n
    _n += _u
UNITS = _n

F_BLOCK = [("F", s * P, P, 0, s * T) for s in range(CB)]
T_BLOCK = [("T", 0, UNIT, h, h * UNIT) for h in range(NT)]
KV0_BLOCK = [("F", 0, P, 0, 0), ("F", 128, P, 0, 256), ("F", 256, P, 0, 512),
             ("T", 384, P, 0, 768), ("T", 384, P, 1, 896)]
KV1_BLOCK = [("F", 0, P, 0, 0), ("T", 128, P, 0, 256), ("T", 128, P, 1, 384),
             ("T", 256, 24, 0, 512), ("T", 256, 24, 1, 576)]
GATE_BLOCK = [("T", 0, 8, 0, 0), ("T", 0, 8, 1, 64)]

ROWS = [(0, f"ln_g{i}", DC) for i in range(7)] + [(1, f"ln_b{i}", DC) for i in range(7)] + [
    (1, "lb", 4), (1, "pool_scale", 4), (1, "sg_b", 4),
    (2, "cw0", FC), (2, "cw1", FC), (2, "cb2", DC),
    (3, "cw2", FC), (3, "cb", FC),
    (4, "c2w0", DC), (4, "c2w1", DC), (4, "c2w2", DC), (4, "c2w3", DC)]
ROW_AT, ROW_N = {}, [0] * 5
for _t, _name, _r in ROWS:
    ROW_AT[_name] = (_t, ROW_N[_t])
    ROW_N[_t] += _r


def shape_tables():
    p = np.arange(P)[:, None]
    u = np.arange(2 * P)[None, :]
    dist = P + p - u
    ident = np.eye(P)
    mean = np.full((P, P), 1.0 / D)
    tri = (p <= np.arange(P)[None, :]) * 1.0
    ones = np.ones((P, P))
    core = np.concatenate([ident, mean, tri, ones], 1)
    alibi = np.where(dist >= 0, dist, FAR)
    end = 16 * np.arange(16) + 31
    cmp_d = [np.where(t0 + p - end >= 0, t0 + p - end, FAR) for t0 in (0, P)]
    nsa = np.concatenate([alibi] + cmp_d, 1)
    level = []
    s, t = np.arange(P)[:, None], np.arange(P)[None, :]
    for l in range(7):
        h = 1 << l
        level.append((s // (2 * h) == t // (2 * h)) & (s % (2 * h) < h) & (t % (2 * h) >= h))
    level = np.concatenate(level, 1) * 1.0
    cnt = np.concatenate([1.0 / np.minimum(np.arange(T) + 1, w) for w in (2, 4, 8, 16)])
    cnt = np.broadcast_to(cnt, (P, 4 * T))
    mult = ((dist >= 0) & (dist <= 128)) * 1.0 + ((dist >= 0) & (dist % 4 == 0)) + ((dist >= 0) & (dist % 16 == 0))
    dil = np.concatenate([mult, np.where(mult > 0, 0.0, NEG)], 1)
    causal = np.where(dist >= 0, 0.0, NEG)
    d = np.maximum(255 - np.arange(SKEW), 0)
    big = np.maximum(d, 1).astype(np.float32)
    lg = 16 + (np.log(big / 16) / np.float32(np.log(2048 / 16)) * 16).astype(np.int32)
    bucket = np.where(d < 16, d, np.minimum(lg, REL - 1))
    hot = np.zeros((P, SKEW))
    hot[:REL] = (np.arange(REL)[:, None] == bucket[None, :])
    parts = {"core": core, "nsa": nsa, "level": level, "cnt": cnt, "dil": dil, "causal": causal, "hot": hot}
    at, n = {}, 0
    for k, v in parts.items():
        at[k] = (n, n + v.shape[1])
        n += v.shape[1]
    return at, np.concatenate(list(parts.values()), 1).astype(np.float32)


class Walk:

    def __init__(self):
        self.n, self.off = {}, {}

    def at(self, key, k=1):
        self.n[key] = self.n.get(key, 0) + k
        return self.n[key] + self.off.get(key, 0)

    def now(self, key):
        return self.n.get(key, 0) + self.off.get(key, 0)

    @contextmanager
    def loop(self, i, first, times, per):
        begin = dict(self.n)
        self.off = {k: (i - first) * v for k, v in per.items()}
        yield
        for k in set(self.n) | set(per):
            assert self.n.get(k, 0) - begin.get(k, 0) == per.get(k, 0), (k, self.n.get(k, 0) - begin.get(k, 0))
            self.n[k] = begin.get(k, 0) + per.get(k, 0) * times
        self.off = {}


def two_blocks(nc, a, tables, out):
    tab_at, _ = shape_tables()
    ctx = ExitStack()
    with ctx:
        def place(name, at, shape, dt=F32):
            n = int(np.prod(shape[1:])) * 4
            assert at + n <= 229344, (name, at + n)
            return nc.alloc_sbuf_tensor_at(name, shape, dt, offset=at)

        def sem(name):
            return ctx.enter_context(nc.semaphore(name))

        KB = 1024
        W0 = 16512
        wraw = place("wraw", W0, [P, SLOTS, CB, UNIT])
        whi = place("whi", W0 + 32 * KB, [P, SLOTS, CB, UNIT], F32R)
        wlo = place("wlo", W0 + 64 * KB, [P, SLOTS, CB, UNIT], F32R)
        A0 = W0 + 96 * KB
        act_h = place("act_h", A0, [P, DC, T], F32R)
        act_l = place("act_l", A0 + 16 * KB, [P, DC, T], F32R)
        X0 = A0 + 32 * KB
        alt_h = place("alt_h", X0, [P, DC, T], F32R)
        alt_l = place("alt_l", X0 + 16 * KB, [P, DC, T], F32R)
        hid = place("hid", X0, [P, FC, T])
        Z0 = X0 + 32 * KB
        res = place("res", Z0, [P, DC, T])
        tok = place("tok", Z0, [P, NT, D])
        Y0 = Z0 + 16 * KB
        core = place("core", Y0, [P, 4 * P])
        pcol = place("pcol", Y0 + 2 * KB, [P, 5, P])
        Y1 = Y0 + 2 * KB + 5 * P * 4
        ident, mean_w, tri, ones = (core[:, P * j:P * j + P] for j in range(4))
        prow = place("prow", Y1, [P, 5, P])
        outt = place("outt", X0, [P, NT, D])

        ln_mean = place("ln_mean", Y1, [P, T])
        ln_rstd = place("ln_rstd", Y1 + KB, [P, T])
        ln_sq = place("ln_sq", Y1 + 2 * KB, [P, 2, CB, T])
        n_q = place("n_q", Y1, [P, 4, T])
        n_kv = place("n_kv", Y1 + 4 * KB, [P, 4, T])
        n_v = place("n_v", Y1 + 8 * KB, [P, 2, NT, P])
        n_s = place("n_s", Y1 + 10 * KB, [P, 4, T])
        n_pt = place("n_pt", Y1 + 14 * KB, [P, NT, 4 * P])
        n_win = place("n_win", Y1 + 18 * KB, [P, 2, 32, NCMP])
        n_tab = place("n_tab", Y1 + 22 * KB, [P, 2 * P + 32])
        n_gate = place("n_gate", Y1 + 24 * KB, [P, NT, 24])
        n_kc = place("n_kc", Y1 + 24 * KB + 256, [P, 16])
        n_vc = place("n_vc", Y1 + 24 * KB + 512, [16, 2, 64])
        n_pos = place("n_pos", Y1 + 25 * KB, [P, 2, 32])
        st = place("st", Y1 + 27 * KB - 256, [P, 128])
        n_w = place("n_w", Z0, [P, 2, 32, 64])
        g_q = place("g_q", Y1, [P, 4, T])
        g_k = place("g_k", Y1 + 4 * KB, [P, 4, T])
        g_v = place("g_v", Y1 + 8 * KB, [P, NT, MIX])
        g_g = place("g_g", Y1 + 12 * KB, [P, NT, MIX])
        g_p = place("g_p", Y1 + 16 * KB, [P, 4 * T])
        g_mask = place("g_mask", Y1 + 20 * KB, [P, 7, P])
        g_norm = place("g_norm", Y1 + 24 * KB, [P, MIX])
        g_qh = place("g_qh", Z0, [P, 4 * T])
        g_kh = place("g_kh", Z0 + 4 * KB, [P, 4 * T])
        g_a = place("g_a", Z0 + 8 * KB, [P, 4, NT, P])
        g_t = place("g_t", Z0 + 12 * KB, [P, 4 * T])
        p_c = place("p_c", Y1, [P, 4, T])
        p_inv = place("p_inv", Y1 + 4 * KB, [P, 4, T])
        p_w = place("p_w", Y1 + 8 * KB, [P, 4, P])
        p_a = place("p_a", Z0, [P, 4, T])
        p_b = place("p_b", Z0 + 4 * KB, [P, 4, T])
        s_u = place("s_u", Y1, [P, NT, MIX])
        s_v = place("s_v", Y1 + 4 * KB, [P, NT, MIX])
        s_w = place("s_w", Y1 + 8 * KB, [P, 4, P])
        s_wt = place("s_wt", Y1 + 10 * KB, [P, 4, P])
        s_g = place("s_g", Y1 + 12 * KB, [P, MIX])
        s_b = place("s_b", Y1 + 14 * KB, [P, MIX])
        s_o = place("s_o", Z0, [P, NT, MIX])
        m_g = place("m_g", Y1, [P, 4, T])
        m_t = place("m_t", Y1 + 4 * KB, [P, 4, T])
        x_q = place("x_q", Y1, [P, 4, T])
        x_k = place("x_k", Y1 + 4 * KB, [P, 4, T])
        x_v = place("x_v", Y1 + 8 * KB, [P, NT, MIX])
        x_s = place("x_s", Y1 + 12 * KB, [P, 4, T])
        x_pt = place("x_pt", Y1 + 16 * KB, [P, NT, 4 * P])
        x_bias = place("x_bias", Y1 + 20 * KB, [P, 4, T])
        x_tab = place("x_tab", Y1 + 24 * KB, [P, 2, T])
        f_h = place("f_h", Y1, [P, 2, CB, T], F32R)
        f_l = place("f_l", Y1 + 8 * KB, [P, 2, CB, T], F32R)
        f_a = place("f_a", Y1 + 16 * KB, [P, CB, T])
        f_b = place("f_b", Y1 + 20 * KB, [P, CB, T])
        l_q = place("l_q", Y1, [P, 4, T])
        l_k = place("l_k", Y1 + 4 * KB, [P, 4, T])
        l_v = place("l_v", Y1 + 8 * KB, [P, NT, MIX])
        l_o = place("l_o", Y1 + 12 * KB, [P, NT, MIX])
        l_norm = place("l_norm", Y1 + 16 * KB, [P, MIX])
        l_tab = place("l_tab", Y1 + 18 * KB, [P, 2 * P])
        l_s = place("l_s", Y1 + 19 * KB, [P, 2, T])
        l_gate = place("l_gate", Y1 + 21 * KB, [P, NT, 8])
        l_gb = place("l_gb", Y1 + 21 * KB + 128, [P, 8])
        l_lf = place("l_lf", Y1 + 21 * KB + 256, [P, NT, 4])
        l_cum = place("l_cum", Y1 + 21 * KB + 512, [P, NT, 4])
        l_i = place("l_i", Y1 + 21 * KB + 640, [P, NT, 4])
        l_e = place("l_e", Y1 + 21 * KB + 768, [P, NT, 4])
        l_a = place("l_a", Z0, [P, 4, T])
        l_b = place("l_b", Z0 + 4 * KB, [P, 4, T])
        l_pt = place("l_pt", Z0 + 8 * KB, [P, NT, 2 * P])
        l_h = place("l_h", Z0 + 10 * KB, [P, MIX])
        b_vec = place("b_vec", Z0, [P, 8, SKEW])
        b_hot = place("b_hot", Y1 + 16 * KB, [REL, SKEW])
        b_rel = place("b_rel", Y1 + 18 * KB, [REL, 8])

        ps = ctx.enter_context(nc.psum_tensor("ps", [P, 8 * 512], F32))
        PC = 2048
        PT_ = 3072
        PO = 3584
        bias_dram = nc.dram_tensor("bias_dram", [8, P, SKEW], F32)

        loaded = [sem(f"loaded{j}") for j in range(SLOTS)]
        hi_done = sem("hi_done")
        lo_done = sem("lo_done")
        unit_done = sem("unit_done")
        block_saved = sem("block_saved")
        tokens_in = sem("tokens_in")
        tokens_turned = sem("tokens_turned")
        operand = sem("operand")
        params_in = sem("params_in")
        params_turned = sem("params_turned")
        small_in = sem("small_in")
        dve_step = sem("dve_step")
        act_step = sem("act_step")
        squares_done = sem("squares_done")
        squares_used = sem("squares_used")
        mean_done = sem("mean_done")
        centred = sem("centred")
        var_done = sem("var_done")
        var_saved = sem("var_saved")
        root_done = sem("root_done")
        result_ready = sem("result_ready")
        shifted = sem("shifted")
        mapped = sem("mapped")
        left_ready = sem("left_ready")
        turned = sem("turned")
        turned_saved = sem("turned_saved")
        gate_done = sem("gate_done")
        gate_read = sem("gate_read")
        conv_done = sem("conv_done")
        silu_done = sem("silu_done")
        silu_used = sem("silu_used")
        merge_added = sem("merge_added")
        hidden_ready = sem("hidden_ready")
        bias_out = sem("bias_out")
        out_done = sem("out_done")

        OPERANDS = ["turn_params", "x", "nsa", "hgrn", "pool", "sgu", "mixed", "mix_out", "x1", "mem_tokens", "memory",
                    "xa", "xo", "x2", "ffn_out", "x3", "bias", "gates2", "ml0", "ml1", "di0", "di1", "out2", "x4",
                    "mem2", "xb", "xo2", "x5", "ffn2_out", "y", "end"]
        SMALL = {"nsa": 5, "hgrn": 7, "pool": 9, "sgu": 12, "bias": 14, "gates2": 16, "ml0": 17, "ml1": 18, "di0": 20, "di1": 21}

        def after(name):
            return OPERANDS.index(name) + 1

        def col(name, c=0, n=1):
            t, r = ROW_AT[name]
            return pcol[:, t, r + c:r + c + n]

        def wide(ap, n):
            return ap.unsqueeze(2).to_broadcast([ap.shape[0], ap.shape[1], n])

        def over(ap, n):
            return ap.unsqueeze(1).to_broadcast([ap.shape[0], n, ap.shape[1]])

        def pair(b):
            return ps[:, (b % 2) * 1024:(b % 2) * 1024 + 1024]

        def tab(name):
            x, y = tab_at[name]
            return tables[:, x:y]

        def rows(w, r0, c0, cols=UNIT):
            return w[r0:r0 + UNIT, c0:c0 + cols].rearrange("(k p) n -> p k n", p=P)

        win, win2 = a["w_in"][0], a["w_in_2"][0]
        wb = a["w_branch"][0]
        gains = [a["ln_mix_g"][0], a["mem_ln_g"], a["ln_x_g"][0], a["ln_ffn_g"][0]] + [a["ln_g_2"][0, j] for j in range(3)]
        biases = [a["ln_mix_b"][0], a["mem_ln_b"], a["ln_x_b"][0], a["ln_ffn_b"][0]] + [a["ln_b_2"][0, j] for j in range(3)]
        prow_src = {f"ln_g{j}": gains[j] for j in range(7)} | {f"ln_b{j}": biases[j] for j in range(7)}
        prow_src |= {"lb": a["hgrn_lb_logits"][0], "pool_scale": a["pool_scale"][0], "cb": a["ffn_conv_b"][0],
                     "cb2": a["conv_b_2"][0]}
        prow_src |= {f"cw{j}": a["ffn_conv_w"][0, j] for j in range(3)} | {f"c2w{j}": a["conv_w_2"][0, j] for j in range(4)}
        block = ctx.enter_context(nc.Block())

        @block.sync
        def _(sp):
            w = Walk()

            def load(src, cols=UNIT, perm=False):
                g = w.at("unit")
                slot = (w.n["unit"] - 1) % SLOTS
                if w.n["unit"] > SLOTS:
                    sp.wait_ge(lo_done, g - SLOTS)
                if perm:
                    for j in range(4):
                        for h in range(2):
                            sp.dma_start(wraw[:, slot, :, j * P + h * 64:j * P + h * 64 + 64],
                                         src[:, :, h * 256 + j * 64:h * 256 + j * 64 + 64]).then_inc(loaded[slot], 16)
                else:
                    sp.dma_start(wraw[:, slot, :, 0:cols], src).then_inc(loaded[slot], 16)

            def column(mat, c0, cols=UNIT, k=D, r0=0):
                for u in range(k // UNIT):
                    load(rows(mat, r0 + u * UNIT, c0, cols), cols)

            sp.dma_start(tok[:, :, :], a["x"][0].rearrange("(n p) d -> p n d", p=P)).then_inc(tokens_in, 16)
            for u in range(4):
                load(rows(win, u * UNIT, C_Q), perm=True)
            column(win, C_KV)
            column(win, C_KV + UNIT, 280)
            for j in range(4):
                column(win, C_HG + j * MIX)
            column(win, C_POOL)
            column(win, C_SG)
            column(win, C_SG + MIX)
            with sp.Fori(0, 4) as i, w.loop(i, 0, 4, {"unit": 20}):
                for cb in range(NB):
                    for u in range(4):
                        load(win[u * UNIT:(u + 1) * UNIT, bass.ds(i * D + (C_MERGE + cb * UNIT), UNIT)]
                             .rearrange("(k p) n -> p k n", p=P))
                    load(wb[i, :, cb * UNIT:(cb + 1) * UNIT].rearrange("(k p) n -> p k n", p=P))

            def square(mat):
                with sp.Fori(0, NB // 2) as i, w.loop(i, 0, NB // 2, {"unit": 8}):
                    for cb in range(2):
                        for u in range(4):
                            load(mat[u * UNIT:(u + 1) * UNIT, bass.ds(i * 2 * UNIT + cb * UNIT, UNIT)]
                                 .rearrange("(k p) n -> p k n", p=P))

            def ffn(gate, gate_c, up, up_c, down):
                with sp.Fori(0, FB) as i, w.loop(i, 0, FB, {"unit": 8}):
                    for mat, c0 in ((gate, gate_c), (up, up_c)):
                        for u in range(4):
                            load(mat[u * UNIT:(u + 1) * UNIT, bass.ds(i * UNIT + c0, UNIT)]
                                 .rearrange("(k p) n -> p k n", p=P))
                with sp.Fori(0, FB) as i, w.loop(i, 0, FB, {"unit": 4}):
                    for cb in range(NB):
                        load(down[bass.ds(i * UNIT, UNIT), cb * UNIT:(cb + 1) * UNIT]
                             .rearrange("(k p) n -> p k n", p=P))

            square(a["w_mix_out"][0])
            column(a["xattn_k"][0], 0)
            sp.wait_ge(operand, after("x1"))
            sp.dma_start(tok[:, :, :], a["mem"][0].rearrange("(n p) d -> p n d", p=P)).then_inc(tokens_in, 16)
            column(a["xattn_v"][0], 0)
            column(a["xattn_q"][0], 0)
            for cb in range(NB):
                column(a["xattn_o"][0], cb * UNIT, k=UNIT)
            ffn(a["ffn_in"][0], 0, a["ffn_in"][0], FF, a["ffn_out"][0])
            column(win2, C2_GATE, 8)
            for g in range(2):
                for c0 in (0, 1024, 2048, 3072):
                    column(win2, c0 + g * UNIT)
            for g in range(2):
                for c0 in (0, 1024, 2048):
                    column(win2, C2_DQ + c0 + g * UNIT)
            square(a["w_out_2"][0])
            sp.wait_ge(operand, after("x4"))
            sp.dma_start(tok[:, :, :], a["mem_2"][0].rearrange("(n p) d -> p n d", p=P)).then_inc(tokens_in, 16)
            with sp.Fori(0, 4) as i, w.loop(i, 0, 4, {"unit": 12}):
                for mat in (a["xk_2"][0], a["xv_2"][0], a["xq_2"][0]):
                    for u in range(4):
                        load(mat[u * UNIT:(u + 1) * UNIT, bass.ds(i * UNIT, UNIT)]
                             .rearrange("(k p) n -> p k n", p=P))
            square(a["xo_2"][0])
            ffn(a["w1_2"][0], 0, a["w3_2"][0], 0, a["w2_2"][0])
            assert w.n["unit"] == UNITS
            sp.wait_ge(operand, after("end"))
            sp.dma_start(out[0].rearrange("(n p) d -> p n d", p=P), outt[:, :, :]).then_inc(out_done, 16)
            sp.wait_ge(out_done, 16)

        @block.gpsimd
        def _(pool):
            with pool.Fori(0, UNITS // SLOTS) as i:
                for slot in range(SLOTS):
                    pool.wait_ge(hi_done, i * SLOTS + (slot + 1))
                    pool.tensor_tensor(wlo[:, slot], wraw[:, slot], whi[:, slot].bitcast(F32),
                                       ALU.subtract).then_inc(lo_done, 1)

        @block.scalar
        def _(act):
            w = Walk()

            def hi(n, first_load=16):
                for _ in range(n):
                    g = w.at("unit")
                    slot = (w.n["unit"] - 1) % SLOTS
                    act.wait_ge(loaded[slot], w.at(f"slot{slot}", first_load))
                    if w.n["unit"] > SLOTS:
                        act.wait_ge(unit_done, g - SLOTS)
                    act.activation(whi[:, slot], wraw[:, slot], ACT.Copy).then_inc(hi_done, 1)

            def small(dst, src):
                act.dma_start(dst, src).then_inc(small_in, 16)

            def mapping(*ins):
                act.wait_ge(shifted, w.at("shifted"))
                for n, (dst, src, fn) in enumerate(ins):
                    x = act.activation(dst, src, fn)
                    if n == len(ins) - 1:
                        x.then_inc(mapped, 1)

            def save_turned(dst, src):
                act.wait_ge(turned, w.at("turned"))
                act.activation(dst, src, ACT.Copy).then_inc(turned_saved, 1)

            def norm():
                for q in range(4):
                    act.wait_ge(centred, w.at("centred"))
                    if q >= 2:
                        act.wait_ge(squares_used, w.now("squares") - 1)
                    w.at("squares")
                    act.activation(ln_sq[:, q % 2], res[:, 4 * q:4 * q + 4, :], ACT.Square).then_inc(squares_done, 1)
                mapping((ln_rstd[:, :], ln_rstd[:, :], ACT.Sqrt))

            for t, name, r in ROWS:
                at = ROW_AT[name][1]
                src = a["sg_b"][0] if name == "sg_b" else prow_src[name].rearrange("(c p) -> c p", p=P)
                act.dma_start(prow[at:at + r, t, :], src).then_inc(params_in, 16)
            act.dma_start(core[:, :], tab("core")).then_inc(params_in, 16)
            hi(4, 128)
            act.wait_ge(operand, after("x"))
            small(n_tab[:, :], tab("nsa"))
            for g in range(2):
                small(n_w[64 * g:64 * g + 64], a["nsa_cmp_w"][0].rearrange("v l d e -> d v l e"))
                with nc.allow_non_contiguous_dma("small"):
                    small(n_pos[64 * g:64 * g + 64], a["nsa_cmp_pos"][0].rearrange("v l d -> d v l"))
            hi(8)
            hi(4)
            mapping((n_gate[:, :, :], n_gate[:, :, :], ACT.Sigmoid))
            for g in range(2):
                for qt in range(NT):
                    for br in range(3):
                        n = NCMP if br == 0 else P * (qt + 1)
                        mapping((n_s[:, :, 0:n], n_s[:, :, 0:n], ACT.Exp))
                        for kt in range(1 if br == 0 else qt + 1):
                            kn = NCMP if br == 0 else P
                            save_turned(n_pt[0:kn, kt, :], ps[0:kn, PT_:PT_ + 512])
            act.wait_ge(operand, after("nsa"))
            small(g_mask[:, :, :], tab("level").rearrange("p (l n) -> p l n", l=7))
            small(g_norm[:, :], a["hgrn_norm_g"][0].partition_broadcast(P))
            hi(12)
            hi(4)
            mapping((st[:, 0:4], st[:, 0:4], ACT.Exp))
            mapping((g_k[:, :, :], g_k[:, :, :], ACT.Sigmoid))
            mapping((g_p[:, :], g_k[:, :, :].rearrange("p h t -> p (h t)"), ACT.Ln))
            for l in range(8):
                h = 1 << l
                v = g_p[:, :].rearrange("p (m two h) -> p m two h", two=2, h=h)
                e = g_t[:, :].rearrange("p (m two h) -> p m two h", two=2, h=h)
                mapping((e[:, :, 0, :], e[:, :, 0, :], ACT.Exp), (e[:, :, 1, :], v[:, :, 1, :], ACT.Exp))
            mapping((g_t[:, :], ps[:, PC:PC + 1024], ACT.Square))
            mapping((st[:, 0:8], st[:, 0:8], ACT.Sqrt))
            mapping((g_g[:, :, :], g_g[:, :, :], ACT.Silu))
            act.wait_ge(operand, after("hgrn"))
            small(p_inv[:, :, :], tab("cnt").rearrange("p (g t) -> p g t", g=4))
            small(p_w[:, :, :], a["pool_w"][0].rearrange("g c d -> c g d"))
            hi(4)
            act.wait_ge(operand, after("pool"))
            small(s_w[:, :, :], a["sg_w"][0].rearrange("g q p -> q g p"))
            small(s_g[:, :], a["sg_ln_g"][0].partition_broadcast(P))
            small(s_b[:, :], a["sg_ln_b"][0].partition_broadcast(P))
            hi(4)
            mapping((s_u[:, :, :], s_u[:, :, :], ACT.Gelu_apprx_tanh))
            mapping((s_v[:, :, :], s_v[:, :, :], ACT.Gelu_apprx_tanh))
            mapping((st[:, 32:34], st[:, 32:34], ACT.Sqrt))
            act.sem_inc(gate_done, 1)
            with act.Fori(0, 4) as i, w.loop(i, 0, 4, {"unit": 20, "gate_read": 4, "gunit": 20, **{f"slot{s}": 80 for s in range(4)}}):
                for cb in range(NB):
                    hi(5)
                    act.wait_ge(unit_done, BASE["merge"] + w.at("gunit", 5) - 1)
                    act.wait_ge(gate_read, w.at("gate_read"))
                    act.activation(m_g[:, :, :], pair(0).rearrange("p (s t) -> p s t", s=4), ACT.Sigmoid).then_inc(gate_done, 1)

            def square():
                with act.Fori(0, 2) as i, w.loop(i, 0, 2, {"unit": 8, **{f"slot{s}": 32 for s in range(4)}}):
                    hi(8)

            def tiles(s, pt, heads=True):
                for qt in range(NT):
                    n = T if heads else P * (qt + 1)
                    mapping((s[:, :, 0:n], s[:, :, 0:n], ACT.Exp))
                    for kt in range(NT if heads else qt + 1):
                        save_turned(pt[:, kt, :], ps[:, PT_:PT_ + 512])

            def ffn(name, conv):
                per = {"unit": 8, "silu": 1, **{f"slot{s}": 32 for s in range(4)}}
                with act.Fori(0, FB) as i, w.loop(i, 0, FB, per):
                    hi(8)
                    n = w.at("silu")
                    if conv:
                        act.wait_ge(conv_done, n + 1)
                        act.activation(f_a[:, :, :], f_a[:, :, :], ACT.Silu).then_inc(silu_done, 1)
                    else:
                        act.wait_ge(unit_done, BASE[name] + 8 * i + 4)
                        act.wait_ge(silu_used, n + 1)
                        act.activation(f_a[:, :, :], pair(0).rearrange("p (s t) -> p s t", s=4),
                                       ACT.Silu).then_inc(silu_done, 1)
                with act.Fori(0, FB) as i, w.loop(i, 0, FB, {"unit": 4, **{f"slot{s}": 16 for s in range(4)}}):
                    hi(4)

            square()
            hi(4)
            norm()
            norm()
            hi(12)
            tiles(x_s, x_pt)
            norm()
            ffn("ffn_in", True)
            norm()
            act.wait_ge(operand, after("x3"))
            small(b_hot[:, :], tab("hot")[0:REL, :])
            small(b_rel[:, :], a["rel_bias_2"])
            act.wait_ge(operand, after("bias"))
            act.dma_start(bias_dram.ap().rearrange("h p n -> p h n"), b_vec[:, :, :]).then_inc(bias_out, 16)
            act.wait_ge(bias_out, 16)
            small(l_gb[:, :], a["gate_b_2"][0].partition_broadcast(P))
            small(l_tab[:, :], tab("causal"))
            hi(4)
            hi(4)
            mapping((l_e[:, :, :], l_e[:, :, :], ACT.Exp))
            mapping((l_e[:, :, :], l_e[:, :, :], ACT.Ln))
            for g in range(2):
                if g:
                    act.wait_ge(operand, after("ml0"))
                small(l_norm[:, :], a["mh_g_2"][0, g * MIX:(g + 1) * MIX].partition_broadcast(P))
                hi(4)
                mapping((l_q[:, :, :], l_a[:, :, :], ACT.Silu))
                hi(4)
                mapping((l_k[:, :, :], l_a[:, :, :], ACT.Silu))
                hi(8)
                mapping((l_o[:, :, :], l_o[:, :, :], ACT.Sigmoid))
                for qt in range(NT):
                    n = P * (qt + 1)
                    mapping((l_s[:, :, 0:n], l_s[:, :, 0:n], ACT.Exp), (st[:, 8:10], st[:, 8:10], ACT.Exp))
                    for kt in range(qt + 1):
                        save_turned(l_pt[:, kt, :], ps[:, PT_:PT_ + 256])
                    mapping((st[:, 32:34], st[:, 32:34], ACT.Sqrt))
            for g in range(2):
                act.wait_ge(operand, after(f"ml1" if g == 0 else "di0"))
                if g == 0:
                    small(x_tab[:, :, :], tab("dil").rearrange("p (a n) -> p a n", a=2))
                skew = bass.AP(bias_dram, 4 * g * P * SKEW + P - 1, [[SKEW - 1, P], [P * SKEW, 4], [1, T]])
                small(x_bias[:, :, :], skew)
                if g == 0:
                    hi(8)
                    hi(4)
                    tiles(x_s, x_pt, False)
                else:
                    hi(8)
                    hi(4)
                    tiles(x_s, x_pt, False)
            hi(12)
            norm()
            per = {"unit": 12, "shifted": 1, "turned": 1, **{f"slot{s}": 48 for s in range(4)}}
            with act.Fori(0, 4) as i, w.loop(i, 0, 4, per):
                hi(12)
                mapping((x_s[:, 0:2, :], x_s[:, 0:2, :], ACT.Exp))
                save_turned(x_pt[:, 0, :], ps[:, PT_:PT_ + 512])
            square()
            norm()
            ffn("ffn2_in", False)
            norm()
            assert w.n["unit"] == UNITS

        @block.tensor
        def _(pe):
            w = Walk()

            def products(pieces, units, hi, lo, bank, chunk=0, fresh=True, last=True, dyn=None):
                for u in range(units):
                    pe.wait_ge(lo_done, w.at("unit"))
                    slot = (w.n["unit"] - 1) % SLOTS
                    for k in range(CB):
                        begun = set()
                        for kind, c, width, h, at in pieces:
                            first = fresh and u == 0 and k == 0 and at // 512 not in begun
                            begun.add(at // 512)
                            stop = last and u == units - 1 and k == CB - 1
                            kc = chunk + u * CB + k
                            for n, (wt, op) in enumerate(((whi, hi), (whi, lo), (wlo, hi))):
                                wk = wt[:, slot, k, c:c + (P if kind == "F" else width)]
                                if kind == "F":
                                    x = op[:, kc, :] if dyn is None else op[:, dyn + k, :]
                                    o = ps[:, bank + at:bank + at + T]
                                    ins = pe.matmul(o, wk, x, start=first and n == 0, stop=stop and n == 2,
                                                    skip_group_check=True)
                                else:
                                    x = op[:, kc, h * P:h * P + P]
                                    o = ps[:, bank + at:bank + at + width]
                                    ins = pe.matmul(o, x, wk, start=first and n == 0, stop=stop and n == 2,
                                                    skip_group_check=True)
                    ins.then_inc(unit_done, 1)

            def column(pieces=F_BLOCK, units=4, hi=act_h, lo=act_l):
                b = w.at("block")
                if w.n["block"] > 2:
                    pe.wait_ge(block_saved, b - 2)
                products(pieces, units, hi, lo, ((w.n["block"] - 1) % 2) * 1024)

            def saved():
                pe.wait_ge(block_saved, w.now("block"))

            def mm(o, left, right, start, stop):
                return pe.matmul(o, left, right, start=start, stop=stop, skip_group_check=True)

            def turn(o, src, n=P):
                k = src.shape[0]
                return pe.matmul(o, src, ident[0:k, 0:k], start=True, stop=True, is_transpose=True, skip_group_check=True)

            def turn_tokens(count):
                pe.wait_ge(tokens_in, 16 * count)
                for c in range(DC):
                    for h in range(NT):
                        x = turn(ps[:, c * T + h * P:c * T + h * P + P], tok[:, h, c * P:c * P + P])
                x.then_inc(tokens_turned, 1)

            def norm(name):
                pe.wait_ge(operand, after(name))
                for c in range(DC):
                    x = mm(ps[:, PC:PC + T], mean_w, res[:, c, :], c == 0, c == DC - 1)
                x.then_inc(mean_done, 1)
                for q in range(4):
                    pe.wait_ge(squares_done, w.at("squares"))
                    for c in range(4):
                        x = mm(ps[:, PC + 512:PC + 512 + T], mean_w, ln_sq[:, q % 2, c, :], q + c == 0, q + c == 6)
                    x.then_inc(squares_used, 1)

            def turn_probs(s, heads, keys):
                for kt in range(-(-keys // P)):
                    kn = min(keys, P)
                    if w.n.get("turned", 0):
                        pe.wait_ge(turned_saved, w.now("turned"))
                    w.at("turned")
                    for j in range(heads):
                        x = turn(ps[0:kn, PT_ + j * P:PT_ + j * P + P], s[:, j, kt * P:kt * P + kn])
                    x.then_inc(turned, 1)
                pe.wait_ge(turned_saved, w.now("turned"))

            def turn_rows(src, blocks, bank=PC):
                pe.wait_ge(left_ready, w.at("left"))
                for j, (o, n, c) in enumerate(blocks):
                    x = turn(ps[:, bank + o:bank + o + P], src[:, n, c * P:c * P + P])
                x.then_inc(result_ready, 1)

            pe.wait_ge(params_in, 16 * (len(ROWS) + 1))
            for t in range(5):
                x = turn(ps[:, t * P:t * P + ROW_N[t]], prow[0:ROW_N[t], t, :])
            x.then_inc(params_turned, 1)
            pe.wait_ge(operand, after("turn_params"))
            turn_tokens(1)
            pe.wait_ge(operand, after("x"))
            column()
            column(KV0_BLOCK)
            column(KV1_BLOCK)
            saved()
            pe.wait_ge(left_ready, w.at("left"))
            for g in range(2):
                r = slice(64 * g, 64 * g + 64)
                for l in range(32):
                    mm(ps[r, PC:PC + NCMP], n_w[r, 0, l, :], n_win[r, 0, l, :], l == 0, l == 31)
            for g in range(2):
                r = slice(64 * g, 64 * g + 64)
                for l in range(32):
                    x = mm(ps[0:NCMP, PC + 512 + 512 * g:PC + 576 + 512 * g], n_win[r, 1, l, :], n_w[r, 1, l, :],
                           l == 0, l == 31)
            x.then_inc(result_ready, 1)
            pe.wait_ge(left_ready, w.at("left"))
            for g in range(2):
                r = slice(64 * g, 64 * g + 64)
                for qt in range(NT):
                    for br in range(3):
                        n = NCMP if br == 0 else P * (qt + 1)
                        keys = n_kc[r, 0:NCMP] if br == 0 else n_kv[r, br + 1, 0:n]
                        for j in range(4):
                            x = mm(ps[:, PC + j * T:PC + j * T + n], n_q[r, j, qt * P:qt * P + P], keys, True, True)
                        x.then_inc(result_ready, 1)
                        pe.wait_ge(left_ready, w.at("left"))
                        turn_probs(n_s, 4, n)
                        for j in range(4):
                            o = ps[64 * (j % 2):64 * (j % 2) + 64, PO + (j // 2) * P:PO + (j // 2) * P + P]
                            for kt in range(-(-n // P)):
                                kn = min(n, P)
                                v = n_vc[0:NCMP, g, :] if br == 0 else n_v[:, br - 1, kt, 64 * g:64 * g + 64]
                                x = mm(o, v, n_pt[0:kn, kt, j * P:j * P + P], br == 0 and j < 2, br == 2 and kt == qt)
                    x.then_inc(result_ready, 1)
            column()
            column()
            column(T_BLOCK)
            column(T_BLOCK)
            saved()
            for l in range(-1, 7):
                pe.wait_ge(left_ready, w.at("left"))
                for h in range(4):
                    for n in range(NT):
                        c = h * T + n * P
                        kk = g_k[:, h, n * P:n * P + P] if l < 0 else g_kh[:, c:c + P]
                        qq = g_q[:, h, n * P:n * P + P] if l < 0 else g_qh[:, c:c + P]
                        x = mm(ps[:, PC + c:PC + c + P], kk, qq, True, True)
                x.then_inc(result_ready, 1)
            pe.wait_ge(left_ready, w.at("left"))
            for h in range(4):
                x = mm(ps[:, PC + h * P:PC + h * P + P], g_kh[:, h * T:h * T + P], g_qh[:, h * T + P:h * T + T], True, True)
            x.then_inc(result_ready, 1)
            pe.wait_ge(left_ready, w.at("left"))
            for n in range(NT):
                for h in range(4):
                    o = ps[:, PC + n * 512 + h * P:PC + n * 512 + h * P + P]
                    x = mm(o, g_a[:, h, n, :], g_v[:, n, h * P:h * P + P], h == 0, n == 0)
                    if n:
                        x = mm(o, g_p[:, h * P:h * P + P], g_v[:, 0, h * P:h * P + P], False, True)
            x.then_inc(result_ready, 1)
            turn_rows(g_t[:, :].rearrange("p (n c) -> p n c", n=NT), [(c * T + n * P, n, c) for c in range(4) for n in range(NT)])
            column()
            pe.wait_ge(left_ready, w.at("left"))
            for g in range(4):
                x = mm(ps[:, PC + g * T:PC + g * T + T], p_w[:, g, :], p_b[:, g, :], g % 2 == 0, True)
            x.then_inc(result_ready, 1)
            column(T_BLOCK)
            column(T_BLOCK)
            pe.wait_ge(left_ready, w.at("left"))
            for g in range(4):
                x = turn(ps[:, PC + g * P:PC + g * P + P], s_w[:, g, :])
            x.then_inc(result_ready, 1)
            pe.wait_ge(left_ready, w.at("left"))
            for n in range(NT):
                for g in range(4):
                    o = n * 512 + g * P
                    x = mm(ps[:, PC + o:PC + o + P], s_wt[:, g, :], s_v[:, n, g * P:g * P + P], g == 0, True)
            x.then_inc(result_ready, 1)
            turn_rows(s_o, [(c * T + n * P, n, c) for c in range(4) for n in range(NT)])
            pe.wait_ge(operand, after("sgu"))
            per = {"unit": 20, "gate": 4, "added": 4}
            with pe.Fori(0, 4) as i, w.loop(i, 0, 4, per):
                for cb in range(NB):
                    pe.wait_ge(gate_done, w.at("gate"))
                    products(F_BLOCK, 4, act_h, act_l, 0)
                    pe.wait_ge(merge_added, w.at("added"))
                    products(F_BLOCK, 1, alt_h, alt_l, 1024, dyn=i * CB)

            def square(hi, lo):
                with pe.Fori(0, 2) as i, w.loop(i, 0, 2, {"unit": 8, "block": 2}):
                    column(hi=hi, lo=lo)
                    column(hi=hi, lo=lo)

            def ffn(conv):
                per = {"unit": 8, "conv": 1, "silu": 1, "used": 1}
                with pe.Fori(0, FB) as i, w.loop(i, 0, FB, per):
                    if conv:
                        pe.wait_ge(conv_done, w.now("conv") + 1)
                    else:
                        pe.wait_ge(silu_done, w.now("silu"))
                    w.at("conv")
                    w.at("silu")
                    products(F_BLOCK, 4, act_h, act_l, 0)
                    pe.wait_ge(silu_used, w.at("used"))
                    products(F_BLOCK, 4, act_h, act_l, 1024)
                w.at("used")

                def piece(fresh, last, parity):
                    pe.wait_ge(hidden_ready, w.at("hidden"))
                    for cb in range(NB):
                        products(F_BLOCK, 1, f_h[:, parity], f_l[:, parity], cb * 1024, fresh=fresh, last=last)

                piece(True, False, 0)
                with pe.Fori(0, FB // 2 - 1) as i, w.loop(i, 0, FB // 2 - 1, {"unit": 8, "hidden": 2}):
                    piece(False, False, 1)
                    piece(False, False, 0)
                piece(False, False, 1)
                piece(False, True, 0)

            pe.wait_ge(operand, after("mixed"))
            assert w.n["block"] % 2 == 0
            square(alt_h, alt_l)
            norm("mix_out")
            pe.wait_ge(operand, after("x1"))
            turn_tokens(2)
            norm("mem_tokens")
            pe.wait_ge(operand, after("memory"))
            column(hi=alt_h, lo=alt_l)
            column(T_BLOCK, hi=alt_h, lo=alt_l)
            column()
            saved()
            for qt in range(NT):
                for j in range(4):
                    x = mm(ps[:, PC + j * T:PC + j * T + T], x_q[:, j, qt * P:qt * P + P], x_k[:, j, :], True, True)
                x.then_inc(result_ready, 1)
                pe.wait_ge(left_ready, w.at("left"))
                turn_probs(x_s, 4, T)
                for j in range(4):
                    for kt in range(NT):
                        x = mm(ps[:, PO + j * P:PO + j * P + P], x_v[:, kt, j * P:j * P + P],
                               x_pt[:, kt, j * P:j * P + P], j + kt == 0, kt == 1)
                x.then_inc(result_ready, 1)
            pe.wait_ge(operand, after("xa"))
            for cb in range(NB):
                column(units=1, hi=alt_h, lo=alt_l)
            norm("xo")
            pe.wait_ge(operand, after("x2"))
            ffn(True)
            norm("ffn_out")
            pe.wait_ge(operand, after("x3"))
            pe.wait_ge(small_in, 16 * SMALL["bias"])
            for h in range(8):
                x = mm(ps[:, h * 512:h * 512 + SKEW], b_rel[:, h:h + 1].to_broadcast([REL, P]), b_hot[:, :], True, True)
            x.then_inc(result_ready, 1)
            pe.wait_ge(operand, after("bias"))
            column(GATE_BLOCK)
            pe.wait_ge(left_ready, w.at("left"))
            mm(ps[:, PC:PC + 4], tri, l_lf[:, 0, :], True, True)
            mm(ps[:, PC + 4:PC + 8], tri, l_lf[:, 1, :], False, False)
            mm(ps[:, PC + 4:PC + 8], ones, l_lf[:, 0, :], False, True).then_inc(result_ready, 1)
            pe.wait_ge(operand, after("gates2"))
            for g in range(2):
                column()
                column()
                column(T_BLOCK)
                column(T_BLOCK)
                saved()
                pe.wait_ge(left_ready, w.at("left"))
                for qt in range(NT):
                    n = P * (qt + 1)
                    for j in range(2):
                        for kt in range(qt + 1):
                            mm(ps[:, PC + j * T + kt * P:PC + j * T + kt * P + P],
                               l_i[:, kt, 2 * g + j:2 * g + j + 1].to_broadcast([P, P]), ident, True, True)
                    for j in range(2):
                        for c in range(2):
                            x = mm(ps[:, PC + 512 + j * T:PC + 512 + j * T + n], l_q[:, 2 * j + c, qt * P:qt * P + P],
                                   l_k[:, 2 * j + c, 0:n], c == 0 and j == 0, c == 1)
                    x.then_inc(result_ready, 1)
                    pe.wait_ge(left_ready, w.at("left"))
                    turn_probs(l_s, 2, n)
                    for j in range(2):
                        for kt in range(qt + 1):
                            x = mm(ps[:, PO + j * T:PO + j * T + T], l_pt[:, kt, j * P:j * P + P],
                                   l_v[:, kt, j * T:j * T + T], j + kt == 0, kt == qt)
                    x.then_inc(result_ready, 1)
                    turn_rows(l_h[:, :].unsqueeze(1), [(c * P, 0, c) for c in range(4)], PT_)
            for g in range(2):
                column()
                column()
                column(T_BLOCK)
                saved()
                for qt in range(NT):
                    n = P * (qt + 1)
                    for j in range(4):
                        x = mm(ps[:, PC + j * T:PC + j * T + n], x_q[:, j, qt * P:qt * P + P], x_k[:, j, 0:n], True, True)
                    x.then_inc(result_ready, 1)
                    pe.wait_ge(left_ready, w.at("left"))
                    turn_probs(x_s, 4, n)
                    for j in range(4):
                        for kt in range(qt + 1):
                            x = mm(ps[:, PO + j * P:PO + j * P + P], x_v[:, kt, j * P:j * P + P],
                                   x_pt[:, kt, j * P:j * P + P], j + kt == 0, kt == qt)
                    x.then_inc(result_ready, 1)
            pe.wait_ge(operand, after("di1"))
            assert w.n["block"] % 2 == 0
            square(alt_h, alt_l)
            norm("out2")
            pe.wait_ge(operand, after("x4"))
            turn_tokens(3)
            pe.wait_ge(operand, after("mem2"))
            per = {"unit": 24, "block": 6, "left": 2, "turned": 2}
            with pe.Fori(0, 2) as i, w.loop(i, 0, 2, per):
                for _ in range(2):
                    column(hi=alt_h, lo=alt_l)
                    column(T_BLOCK, hi=alt_h, lo=alt_l)
                    column()
                    saved()
                    for qt in range(NT):
                        for c in range(4):
                            x = mm(ps[:, PC + qt * T:PC + qt * T + T], x_q[:, c, qt * P:qt * P + P], x_k[:, c, :],
                                   c + qt == 0, c == 3)
                    x.then_inc(result_ready, 1)
                    pe.wait_ge(left_ready, w.at("left"))
                    pe.wait_ge(turned_saved, w.now("turned"))
                    w.at("turned")
                    for kt in range(NT):
                        for qt in range(NT):
                            x = turn(ps[:, PT_ + kt * T + qt * P:PT_ + kt * T + qt * P + P],
                                     x_s[:, qt, kt * P:kt * P + P])
                    x.then_inc(turned, 1)
                    pe.wait_ge(turned_saved, w.now("turned"))
                    for c in range(4):
                        for kt in range(NT):
                            x = mm(ps[:, PC + c * T:PC + c * T + T], x_v[:, kt, c * P:c * P + P],
                                   x_pt[:, 0, kt * T:kt * T + T], (c % 2) + kt == 0, kt == 1)
                    x.then_inc(result_ready, 1)
            pe.wait_ge(operand, after("xb"))
            square(alt_h, alt_l)
            norm("xo2")
            pe.wait_ge(operand, after("x5"))
            ffn(False)
            norm("ffn2_out")
            pe.wait_ge(operand, after("y"))
            for c in range(DC):
                for h in range(NT):
                    x = turn(ps[:, h * D + c * P:h * D + c * P + P], res[:, c, h * P:h * P + P])
            x.then_inc(tokens_turned, 1)
            assert w.n["unit"] == UNITS

        @block.vector
        def _(dve):
            w = Walk()
            told = [0]

            def link(ins):
                ins.then_inc(dve_step, 1)
                dve.wait_ge(dve_step, w.at("step"))

            def tell(name, ins):
                told[0] += 1
                assert after(name) == told[0], name
                ins.then_inc(operand, 1)
                dve.wait_ge(operand, told[0])

            def to_act(ins):
                ins.then_inc(shifted, 1)
                dve.wait_ge(mapped, w.at("mapped"))

            def to_pe(ins):
                ins.then_inc(left_ready, 1)
                dve.wait_ge(left_ready, w.at("left"))

            def from_pe():
                dve.wait_ge(result_ready, w.at("result"))

            def copy(dst, src):
                return dve.tensor_copy(dst, src)

            def tt(dst, x, y, op):
                return dve.tensor_tensor(dst, x, y, op)

            def split(hi, lo, src, name=None):
                link(copy(hi, src))
                x = tt(lo, src, hi.bitcast(F32), ALU.subtract)
                if name:
                    tell(name, x)
                else:
                    link(x)

            def arrived(units):
                dve.wait_ge(unit_done, w.at("unit", units))
                b = w.at("block")
                return pair(w.n["block"] - 1)

            def kept(ins):
                ins.then_inc(block_saved, 1)
                dve.wait_ge(block_saved, w.now("block"))

            def four(x):
                return x.rearrange("p (s t) -> p s t", s=4)

            def two(x):
                return x.rearrange("p (n c) -> p n c", n=NT)

            def turned_tokens(count, hi, lo, name):
                dve.wait_ge(tokens_turned, count)
                for q in range(4):
                    x = four(ps[:, q * 1024:q * 1024 + 1024])
                    split(hi[:, 4 * q:4 * q + 4, :], lo[:, 4 * q:4 * q + 4, :], x, name if q == 3 else None)

            def softmax(s, heads, n, gate=None, floor=False, weight=None):
                m, r = st[:, 0:heads], st[:, 16:16 + heads]
                link(dve.tensor_reduce(m, s, AX, ALU.max))
                if floor:
                    link(dve.tensor_scalar(m, m, NEG, None, ALU.max))
                to_act(tt(s, s, wide(m, n), ALU.subtract))
                if weight is not None:
                    link(tt(s, s, weight, ALU.mult))
                link(dve.tensor_reduce(r, s, AX, ALU.add))
                if floor:
                    link(dve.tensor_scalar(r, r, 1e-30, None, ALU.max))
                link(dve.reciprocal(r, r))
                if gate is not None:
                    link(tt(r, r, gate, ALU.mult))
                to_pe(tt(s, s, wide(r, n), ALU.mult))

            def residual(units, times):
                for cb in range(times):
                    x = four(arrived(units))
                    sl = slice(4 * cb, 4 * cb + 4)
                    link(dve.scalar_tensor_tensor(res[:, sl, :], act_h[:, sl, :].bitcast(F32), ALPHA, x, ALU.mult, ALU.add))
                    x = dve.scalar_tensor_tensor(res[:, sl, :], act_l[:, sl, :].bitcast(F32), ALPHA, res[:, sl, :],
                                                 ALU.mult, ALU.add)
                    kept(x)

            def norm(which, hi, lo, name):
                dve.wait_ge(mean_done, w.at("mean"))
                link(copy(ln_mean[:, :], ps[:, PC:PC + T]))
                for q in range(4):
                    r = res[:, 4 * q:4 * q + 4, :]
                    x = tt(r, r, over(ln_mean[:, :], 4), ALU.subtract)
                    x.then_inc(centred, 1)
                dve.wait_ge(centred, w.at("centred", 4))
                dve.wait_ge(squares_used, w.at("squares", 4))
                to_act(dve.tensor_scalar(ln_rstd[:, :], ps[:, PC + 512:PC + 512 + T], EPS, None, ALU.add))
                link(dve.reciprocal(ln_rstd[:, :], ln_rstd[:, :]))
                for q in range(4):
                    r = res[:, 4 * q:4 * q + 4, :]
                    link(tt(r, r, over(ln_rstd[:, :], 4), ALU.mult))
                    for c in range(4 * q, 4 * q + 4):
                        x = dve.tensor_scalar(res[:, c, :], res[:, c, :], col(f"ln_g{which}", c), col(f"ln_b{which}", c),
                                              ALU.mult, ALU.add)
                        if name == "y" and c == DC - 1:
                            tell(name, x)
                        else:
                            link(x)
                    if name != "y":
                        split(hi[:, 4 * q:4 * q + 4, :], lo[:, 4 * q:4 * q + 4, :], r, name if q == 3 else None)

            dve.wait_ge(params_turned, 1)
            for t in range(5):
                x = copy(pcol[:, t, 0:ROW_N[t]], ps[:, t * P:t * P + ROW_N[t]])
                tell("turn_params", x) if t == 4 else link(x)
            turned_tokens(1, act_h, act_l, "x")

            kept(dve.tensor_scalar(n_q[:, :, :], four(arrived(4)), 0.125, None, ALU.mult))
            x = arrived(4)
            link(copy(n_kv[:, 0:3, :], x[:, 0:768].rearrange("p (s t) -> p s t", s=3)))
            kept(copy(n_v[:, 0, :, :], two(x[:, 768:1024])))
            x = arrived(4)
            link(copy(n_kv[:, 3, :], x[:, 0:256]))
            link(copy(n_v[:, 1, :, :], two(x[:, 256:512])))
            kept(copy(n_gate[:, :, :], x[:, 512:640].rearrange("p (n c) -> p n c", n=2)[:, :, 0:24]))
            to_act(copy(n_gate[:, :, :], n_gate[:, :, :]))
            dve.wait_ge(small_in, 16 * SMALL["nsa"])
            for kv in range(2):
                for half in range(2):
                    src = n_kv[:, kv, 16 * half:16 * half + 240].rearrange("p (c l) -> p l c", l=16)
                    x = tt(n_win[:, kv, 16 * half:16 * half + 16, :], src,
                           n_pos[:, kv, 16 * half:16 * half + 16].unsqueeze(2).to_broadcast([P, 16, NCMP]), ALU.add)
                    to_pe(x) if kv + half == 2 else link(x)
            from_pe()
            link(copy(n_kc[:, 0:NCMP], ps[:, PC:PC + NCMP]))
            to_pe(copy(n_vc[0:NCMP, :, :], ps[0:NCMP, PC + 512:PC + 1536].rearrange("p (g e) -> p g e", g=2)[:, :, 0:64]))
            for g in range(2):
                for qt in range(NT):
                    for br in range(3):
                        n = NCMP if br == 0 else P * (qt + 1)
                        dist = n_tab[:, 2 * P + 16 * qt:2 * P + 16 * qt + n] if br == 0 else n_tab[:, 2 * P - n:2 * P]
                        from_pe()
                        for j in range(4):
                            slope = 2.0 ** -(4 * g + j + 1)
                            link(dve.scalar_tensor_tensor(n_s[:, j, 0:n], dist, -slope, ps[:, PC + j * T:PC + j * T + n],
                                                          ALU.mult, ALU.add))
                        o = 12 * g + br
                        softmax(n_s[:, :, 0:n], 4, n, gate=n_gate[:, qt, o:o + 10:3], floor=br == 0)
                    from_pe()
                    o = two(ps[:, PO:PO + 256])
                    at = (slice(None), slice(2 * g, 2 * g + 2), slice(qt * P, qt * P + P))
                    split(alt_h[at], alt_l[at], o, "nsa" if g + qt == 2 else None)

            kept(copy(g_q[:, :, :], four(arrived(4))))
            kept(copy(g_k[:, :, :], four(arrived(4))))
            kept(copy(g_v[:, :, :], two(arrived(4))))
            kept(copy(g_g[:, :, :], two(arrived(4))))
            lb, e = col("lb", 0, 4), st[:, 0:4]
            to_act(tt(e, lb, lb, ALU.subtract))
            link(dve.reciprocal(st[:, 4:8], e))
            link(tt(e, e, st[:, 4:8], ALU.mult))
            link(tt(st[:, 8:12], e, e, ALU.subtract))
            link(dve.tensor_scalar(st[:, 12:16], st[:, 8:12], -1.0, 1.0, ALU.mult, ALU.add))
            to_act(copy(g_k[:, :, :], g_k[:, :, :]))
            for h in range(4):
                link(dve.tensor_scalar(g_k[:, h, :], g_k[:, h, :], st[:, 12 + h:13 + h], st[:, 8 + h:9 + h],
                                       ALU.mult, ALU.add))
            to_act(dve.tensor_scalar(g_k[:, :, :], g_k[:, :, :], 1e-6, None, ALU.max))
            link(dve.tensor_scalar(g_k[:, :, :], g_k[:, :, :], -1.0, 1.0, ALU.mult, ALU.add))
            link(copy(g_qh[:, :], g_q[:, :, :].rearrange("p h t -> p (h t)")))
            to_pe(copy(g_kh[:, :], g_k[:, :, :].rearrange("p h t -> p (h t)")))
            q = g_q[:, :, :].rearrange("p h t -> p (h t)")
            k = g_k[:, :, :].rearrange("p h t -> p (h t)")
            acc = g_a[:, :, :, :].rearrange("p h n t -> p (h n) t")
            blocks8 = ps[:, PC:PC + 1024].rearrange("p (b t) -> p b t", b=8)
            dve.wait_ge(small_in, 16 * SMALL["hgrn"])
            from_pe()
            link(tt(acc, blocks8, over(ident, 8), ALU.mult))
            for l in range(8):
                h = 1 << l

                def halves(x):
                    return x.rearrange("p (m two h) -> p m two h", two=2, h=h)

                pv, ev = halves(g_p[:, :]), halves(g_t[:, :])
                last = pv[:, :, 0, h - 1:h].to_broadcast([P, 512 // h, h])
                to_act(tt(ev[:, :, 0, :], last, pv[:, :, 0, :], ALU.subtract))
                link(tt(halves(g_qh[:, :])[:, :, 1, :], halves(q)[:, :, 1, :], ev[:, :, 1, :], ALU.mult))
                to_pe(tt(halves(g_kh[:, :])[:, :, 0, :], halves(k)[:, :, 0, :], ev[:, :, 0, :], ALU.mult))
                if l < 7:
                    link(tt(pv[:, :, 1, :], pv[:, :, 1, :], last, ALU.add))
                    from_pe()
                    t8 = g_t[:, :].rearrange("p (b t) -> p b t", b=8)
                    link(tt(t8, blocks8, over(g_mask[:, l, :], 8), ALU.mult))
                    link(tt(acc, acc, t8, ALU.add))
                else:
                    from_pe()
                    to_pe(copy(g_p[:, 0:512], ps[:, PC:PC + 512]))
            from_pe()
            x8 = g_t[:, :].rearrange("p (b t) -> p b t", b=8)
            to_act(copy(st[:, 16:17], st[:, 12:13]))
            link(dve.tensor_reduce(st[:, 0:8], x8, AX, ALU.add))
            to_act(dve.tensor_scalar(st[:, 0:8], st[:, 0:8], 1.0 / P, EPS, ALU.mult, ALU.add))
            link(dve.reciprocal(st[:, 0:8], st[:, 0:8]))
            link(tt(x8, blocks8, wide(st[:, 0:8], P), ALU.mult))
            o2 = two(g_t[:, :])
            to_act(tt(o2, o2, over(g_norm[:, :], NT), ALU.mult))
            to_pe(tt(o2, o2, g_g[:, :, :], ALU.mult))
            from_pe()
            split(alt_h[:, 4:8, :], alt_l[:, 4:8, :], four(ps[:, PC:PC + 1024]), "hgrn")

            kept(copy(p_c[:, :, :], four(arrived(4))))
            src = p_c
            for g in range(4):
                h = 1 << g
                dst = (p_a, p_b)[g % 2]
                link(tt(dst[:, g:4, h:T], src[:, g:4, h:T], src[:, g:4, 0:T - h], ALU.add))
                link(copy(dst[:, g:4, 0:h], src[:, g:4, 0:h]))
                src = dst
            link(copy(p_b[:, 0, :], p_a[:, 0, :]))
            link(copy(p_b[:, 2, :], p_a[:, 2, :]))
            dve.wait_ge(small_in, 16 * SMALL["pool"])
            link(tt(p_b[:, :, :], p_b[:, :, :], p_inv[:, :, :], ALU.mult))
            to_pe(tt(p_b[:, :, :], p_b[:, :, :], p_c[:, :, :], ALU.subtract))
            from_pe()
            for g in range(4):
                link(dve.tensor_scalar(p_a[:, g, :], ps[:, PC + g * T:PC + g * T + T], col("pool_scale", g), None, ALU.mult))
            split(alt_h[:, 8:12, :], alt_l[:, 8:12, :], p_a[:, :, :], "pool")

            kept(copy(s_u[:, :, :], two(arrived(4))))
            kept(copy(s_v[:, :, :], two(arrived(4))))
            dve.wait_ge(small_in, 16 * SMALL["sgu"])
            to_act(copy(st[:, 16:17], s_v[:, 0, 0:1]))
            to_act(copy(st[:, 16:17], s_v[:, 0, 0:1]))
            for n in range(NT):
                link(dve.bn_stats(st[:, 64 + 6 * n:70 + 6 * n], s_v[:, n, :]))
                link(dve.bn_aggr(st[:, 40 + 2 * n:42 + 2 * n], st[:, 64 + 6 * n:70 + 6 * n]))
            to_act(dve.tensor_scalar(st[:, 32:34], st[:, 41:44:2], EPS, None, ALU.add))
            link(dve.reciprocal(st[:, 32:34], st[:, 32:34]))
            for n in range(NT):
                link(dve.tensor_scalar(s_v[:, n, :], s_v[:, n, :], st[:, 40 + 2 * n:41 + 2 * n], st[:, 32 + n:33 + n],
                                       ALU.subtract, ALU.mult))
            link(tt(s_v[:, :, :], s_v[:, :, :], over(s_g[:, :], NT), ALU.mult))
            to_pe(tt(s_v[:, :, :], s_v[:, :, :], over(s_b[:, :], NT), ALU.add))
            from_pe()
            to_pe(tt(s_wt[:, :, :], four(ps[:, PC:PC + 512]), over(tri, 4), ALU.mult))
            from_pe()
            vs = two(ps[:, PC:PC + 1024])
            for g in range(4):
                c = slice(g * P, g * P + P)
                x = dve.scalar_tensor_tensor(s_o[:, :, c], vs[:, :, c], col("sg_b", g), s_u[:, :, c], ALU.add, ALU.mult)
                to_pe(x) if g == 3 else link(x)
            from_pe()
            split(alt_h[:, 12:16, :], alt_l[:, 12:16, :], four(ps[:, PC:PC + 1024]), "sgu")

            dve.sem_inc(merge_added, 1)
            w.at("added")
            dve.memset(res[:, :, :], 0.0).then_inc(gate_read, 1)
            dve.wait_ge(gate_read, w.at("gate_read"))
            per = {"unit": 20, "added": 4, "gate_read": 4, "gate": 4}
            with dve.Fori(0, 4) as i, w.loop(i, 0, 4, per):
                for cb in range(NB):
                    dve.wait_ge(unit_done, w.at("unit", 5))
                    dve.wait_ge(gate_done, w.at("gate") + 1)
                    dve.wait_ge(gate_read, w.now("gate_read"))
                    dve.tensor_tensor(m_t[:, :, :], four(ps[:, 1024:2048]), m_g[:, :, :], ALU.mult).then_inc(gate_read, 1)
                    dve.wait_ge(gate_read, w.at("gate_read"))
                    sl = slice(4 * cb, 4 * cb + 4)
                    dve.tensor_tensor(res[:, sl, :], res[:, sl, :], m_t[:, :, :], ALU.add).then_inc(merge_added, 1)
                    dve.wait_ge(merge_added, w.at("added"))
            for q in range(4):
                split(alt_h[:, 4 * q:4 * q + 4, :], alt_l[:, 4 * q:4 * q + 4, :], res[:, 4 * q:4 * q + 4, :],
                      "mixed" if q == 3 else None)

            def outputs(name):
                residual(4, 4)
                tell(name, copy(st[:, 16:17], ident[:, 0:1]))

            def ffn(conv, name):
                for s in (conv_done, silu_used) if conv else (silu_used,):
                    dve.sem_inc(s, 1)
                w.at("conv")
                w.at("used")
                per = {"unit": 8, "silu": 1, "used": 1}
                if conv:
                    per |= {"conv": 1, "step": 7}
                with dve.Fori(0, FB) as i, w.loop(i, 0, FB, per):
                    w.at("unit", 8)
                    u = w.now("unit")
                    if conv:
                        dve.wait_ge(unit_done, u - 4)
                        gate = four(ps[:, 0:1024])

                        def tap(name):
                            t, r = ROW_AT[name]
                            return pcol[:, t, bass.ds(i * 4 + r, 4)]

                        link(tt(f_a[:, :, :], gate, wide(tap("cw2"), T), ALU.mult))
                        for j, s in ((1, 1), (0, 2)):
                            link(tt(f_b[:, :, 0:T - s], gate[:, :, 0:T - s], wide(tap(f"cw{j}"), T - s), ALU.mult))
                            link(tt(f_a[:, :, s:T], f_a[:, :, s:T], f_b[:, :, 0:T - s], ALU.add))
                        link(copy(st[:, 16:17], ident[:, 0:1]))
                        link(copy(st[:, 16:17], ident[:, 0:1]))
                        tt(f_a[:, :, :], f_a[:, :, :], wide(tap("cb"), T), ALU.add).then_inc(conv_done, 1)
                        dve.wait_ge(conv_done, w.at("conv"))
                    dve.wait_ge(unit_done, u)
                    dve.wait_ge(silu_done, w.at("silu"))
                    dve.tensor_tensor(hid[:, bass.ds(i * 4, 4), :], f_a[:, :, :], four(ps[:, 1024:2048]),
                                      ALU.mult).then_inc(silu_used, 1)
                    dve.wait_ge(silu_used, w.at("used"))

                def piece(k, parity, first):
                    w.at("unit", 4)
                    if not first:
                        dve.wait_ge(unit_done, w.now("unit") - 8)
                    src = hid[:, k, :] if isinstance(k, slice) else hid[:, bass.ds(k, 4), :]
                    dve.tensor_copy(f_h[:, parity], src).then_inc(dve_step, 1)
                    dve.wait_ge(dve_step, w.at("step"))
                    dve.tensor_tensor(f_l[:, parity], src, f_h[:, parity].bitcast(F32), ALU.subtract).then_inc(hidden_ready, 1)
                    w.at("hidden")

                piece(slice(0, 4), 0, True)
                piece(slice(4, 8), 1, True)
                with dve.Fori(0, 4) as i, w.loop(i, 0, 4, {"unit": 8, "hidden": 2, "step": 2}):
                    piece(i * 8 + 8, 0, False)
                    piece(i * 8 + 12, 1, False)
                piece(slice(40, 44), 0, False)
                dve.wait_ge(hidden_ready, w.now("hidden"))
                dve.wait_ge(unit_done, w.now("unit"))
                for cb in range(NB):
                    x = four(ps[:, cb * 1024:cb * 1024 + 1024])
                    sl = slice(4 * cb, 4 * cb + 4)
                    link(dve.scalar_tensor_tensor(res[:, sl, :], act_h[:, sl, :].bitcast(F32), ALPHA, x, ALU.mult, ALU.add))
                    x = dve.scalar_tensor_tensor(res[:, sl, :], act_l[:, sl, :].bitcast(F32), ALPHA, res[:, sl, :],
                                                 ALU.mult, ALU.add)
                    tell(name, x) if cb == 3 else link(x)

            outputs("mix_out")
            norm(0, act_h, act_l, "x1")
            dve.wait_ge(tokens_turned, 2)
            for q in range(4):
                x = copy(res[:, 4 * q:4 * q + 4, :], four(ps[:, q * 1024:q * 1024 + 1024]))
                tell("mem_tokens", x) if q == 3 else link(x)
            norm(1, alt_h, alt_l, "memory")
            kept(dve.tensor_scalar(x_k[:, :, :], four(arrived(4)), 128 ** -0.5, None, ALU.mult))
            kept(copy(x_v[:, :, :], two(arrived(4))))
            kept(copy(x_q[:, :, :], four(arrived(4))))
            for qt in range(NT):
                from_pe()
                link(copy(x_s[:, :, :], four(ps[:, PC:PC + 1024])))
                softmax(x_s[:, :, :], 4, T)
                from_pe()
                at = (slice(None), slice(0, 4), slice(qt * P, qt * P + P))
                split(alt_h[at], alt_l[at], four(ps[:, PO:PO + 512]), "xa" if qt else None)
            residual(1, 4)
            tell("xo", copy(st[:, 16:17], ident[:, 0:1]))
            norm(2, act_h, act_l, "x2")
            ffn(True, "ffn_out")
            norm(3, act_h, act_l, "x3")

            from_pe()
            for h in range(8):
                x = copy(b_vec[:, h, :], ps[:, h * 512:h * 512 + SKEW])
                tell("bias", x) if h == 7 else link(x)
            x = arrived(4)
            dve.wait_ge(small_in, 16 * SMALL["gates2"])
            kept(tt(l_gate[:, :, :], x[:, 0:128].rearrange("p (n c) -> p n c", n=2)[:, :, 0:8], over(l_gb[:, :], NT), ALU.add))
            f = l_gate[:, :, 4:8]
            link(dve.tensor_scalar(l_e[:, :, :], f, -1.0, None, ALU.mult))
            to_act(tt(l_e[:, :, :], l_e[:, :, :], f, ALU.min))
            to_act(dve.tensor_scalar(l_e[:, :, :], l_e[:, :, :], 1.0, None, ALU.add))
            link(dve.tensor_scalar(l_lf[:, :, :], f, 0.0, None, ALU.min))
            to_pe(tt(l_lf[:, :, :], l_lf[:, :, :], l_e[:, :, :], ALU.subtract))
            from_pe()
            link(copy(l_cum[:, :, :], ps[:, PC:PC + 8].rearrange("p (n h) -> p n h", n=2)))
            tell("gates2", tt(l_i[:, :, :], l_gate[:, :, 0:4], l_cum[:, :, :], ALU.subtract))
            for g in range(2):
                dve.wait_ge(small_in, 16 * SMALL[f"ml{g}"])
                for part in range(2):
                    x = four(arrived(4))
                    r = part * 8 + 4 * g

                    def tap(j):
                        return col(f"c2w{j}", r, 4)

                    link(tt(l_a[:, :, :], x, wide(tap(3), T), ALU.mult))
                    for j, s in ((2, 1), (1, 2), (0, 3)):
                        y = tt(l_b[:, :, 0:T - s], x[:, :, 0:T - s], wide(tap(j), T - s), ALU.mult)
                        kept(y) if j == 0 else link(y)
                        link(tt(l_a[:, :, s:T], l_a[:, :, s:T], l_b[:, :, 0:T - s], ALU.add))
                    to_act(tt(l_a[:, :, :], l_a[:, :, :], wide(col("cb2", r, 4), T), ALU.add))
                kept(copy(l_v[:, :, :], two(arrived(4))))
                kept(copy(l_o[:, :, :], two(arrived(4))))
                to_act(copy(st[:, 16:17], ident[:, 0:1]))
                to_pe(dve.tensor_scalar(l_k[:, :, :], l_k[:, :, :], 1.0 / 16, None, ALU.mult))
                for qt in range(NT):
                    n = P * (qt + 1)
                    from_pe()
                    for j in range(2):
                        link(dve.scalar_tensor_tensor(l_s[:, j, 0:n], ps[:, PC + j * T:PC + j * T + n],
                                                      l_cum[:, qt, 2 * g + j:2 * g + j + 1], l_tab[:, 2 * P - n:2 * P],
                                                      ALU.add, ALU.add))
                    m = st[:, 0:2]
                    link(dve.tensor_reduce(m, l_s[:, :, 0:n], AX, ALU.max))
                    link(tt(m, m, l_cum[:, qt, 2 * g:2 * g + 2], ALU.max))
                    link(dve.tensor_scalar(st[:, 8:10], m, -1.0, None, ALU.mult))
                    to_act(tt(l_s[:, :, 0:n], l_s[:, :, 0:n], wide(m, n), ALU.subtract))
                    qk = ps[:, PC + 512:PC + 1024].rearrange("p (j t) -> p j t", j=2)[:, :, 0:n]
                    link(tt(l_s[:, :, 0:n], l_s[:, :, 0:n], qk, ALU.mult))
                    link(dve.tensor_reduce(st[:, 4:6], l_s[:, :, 0:n], AX, ALU.add))
                    link(dve.tensor_scalar(st[:, 6:8], st[:, 4:6], -1.0, None, ALU.mult))
                    link(tt(st[:, 4:6], st[:, 4:6], st[:, 6:8], ALU.max))
                    link(tt(st[:, 4:6], st[:, 4:6], st[:, 8:10], ALU.max))
                    link(dve.reciprocal(st[:, 4:6], st[:, 4:6]))
                    to_pe(tt(l_s[:, :, 0:n], l_s[:, :, 0:n], wide(st[:, 4:6], n), ALU.mult))
                    from_pe()
                    link(copy(l_h[:, :], ps[:, PO:PO + 512]))
                    for j in range(2):
                        link(dve.bn_stats(st[:, 64 + 6 * j:70 + 6 * j], l_h[:, j * T:j * T + T]))
                        link(dve.bn_aggr(st[:, 40 + 2 * j:42 + 2 * j], st[:, 64 + 6 * j:70 + 6 * j]))
                    to_act(dve.tensor_scalar(st[:, 32:34], st[:, 41:44:2], EPS, None, ALU.add))
                    link(dve.reciprocal(st[:, 32:34], st[:, 32:34]))
                    for j in range(2):
                        link(dve.tensor_scalar(l_h[:, j * T:j * T + T], l_h[:, j * T:j * T + T], st[:, 40 + 2 * j:41 + 2 * j],
                                               st[:, 32 + j:33 + j], ALU.subtract, ALU.mult))
                    link(tt(l_h[:, :], l_h[:, :], l_norm[:, :], ALU.mult))
                    to_pe(tt(l_h[:, :], l_h[:, :], l_o[:, qt, :], ALU.mult))
                    from_pe()
                    at = (slice(None), slice(4 * g, 4 * g + 4), slice(qt * P, qt * P + P))
                    split(alt_h[at], alt_l[at], four(ps[:, PT_:PT_ + 512]), f"ml{g}" if qt else None)
            for g in range(2):
                kept(dve.tensor_scalar(x_q[:, :, :], four(arrived(4)), 128 ** -0.5, None, ALU.mult))
                kept(copy(x_k[:, :, :], four(arrived(4))))
                kept(copy(x_v[:, :, :], two(arrived(4))))
                dve.wait_ge(small_in, 16 * SMALL[f"di{g}"])
                link(tt(x_bias[:, :, :], x_bias[:, :, :], over(x_tab[:, 1, :], 4), ALU.add))
                for qt in range(NT):
                    n = P * (qt + 1)
                    from_pe()
                    link(tt(x_s[:, :, 0:n], four(ps[:, PC:PC + 1024])[:, :, 0:n], x_bias[:, :, T - n:T], ALU.add))
                    softmax(x_s[:, :, 0:n], 4, n, weight=over(x_tab[:, 0, T - n:T], 4))
                    from_pe()
                    at = (slice(None), slice(8 + 4 * g, 12 + 4 * g), slice(qt * P, qt * P + P))
                    split(alt_h[at], alt_l[at], four(ps[:, PO:PO + 512]), f"di{g}" if qt else None)
            outputs("out2")
            norm(4, act_h, act_l, "x4")
            turned_tokens(3, alt_h, alt_l, "mem2")
            per = {"unit": 24, "block": 6, "step": 12, "result": 4, "mapped": 2, "left": 2}
            with dve.Fori(0, 2) as i, w.loop(i, 0, 2, per):
                for h in range(2):
                    kept(dve.tensor_scalar(x_k[:, :, :], four(arrived(4)), 512 ** -0.5, None, ALU.mult))
                    kept(copy(x_v[:, :, :], two(arrived(4))))
                    kept(copy(x_q[:, :, :], four(arrived(4))))
                    from_pe()
                    link(copy(x_s[:, 0:2, :], two(ps[:, PC:PC + 512])))
                    softmax(x_s[:, 0:2, :], 2, T)
                    from_pe()
                    link(copy(res[:, bass.ds(i * 8 + h * 4, 4), :], four(ps[:, PC:PC + 1024])))
                    link(copy(st[:, 16:17], ident[:, 0:1]))
            for q in range(4):
                split(alt_h[:, 4 * q:4 * q + 4, :], alt_l[:, 4 * q:4 * q + 4, :], res[:, 4 * q:4 * q + 4, :],
                      "xb" if q == 3 else None)
            outputs("xo2")
            norm(5, act_h, act_l, "x5")
            ffn(False, "ffn2_out")
            norm(6, None, None, "y")
            dve.wait_ge(tokens_turned, 4)
            for q in range(4):
                h, c = q // 2, (q % 2) * 1024
                x = copy(outt[:, h, c:c + 1024], ps[:, q * 1024:q * 1024 + 1024])
                tell("end", x) if q == 3 else link(x)
            assert w.n["unit"] == UNITS


def kernel(**inputs):
    import concourse.bacc as bacc
    from concourse.bass_utils import run_bass_kernel_spmd

    nc = bacc.Bacc("TRN2", target_bir_lowering=False, num_devices=1)
    arrays, aps = {}, {}
    for name, value in inputs.items():
        v = np.ascontiguousarray(value)
        arrays[f"in_{name}"] = v
        aps[name] = nc.dram_tensor(f"in_{name}", v.shape, mybir.dt.from_np(v.dtype), kind="ExternalInput").ap()
    _, table = shape_tables()
    arrays["shape_tables"] = table
    tables = nc.dram_tensor("shape_tables", table.shape, F32, kind="ExternalInput").ap()
    out = nc.dram_tensor("out_x", (1, T, D), F32, kind="ExternalOutput").ap()
    two_blocks(nc, aps, tables, out)
    r = run_bass_kernel_spmd(nc, [arrays], core_ids=[0])
    return r.results[0]["out_x"]
```

```python
from contextlib import ExitStack, contextmanager

import numpy as np
import concourse.bass as bass
from concourse import mybir

F32 = mybir.dt.float32
F32R = mybir.dt.float32r
ALU = mybir.AluOpType
ACT = mybir.ActivationFunctionType
AX = mybir.AxisListType.X

P = 128
T = 256
NT = T // P
D = 2048
DC = D // P
CB = 4
UNIT = CB * P
SLOTS = 4
NB = D // UNIT
FF = 5632
FC = FF // P
FB = FF // UNIT
ALPHA = 2.0 ** 0.25
EPS = 1e-5
NEG = -1e30
FAR = 1e35
MIX = 512
C_Q, C_KV, C_HG, C_POOL, C_SG, C_MERGE = 0, 512, 1304, 3352, 3864, 4888
C2_GATE, C2_DQ = 4096, 4104
NCMP = 15
REL = 32
SKEW = 384

STAGES = [("nsa_q", 4), ("nsa_kv", 8), ("hgrn", 16), ("pool", 4), ("sgu", 8), ("gates", 64), ("merge", 16),
          ("mix_out", 16), ("xmem", 8), ("xq", 4), ("xo", 4), ("ffn_in", 8 * FB), ("ffn_out", 4 * FB),
          ("gates2", 4), ("mlstm", 16), ("mlstm1", 16), ("dilated", 24), ("out2", 16), ("x2", 48), ("xo2", 16),
          ("ffn2_in", 8 * FB), ("ffn2_out", 4 * FB)]
BASE, _n = {}, 0
for _name, _u in STAGES:
    BASE[_name] = _n
    _n += _u
UNITS = _n

FIRST_GATE = 10
LSTM_FILL = [(4, 3, 3, 3, 3), (4, 2, 2, 2, 2)]

F_BLOCK = [("F", s * P, P, 0, s * T) for s in range(CB)]
T_BLOCK = [("T", 0, UNIT, h, h * UNIT) for h in range(NT)]
KV0_BLOCK = [("F", 0, P, 0, 0), ("F", 128, P, 0, 256), ("F", 256, P, 0, 512),
             ("T", 384, P, 0, 768), ("T", 384, P, 1, 896)]
KV1_BLOCK = [("F", 0, P, 0, 0), ("T", 128, P, 0, 256), ("T", 128, P, 1, 384),
             ("T", 256, 24, 0, 512), ("T", 256, 24, 1, 576)]
GATE_BLOCK = [("T", 0, 8, 0, 0), ("T", 0, 8, 1, 64)]

ROWS = [(0, f"ln_g{i}", DC) for i in range(7)] + [(1, f"ln_b{i}", DC) for i in range(7)] + [
    (1, "lb", 4), (1, "pool_scale", 4), (1, "sg_b", 4),
    (2, "cw0", FC), (2, "cw1", FC), (2, "cb2", DC),
    (3, "cw2", FC), (3, "cb", FC),
    (4, "c2w0", DC), (4, "c2w1", DC), (4, "c2w2", DC), (4, "c2w3", DC)]
ROW_AT, ROW_N = {}, [0] * 5
for _t, _name, _r in ROWS:
    ROW_AT[_name] = (_t, ROW_N[_t])
    ROW_N[_t] += _r


def shape_tables():
    p = np.arange(P)[:, None]
    u = np.arange(2 * P)[None, :]
    dist = P + p - u
    ident = np.eye(P)
    mean = np.full((P, P), 1.0 / D)
    tri = (p <= np.arange(P)[None, :]) * 1.0
    ones = np.ones((P, P))
    core = np.concatenate([ident, mean, tri, ones], 1)
    alibi = np.where(dist >= 0, dist, FAR)
    end = 16 * np.arange(16) + 31
    cmp_d = [np.where(t0 + p - end >= 0, t0 + p - end, FAR) for t0 in (0, P)]
    nsa = np.concatenate([alibi] + cmp_d, 1)
    level = []
    s, t = np.arange(P)[:, None], np.arange(P)[None, :]
    for l in range(7):
        h = 1 << l
        level.append((s // (2 * h) == t // (2 * h)) & (s % (2 * h) < h) & (t % (2 * h) >= h))
    level = np.concatenate(level, 1) * 1.0
    cnt = np.concatenate([1.0 / np.minimum(np.arange(T) + 1, w) for w in (2, 4, 8, 16)])
    cnt = np.broadcast_to(cnt, (P, 4 * T))
    mult = ((dist >= 0) & (dist <= 128)) * 1.0 + ((dist >= 0) & (dist % 4 == 0)) + ((dist >= 0) & (dist % 16 == 0))
    dil = np.concatenate([mult, np.where(mult > 0, 0.0, NEG)], 1)
    causal = np.where(dist >= 0, 0.0, NEG)
    d = np.maximum(255 - np.arange(SKEW), 0)
    big = np.maximum(d, 1).astype(np.float32)
    lg = 16 + (np.log(big / 16) / np.float32(np.log(2048 / 16)) * 16).astype(np.int32)
    bucket = np.where(d < 16, d, np.minimum(lg, REL - 1))
    hot = np.zeros((P, SKEW))
    hot[:REL] = (np.arange(REL)[:, None] == bucket[None, :])
    parts = {"core": core, "nsa": nsa, "level": level, "cnt": cnt, "dil": dil, "causal": causal, "hot": hot}
    at, n = {}, 0
    for k, v in parts.items():
        at[k] = (n, n + v.shape[1])
        n += v.shape[1]
    return at, np.concatenate(list(parts.values()), 1).astype(np.float32)


class Walk:

    def __init__(self):
        self.n, self.off = {}, {}

    def at(self, key, k=1):
        self.n[key] = self.n.get(key, 0) + k
        return self.n[key] + self.off.get(key, 0)

    def now(self, key):
        return self.n.get(key, 0) + self.off.get(key, 0)

    @contextmanager
    def loop(self, i, first, times, per):
        begin = dict(self.n)
        self.off = {k: (i - first) * v for k, v in per.items()}
        yield
        for k in set(self.n) | set(per):
            assert self.n.get(k, 0) - begin.get(k, 0) == per.get(k, 0), (k, self.n.get(k, 0) - begin.get(k, 0))
            self.n[k] = begin.get(k, 0) + per.get(k, 0) * times
        self.off = {}


class Shadow:

    def __init__(self, first, end, blocks):
        self.first, self.end, self.blocks = BASE[first], BASE[end], blocks
        assert self.end - self.first == CB * len(blocks)

    def upto(self, unit, k):
        assert k <= SLOTS
        return min(unit + k, self.end)

    def complete(self, unit):
        return (unit - self.first) // CB


def two_blocks(nc, a, tables, out):
    tab_at, _ = shape_tables()
    ctx = ExitStack()
    with ctx:
        def place(name, at, shape, dt=F32):
            n = int(np.prod(shape[1:])) * 4
            assert at + n <= 229344, (name, at + n)
            return nc.alloc_sbuf_tensor_at(name, shape, dt, offset=at)

        def sem(name):
            return ctx.enter_context(nc.semaphore(name))

        KB = 1024
        W0 = 16512
        wraw = place("wraw", W0, [P, SLOTS, CB, UNIT])
        whi = place("whi", W0 + 32 * KB, [P, SLOTS, CB, UNIT], F32R)
        wlo = place("wlo", W0 + 64 * KB, [P, SLOTS, CB, UNIT], F32R)
        A0 = W0 + 96 * KB
        act_h = place("act_h", A0, [P, DC, T], F32R)
        act_l = place("act_l", A0 + 16 * KB, [P, DC, T], F32R)
        X0 = A0 + 32 * KB
        alt_h = place("alt_h", X0, [P, DC, T], F32R)
        alt_l = place("alt_l", X0 + 16 * KB, [P, DC, T], F32R)
        hid = place("hid", X0, [P, FC, T])
        Z0 = X0 + 32 * KB
        res = place("res", Z0, [P, DC, T])
        tok = place("tok", Z0, [P, NT, D])
        Y0 = Z0 + 16 * KB
        core = place("core", Y0, [P, 4 * P])
        pcol = place("pcol", Y0 + 2 * KB, [P, 5, P])
        Y1 = Y0 + 2 * KB + 5 * P * 4
        ident, mean_w, tri, ones = (core[:, P * j:P * j + P] for j in range(4))
        prow = place("prow", Y1, [P, 5, P])
        outt = place("outt", X0, [P, NT, D])

        ln_a = place("ln_a", Y1 + 16 * KB, [P, T])
        ln_s1 = place("ln_s1", Y1 + 17 * KB, [P, T])
        ln_s2 = place("ln_s2", Y1 + 18 * KB, [P, T])
        ln_t = place("ln_t", Y1 + 19 * KB, [P, T])
        ln_c = place("ln_c", Y1 + 20 * KB, [P, T])
        ln_rstd = place("ln_rstd", Y1 + 21 * KB, [P, T])
        ln_sq = place("ln_sq", Y1 + 22 * KB, [P, CB, T])
        n_q = place("n_q", Y1, [P, 4, T])
        n_kv = place("n_kv", Y1 + 4 * KB, [P, 4, T])
        n_v = place("n_v", Y1 + 8 * KB, [P, 2, NT, P])
        n_s = place("n_s", Y1 + 10 * KB, [P, 4, T])
        n_pt = place("n_pt", Y1 + 14 * KB, [P, NT, 4 * P])
        n_win = place("n_win", Y1 + 18 * KB, [P, 2, 32, NCMP])
        n_tab = place("n_tab", Y1 + 22 * KB, [P, 2 * P + 32])
        n_gate = place("n_gate", Y1 + 24 * KB, [P, NT, 24])
        n_kc = place("n_kc", Y1 + 24 * KB + 256, [P, 16])
        n_vc = place("n_vc", Y1 + 24 * KB + 512, [16, 2, 64])
        n_pos = place("n_pos", Y1 + 25 * KB, [P, 2, 32])
        st = place("st", Y1 + 27 * KB - 256, [P, 128])
        n_w = place("n_w", Z0, [P, 2, 32, 64])
        mixed_in = place("mixed_in", X0 + 16 * KB, [P, DC, T])
        g_out = place("g_out", Z0 + 12 * KB, [P, 4 * T])
        g_q = place("g_q", X0, [P, 4, T])
        g_k = place("g_k", X0 + 4 * KB, [P, 4, T])
        g_v = place("g_v", X0 + 8 * KB, [P, NT, MIX])
        g_g = place("g_g", X0 + 12 * KB, [P, NT, MIX])
        g_p = place("g_p", Y1 + 16 * KB, [P, 4 * T])
        g_mask = place("g_mask", Y1 + 20 * KB, [P, 7, P])
        g_norm = place("g_norm", Y1 + 24 * KB, [P, MIX])
        g_qh = place("g_qh", Y1, [P, 4 * T])
        g_kh = place("g_kh", Y1 + 4 * KB, [P, 4 * T])
        g_a = place("g_a", Y1 + 8 * KB, [P, 4, NT, P])
        g_t = place("g_t", Y1 + 12 * KB, [P, 4 * T])
        p_c = place("p_c", Z0, [P, 4, T])
        p_inv = place("p_inv", Y1, [P, 4, T])
        p_w = place("p_w", Y1 + 4 * KB, [P, 4, P])
        p_a = place("p_a", Y1 + 6 * KB, [P, 4, T])
        p_b = place("p_b", Y1 + 10 * KB, [P, 4, T])
        s_u = place("s_u", Z0 + 4 * KB, [P, NT, MIX])
        s_v = place("s_v", Z0 + 8 * KB, [P, NT, MIX])
        s_w = place("s_w", Y1, [P, 4, P])
        s_wt = place("s_wt", Y1 + 2 * KB, [P, 4, P])
        s_g = place("s_g", Y1 + 4 * KB, [P, MIX])
        s_b = place("s_b", Y1 + 6 * KB, [P, MIX])
        s_o = place("s_o", Y1 + 8 * KB, [P, NT, MIX])
        m_g = place("m_g", Y1, [P, 2, 4 * T])
        m_t = place("m_t", Y1 + 8 * KB, [P, 4, T])
        x_q = place("x_q", Y1, [P, 4, T])
        x_k = place("x_k", Y1 + 4 * KB, [P, 4, T])
        x_v = place("x_v", Y1 + 8 * KB, [P, NT, MIX])
        x_s = place("x_s", Y1 + 12 * KB, [P, 4, T])
        x_pt = place("x_pt", Y1 + 16 * KB, [P, NT, 4 * P])
        x_v2 = place("x_v2", Y1 + 20 * KB, [P, NT, MIX])
        d_in = [[place(f"d{x}{g}", at + 4 * j * KB, [P, 4, T] if x != "v" else [P, NT, MIX]) for j, x in enumerate("qkv")]
                for g, at in ((0, X0), (1, Z0))]
        d_s = place("d_s", Y1, [P, 4, T])
        d_pt = place("d_pt", Y1 + 4 * KB, [P, NT, 4 * P])
        d_bias = place("d_bias", Y1 + 8 * KB, [P, 4, T])
        d_tab = place("d_tab", Y1 + 12 * KB, [P, 2, T])
        f_h = place("f_h", Y1, [P, 2, CB, T], F32R)
        f_l = place("f_l", Y1 + 8 * KB, [P, 2, CB, T], F32R)
        f_a = place("f_a", Y1 + 16 * KB, [P, CB, T])
        f_b = place("f_b", Y1 + 20 * KB, [P, CB, T])
        l_in = [[place(f"l{x}{g}", at + 4 * j * KB, [P, 4, T] if x in "qk" else [P, NT, MIX]) for j, x in enumerate("qkvo")]
                for g, at in ((0, X0), (1, Z0))]
        l_norm = place("l_norm", Y1 + 16 * KB, [P, MIX])
        l_tab = place("l_tab", Y1 + 18 * KB, [P, 2 * P])
        l_s = place("l_s", Y1 + 19 * KB, [P, 2, T])
        l_gate = place("l_gate", Y1 + 21 * KB, [P, NT, 8])
        l_gb = place("l_gb", Y1 + 21 * KB + 128, [P, 8])
        l_lf = place("l_lf", Y1 + 21 * KB + 256, [P, NT, 4])
        l_cum = place("l_cum", Y1 + 21 * KB + 512, [P, NT, 4])
        l_i = place("l_i", Y1 + 21 * KB + 640, [P, NT, 4])
        l_e = place("l_e", Y1 + 21 * KB + 768, [P, NT, 4])
        l_a = place("l_a", Y1, [P, 4, T])
        l_b = place("l_b", Y1 + 4 * KB, [P, 4, T])
        l_pt = place("l_pt", Y1 + 8 * KB, [P, NT, 2 * P])
        l_h = place("l_h", Y1 + 10 * KB, [P, MIX])
        b_vec = place("b_vec", Z0, [P, 8, SKEW])
        b_hot = place("b_hot", Y1 + 16 * KB, [REL, SKEW])
        b_rel = place("b_rel", Y1 + 18 * KB, [REL, 8])

        ps = ctx.enter_context(nc.psum_tensor("ps", [P, 8 * 512], F32))
        PC = 2048
        PT_ = 3072
        PO = 3584
        gate_dram = nc.dram_tensor("gate_dram", [4, NB, P, 4 * T], F32)
        bias_dram = nc.dram_tensor("bias_dram", [8, P, SKEW], F32)

        loaded = [sem(f"loaded{j}") for j in range(SLOTS)]
        hi_done = sem("hi_done")
        lo_done = sem("lo_done")
        unit_done = sem("unit_done")
        block_saved = sem("block_saved")
        tokens_in = sem("tokens_in")
        tokens_turned = sem("tokens_turned")
        operand = sem("operand")
        params_in = sem("params_in")
        params_turned = sem("params_turned")
        small_in = sem("small_in")
        dve_step = sem("dve_step")
        act_step = sem("act_step")
        centred = sem("centred")
        squares_done = sem("squares_done")
        piece_ready = sem("piece_ready")
        result_ready = sem("result_ready")
        shifted = sem("shifted")
        mapped = sem("mapped")
        left_ready = sem("left_ready")
        turned = sem("turned")
        turned_saved = sem("turned_saved")
        gate_done = sem("gate_done")
        gate_spilled = sem("gate_spilled")
        gate_loaded = [sem(f"gate_loaded{j}") for j in range(2)]
        conv_done = sem("conv_done")
        silu_done = sem("silu_done")
        silu_used = sem("silu_used")
        merge_added = sem("merge_added")
        hidden_ready = sem("hidden_ready")
        bias_out = sem("bias_out")
        out_done = sem("out_done")

        OPERANDS = ["turn_params", "nsa", "mem_tokens", "xa", "bias", "gates2", "ml0", "ml1", "di0", "y", "end"]
        WHOLE = ["x", "branches", "mixed", "x1", "memory", "x2", "x3", "mixed2", "x4", "mem2", "xb", "x5"]
        SMALL = {"nsa": 5, "hgrn": 7, "pool": 9, "sgu": 12, "bias": 14, "gates2": 16, "ml0": 17, "ml1": 18, "di0": 20, "di1": 21}

        def after(name):
            return OPERANDS.index(name) + 1

        def pieces(name, n=4):
            return 4 * WHOLE.index(name) + n

        def col(name, c=0, n=1):
            t, r = ROW_AT[name]
            return pcol[:, t, r + c:r + c + n]

        def wide(ap, n):
            return ap.unsqueeze(2).to_broadcast([ap.shape[0], ap.shape[1], n])

        def over(ap, n):
            return ap.unsqueeze(1).to_broadcast([ap.shape[0], n, ap.shape[1]])

        def pair(b):
            return ps[:, (b % 2) * 1024:(b % 2) * 1024 + 1024]

        def tab(name):
            x, y = tab_at[name]
            return tables[:, x:y]

        def rows(w, r0, c0, cols=UNIT):
            return w[r0:r0 + UNIT, c0:c0 + cols].rearrange("(k p) n -> p k n", p=P)

        win, win2 = a["w_in"][0], a["w_in_2"][0]
        wb = a["w_branch"][0]
        gains = [a["ln_mix_g"][0], a["mem_ln_g"], a["ln_x_g"][0], a["ln_ffn_g"][0]] + [a["ln_g_2"][0, j] for j in range(3)]
        biases = [a["ln_mix_b"][0], a["mem_ln_b"], a["ln_x_b"][0], a["ln_ffn_b"][0]] + [a["ln_b_2"][0, j] for j in range(3)]
        prow_src = {f"ln_g{j}": gains[j] for j in range(7)} | {f"ln_b{j}": biases[j] for j in range(7)}
        prow_src |= {"lb": a["hgrn_lb_logits"][0], "pool_scale": a["pool_scale"][0], "cb": a["ffn_conv_b"][0],
                     "cb2": a["conv_b_2"][0]}
        prow_src |= {f"cw{j}": a["ffn_conv_w"][0, j] for j in range(3)} | {f"c2w{j}": a["conv_w_2"][0, j] for j in range(4)}
        behind_sparse = Shadow("hgrn", "merge", [("F", g_q), ("F", g_k), ("T", g_v), ("T", g_g), ("F", p_c),
                                                 ("T", s_u), ("T", s_v)] + [("F", None)] * (4 * NB))
        behind_lstm = Shadow("mlstm1", "out2", [*zip("FFTT", l_in[1]), *zip("FFT", d_in[0]), *zip("FFT", d_in[1])])
        block = ctx.enter_context(nc.Block())

        @block.sync
        def _(sp):
            w = Walk()

            def load(src, cols=UNIT, perm=False):
                g = w.at("unit")
                slot = (w.n["unit"] - 1) % SLOTS
                if w.n["unit"] > SLOTS:
                    sp.wait_ge(lo_done, g - SLOTS)
                if perm:
                    for j in range(4):
                        for h in range(2):
                            sp.dma_start(wraw[:, slot, :, j * P + h * 64:j * P + h * 64 + 64],
                                         src[:, :, h * 256 + j * 64:h * 256 + j * 64 + 64]).then_inc(loaded[slot], 16)
                else:
                    sp.dma_start(wraw[:, slot, :, 0:cols], src).then_inc(loaded[slot], 16)

            def column(mat, c0, cols=UNIT, k=D, r0=0):
                for u in range(k // UNIT):
                    load(rows(mat, r0 + u * UNIT, c0, cols), cols)

            sp.dma_start(tok[:, :, :], a["x"][0].rearrange("(n p) d -> p n d", p=P)).then_inc(tokens_in, 16)
            for u in range(4):
                load(rows(win, u * UNIT, C_Q), perm=True)
            column(win, C_KV)
            column(win, C_KV + UNIT, 280)
            for j in range(4):
                column(win, C_HG + j * MIX)
            column(win, C_POOL)
            column(win, C_SG)
            column(win, C_SG + MIX)
            for n in range(4):
                for cb in range(NB):
                    column(win, C_MERGE + n * D + cb * UNIT)
            with sp.Fori(0, 4) as i, w.loop(i, 0, 4, {"unit": 4}):
                for cb in range(NB):
                    load(wb[i, :, cb * UNIT:(cb + 1) * UNIT].rearrange("(k p) n -> p k n", p=P))

            def square(mat):
                with sp.Fori(0, NB // 2) as i, w.loop(i, 0, NB // 2, {"unit": 8}):
                    for cb in range(2):
                        for u in range(4):
                            load(mat[u * UNIT:(u + 1) * UNIT, bass.ds(i * 2 * UNIT + cb * UNIT, UNIT)]
                                 .rearrange("(k p) n -> p k n", p=P))

            def ffn(gate, gate_c, up, up_c, down):
                with sp.Fori(0, FB) as i, w.loop(i, 0, FB, {"unit": 8}):
                    for mat, c0 in ((gate, gate_c), (up, up_c)):
                        for u in range(4):
                            load(mat[u * UNIT:(u + 1) * UNIT, bass.ds(i * UNIT + c0, UNIT)]
                                 .rearrange("(k p) n -> p k n", p=P))
                with sp.Fori(0, FB) as i, w.loop(i, 0, FB, {"unit": 4}):
                    for cb in range(NB):
                        load(down[bass.ds(i * UNIT, UNIT), cb * UNIT:(cb + 1) * UNIT]
                             .rearrange("(k p) n -> p k n", p=P))

            square(a["w_mix_out"][0])
            column(a["xattn_k"][0], 0)
            sp.wait_ge(piece_ready, pieces("x1"))
            sp.dma_start(tok[:, :, :], a["mem"][0].rearrange("(n p) d -> p n d", p=P)).then_inc(tokens_in, 16)
            column(a["xattn_v"][0], 0)
            column(a["xattn_q"][0], 0)
            for cb in range(NB):
                column(a["xattn_o"][0], cb * UNIT, k=UNIT)
            ffn(a["ffn_in"][0], 0, a["ffn_in"][0], FF, a["ffn_out"][0])
            column(win2, C2_GATE, 8)
            for g in range(2):
                for c0 in (0, 1024, 2048, 3072):
                    column(win2, c0 + g * UNIT)
            for g in range(2):
                for c0 in (0, 1024, 2048):
                    column(win2, C2_DQ + c0 + g * UNIT)
            square(a["w_out_2"][0])
            sp.wait_ge(piece_ready, pieces("x4"))
            sp.dma_start(tok[:, :, :], a["mem_2"][0].rearrange("(n p) d -> p n d", p=P)).then_inc(tokens_in, 16)
            with sp.Fori(0, 4) as i, w.loop(i, 0, 4, {"unit": 12}):
                for mat in (a["xk_2"][0], a["xv_2"][0], a["xq_2"][0]):
                    for u in range(4):
                        load(mat[u * UNIT:(u + 1) * UNIT, bass.ds(i * UNIT, UNIT)]
                             .rearrange("(k p) n -> p k n", p=P))
            square(a["xo_2"][0])
            ffn(a["w1_2"][0], 0, a["w3_2"][0], 0, a["w2_2"][0])
            assert w.n["unit"] == UNITS
            sp.wait_ge(operand, after("end"))
            sp.dma_start(out[0].rearrange("(n p) d -> p n d", p=P), outt[:, :, :]).then_inc(out_done, 16)
            sp.wait_ge(out_done, 16)

        @block.gpsimd
        def _(pool):
            with pool.Fori(0, UNITS // SLOTS) as i:
                for slot in range(SLOTS):
                    pool.wait_ge(hi_done, i * SLOTS + (slot + 1))
                    pool.tensor_tensor(wlo[:, slot], wraw[:, slot], whi[:, slot].bitcast(F32),
                                       ALU.subtract).then_inc(lo_done, 1)

        @block.scalar
        def _(act):
            w = Walk()

            def hi(n, first_load=16):
                for _ in range(n):
                    g = w.at("unit")
                    slot = (w.n["unit"] - 1) % SLOTS
                    act.wait_ge(loaded[slot], w.at(f"slot{slot}", first_load))
                    if w.n["unit"] > SLOTS:
                        act.wait_ge(unit_done, g - SLOTS)
                    act.activation(whi[:, slot], wraw[:, slot], ACT.Copy).then_inc(hi_done, 1)

            def small(dst, src):
                act.dma_start(dst, src).then_inc(small_in, 16)

            def mapping(*ins):
                act.wait_ge(shifted, w.at("shifted"))
                for n, (dst, src, fn) in enumerate(ins):
                    x = act.activation(dst, src, fn)
                    if n == len(ins) - 1:
                        x.then_inc(mapped, 1)

            def save_turned(dst, src):
                act.wait_ge(turned, w.at("turned"))
                act.activation(dst, src, ACT.Copy).then_inc(turned_saved, 1)

            def square(cb):
                act.wait_ge(centred, w.at("centred"))
                act.activation(ln_sq[:, :, :], res[:, 4 * cb:4 * cb + 4, :], ACT.Square).then_inc(squares_done, 1)

            def norm(ahead=0, units=4):
                for cb in range(4):
                    hi(ahead if cb == 3 else units)
                    square(cb)
                mapping((ln_rstd[:, :], ln_rstd[:, :], ACT.Sqrt))

            at_unit = [behind_sparse.first]
            gates = [0]

            def fill(shadow, k):
                hi(min(at_unit[0] + SLOTS, shadow.end) - w.n["unit"])
                while shadow is behind_sparse and gates[0] < (at_unit[0] - BASE["gates"]) // CB:
                    save_gates()
                at_unit[0] = shadow.upto(at_unit[0], k)

            def save_gates():
                n = gates[0]
                if n:
                    act.wait_ge(gate_spilled, 16 * n)
                act.wait_ge(unit_done, BASE["gates"] + CB * (n + 1))
                act.activation(g_out[:, :], pair(FIRST_GATE + n), ACT.Sigmoid).then_inc(gate_done, 1)
                act.wait_ge(gate_done, n + 1)
                act.dma_start(gate_dram[n // NB, n % NB], g_out[:, :]).then_inc(gate_spilled, 16)
                gates[0] += 1

            for t, name, r in ROWS:
                at = ROW_AT[name][1]
                src = a["sg_b"][0] if name == "sg_b" else prow_src[name].rearrange("(c p) -> c p", p=P)
                act.dma_start(prow[at:at + r, t, :], src).then_inc(params_in, 16)
            act.dma_start(core[:, :], tab("core")).then_inc(params_in, 16)
            hi(4, 128)
            act.wait_ge(piece_ready, pieces("x"))
            small(n_tab[:, :], tab("nsa"))
            for g in range(2):
                small(n_w[64 * g:64 * g + 64], a["nsa_cmp_w"][0].rearrange("v l d e -> d v l e"))
                with nc.allow_non_contiguous_dma("small"):
                    small(n_pos[64 * g:64 * g + 64], a["nsa_cmp_pos"][0].rearrange("v l d -> d v l"))
            hi(8)
            hi(4)
            mapping((n_gate[:, :, :], n_gate[:, :, :], ACT.Sigmoid))
            for g in range(2):
                for qt in range(NT):
                    for br in range(3):
                        n = NCMP if br == 0 else P * (qt + 1)
                        fill(behind_sparse, 3)
                        mapping((n_s[:, :, 0:n], n_s[:, :, 0:n], ACT.Exp))
                        for kt in range(1 if br == 0 else qt + 1):
                            kn = NCMP if br == 0 else P
                            save_turned(n_pt[0:kn, kt, :], ps[0:kn, PT_:PT_ + 512])
            act.wait_ge(operand, after("nsa"))
            small(g_mask[:, :, :], tab("level").rearrange("p (l n) -> p l n", l=7))
            small(g_norm[:, :], a["hgrn_norm_g"][0].partition_broadcast(P))
            mapping((st[:, 0:4], st[:, 0:4], ACT.Exp))
            fill(behind_sparse, 4)
            mapping((g_k[:, :, :], g_k[:, :, :], ACT.Sigmoid))
            mapping((g_p[:, :], g_k[:, :, :].rearrange("p h t -> p (h t)"), ACT.Ln))
            for l in range(8):
                h = 1 << l
                fill(behind_sparse, 3)
                v = g_p[:, :].rearrange("p (m two h) -> p m two h", two=2, h=h)
                e = g_t[:, :].rearrange("p (m two h) -> p m two h", two=2, h=h)
                mapping((e[:, :, 0, :], e[:, :, 0, :], ACT.Exp), (e[:, :, 1, :], v[:, :, 1, :], ACT.Exp))
            fill(behind_sparse, 2)
            fill(behind_sparse, 3)
            mapping((g_t[:, :], ps[:, PC:PC + 1024], ACT.Square))
            mapping((st[:, 0:8], st[:, 0:8], ACT.Sqrt))
            mapping((g_g[:, :, :], g_g[:, :, :], ACT.Silu))
            act.wait_ge(piece_ready, pieces("branches", 2))
            small(p_inv[:, :, :], tab("cnt").rearrange("p (g t) -> p g t", g=4))
            small(p_w[:, :, :], a["pool_w"][0].rearrange("g c d -> c g d"))
            fill(behind_sparse, 3)
            act.wait_ge(piece_ready, pieces("branches", 3))
            small(s_w[:, :, :], a["sg_w"][0].rearrange("g q p -> q g p"))
            small(s_g[:, :], a["sg_ln_g"][0].partition_broadcast(P))
            small(s_b[:, :], a["sg_ln_b"][0].partition_broadcast(P))
            fill(behind_sparse, 4)
            mapping((s_u[:, :, :], s_u[:, :, :], ACT.Gelu_apprx_tanh))
            mapping((s_v[:, :, :], s_v[:, :, :], ACT.Gelu_apprx_tanh))
            mapping((st[:, 32:34], st[:, 32:34], ACT.Sqrt))
            fill(behind_sparse, 1)
            fill(behind_sparse, 2)
            while at_unit[0] < behind_sparse.end:
                fill(behind_sparse, 4)
            while gates[0] < 4 * NB:
                save_gates()
            act.wait_ge(gate_spilled, 16 * 4 * NB)
            act.wait_ge(piece_ready, pieces("branches"))
            with act.Fori(0, 4) as i, w.loop(i, 0, 4, {"unit": 4, "added": 4, **{f"slot{s}": 16 for s in range(4)}}):
                for cb in range(NB):
                    act.wait_ge(merge_added, w.at("added"))
                    act.dma_start(m_g[:, cb % 2, :], gate_dram.ap()[bass.ds(i, 1), cb].rearrange("o p n -> (o p) n")
                                  ).then_inc(gate_loaded[cb % 2], 16)
                    hi(1)

            def ffn(name, conv, ahead):
                per = {"unit": 8, "silu": 1, **{f"slot{s}": 32 for s in range(4)}}
                with act.Fori(0, FB) as i, w.loop(i, 0, FB, per):
                    hi(6)
                    n = w.at("silu")
                    if conv:
                        act.wait_ge(conv_done, n + 1)
                        act.activation(f_a[:, :, :], f_a[:, :, :], ACT.Silu).then_inc(silu_done, 1)
                    else:
                        act.wait_ge(unit_done, BASE[name] + 8 * i + 4)
                        act.wait_ge(silu_used, n + 1)
                        act.activation(f_a[:, :, :], pair(0).rearrange("p (s t) -> p s t", s=4),
                                       ACT.Silu).then_inc(silu_done, 1)
                    hi(2)
                with act.Fori(0, FB - 1) as i, w.loop(i, 0, FB - 1, {"unit": 4, **{f"slot{s}": 16 for s in range(4)}}):
                    hi(4)
                norm(ahead, 0)

            hi(4)
            norm(4)
            norm(0, 0)
            hi(12)
            for qt in range(NT):
                mapping((x_s[:, :, :], x_s[:, :, :], ACT.Exp))
                for kt in range(NT):
                    save_turned(x_pt[:, kt, :], ps[:, PT_:PT_ + 512])
            norm(4, 0)
            ffn("ffn_in", True, 4)
            act.wait_ge(piece_ready, pieces("x3"))
            small(b_hot[:, :], tab("hot")[0:REL, :])
            small(b_rel[:, :], a["rel_bias_2"])
            act.wait_ge(operand, after("bias"))
            act.dma_start(bias_dram.ap().rearrange("h p n -> p h n"), b_vec[:, :, :]).then_inc(bias_out, 16)
            act.wait_ge(bias_out, 16)
            small(l_gb[:, :], a["gate_b_2"][0].partition_broadcast(P))
            small(l_tab[:, :], tab("causal"))
            hi(4)
            mapping((l_e[:, :, :], l_e[:, :, :], ACT.Exp))
            mapping((l_e[:, :, :], l_e[:, :, :], ACT.Ln))
            at_unit[0] = behind_lstm.first
            for g in range(2):
                if g:
                    act.wait_ge(operand, after("ml0"))
                small(l_norm[:, :], a["mh_g_2"][0, g * MIX:(g + 1) * MIX].partition_broadcast(P))
                if g == 0:
                    hi(16)
                q, k, _, o = l_in[g]
                fill(behind_lstm, LSTM_FILL[g][0])
                mapping((q[:, :, :], l_a[:, :, :], ACT.Silu))
                mapping((k[:, :, :], l_a[:, :, :], ACT.Silu))
                mapping((o[:, :, :], o[:, :, :], ACT.Sigmoid))
                for qt in range(NT):
                    n = P * (qt + 1)
                    fill(behind_lstm, LSTM_FILL[g][1 + 2 * qt])
                    mapping((l_s[:, :, 0:n], l_s[:, :, 0:n], ACT.Exp), (st[:, 8:10], st[:, 8:10], ACT.Exp))
                    for kt in range(qt + 1):
                        save_turned(l_pt[:, kt, :], ps[:, PT_:PT_ + 256])
                    fill(behind_lstm, LSTM_FILL[g][2 + 2 * qt])
                    mapping((st[:, 32:34], st[:, 32:34], ACT.Sqrt))
            for g in range(2):
                act.wait_ge(operand, after(f"ml1" if g == 0 else "di0"))
                if g == 0:
                    small(d_tab[:, :, :], tab("dil").rearrange("p (a n) -> p a n", a=2))
                skew = bass.AP(bias_dram, 4 * g * P * SKEW + P - 1, [[SKEW - 1, P], [P * SKEW, 4], [1, T]])
                small(d_bias[:, :, :], skew)
                if g == 0:
                    fill(behind_lstm, 4)
                for qt in range(NT):
                    n = P * (qt + 1)
                    if g == 0:
                        fill(behind_lstm, 4)
                    mapping((d_s[:, :, 0:n], d_s[:, :, 0:n], ACT.Exp))
                    for kt in range(qt + 1):
                        save_turned(d_pt[:, kt, :], ps[:, PT_:PT_ + 512])
            hi(4)
            norm(0)
            per = {"unit": 12, "shifted": 1, "turned": 1, **{f"slot{s}": 48 for s in range(4)}}
            with act.Fori(0, 4) as i, w.loop(i, 0, 4, per):
                hi(12)
                mapping((x_s[:, 0:2, :], x_s[:, 0:2, :], ACT.Exp))
                save_turned(x_pt[:, 0, :], ps[:, PT_:PT_ + 512])
            hi(4)
            norm(4)
            ffn("ffn2_in", False, 0)
            assert w.n["unit"] == UNITS

        @block.tensor
        def _(pe):
            w = Walk()

            def products(parts, units, hi, lo, bank, chunk=0, fresh=True, last=True, dyn=None, first_of=None,
                         begin=0):
                for u in range(begin, units):
                    if first_of:
                        pe.wait_ge(piece_ready, pieces(first_of, u + 1))
                    pe.wait_ge(lo_done, w.at("unit"))
                    slot = (w.n["unit"] - 1) % SLOTS
                    for k in range(CB):
                        begun = set()
                        for kind, c, width, h, at in parts:
                            first = fresh and u == 0 and k == 0 and at // 512 not in begun
                            begun.add(at // 512)
                            stop = last and u == units - 1 and k == CB - 1
                            kc = chunk + u * CB + k
                            for n, (wt, op) in enumerate(((whi, hi), (whi, lo), (wlo, hi))):
                                wk = wt[:, slot, k, c:c + (P if kind == "F" else width)]
                                if kind == "F":
                                    x = op[:, kc, :] if dyn is None else op[:, dyn + k, :]
                                    o = ps[:, bank + at:bank + at + T]
                                    ins = pe.matmul(o, wk, x, start=first and n == 0, stop=stop and n == 2,
                                                    skip_group_check=True)
                                else:
                                    x = op[:, kc, h * P:h * P + P]
                                    o = ps[:, bank + at:bank + at + width]
                                    ins = pe.matmul(o, x, wk, start=first and n == 0, stop=stop and n == 2,
                                                    skip_group_check=True)
                    ins.then_inc(unit_done, 1)

            def column(parts=F_BLOCK, units=4, hi=act_h, lo=act_l, first_of=None, dyn=None):
                b = w.at("block")
                if w.n["block"] > 2:
                    pe.wait_ge(block_saved, b - 2)
                products(parts, units, hi, lo, ((w.n["block"] - 1) % 2) * 1024, first_of=first_of, dyn=dyn)

            def fill(shadow, k):
                for unit in range(w.n["unit"], shadow.upto(w.n["unit"], k)):
                    n, u = divmod(unit - shadow.first, CB)
                    kind, place = shadow.blocks[n]
                    if u == 0:
                        b = w.at("block")
                        if b - 2 <= FIRST_GATE or shadow is not behind_sparse:
                            pe.wait_ge(block_saved, b - 2)
                        else:
                            pe.wait_ge(gate_done, b - 2 - FIRST_GATE)
                    products(F_BLOCK if kind == "F" else T_BLOCK, u + 1, act_h, act_l, ((w.n["block"] - 1) % 2) * 1024,
                             begin=u, last=u == CB - 1)

            def saved():
                pe.wait_ge(block_saved, w.now("block"))

            def mm(o, left, right, start, stop):
                return pe.matmul(o, left, right, start=start, stop=stop, skip_group_check=True)

            def turn(o, src, n=P):
                k = src.shape[0]
                return pe.matmul(o, src, ident[0:k, 0:k], start=True, stop=True, is_transpose=True, skip_group_check=True)

            def turn_tokens(count):
                pe.wait_ge(tokens_in, 16 * count)
                for c in range(DC):
                    for h in range(NT):
                        x = turn(ps[:, c * T + h * P:c * T + h * P + P], tok[:, h, c * P:c * P + P])
                x.then_inc(tokens_turned, 1)

            def norm():
                for x in (ln_t, ln_s2):
                    pe.wait_ge(left_ready, w.at("left"))
                    mm(ps[:, PC:PC + T], mean_w, x[:, :], True, True).then_inc(result_ready, 1)

            def turn_probs(s, heads, keys):
                for kt in range(-(-keys // P)):
                    kn = min(keys, P)
                    if w.n.get("turned", 0):
                        pe.wait_ge(turned_saved, w.now("turned"))
                    w.at("turned")
                    for j in range(heads):
                        x = turn(ps[0:kn, PT_ + j * P:PT_ + j * P + P], s[:, j, kt * P:kt * P + kn])
                    x.then_inc(turned, 1)
                pe.wait_ge(turned_saved, w.now("turned"))

            def turn_rows(src, blocks, bank=PC):
                pe.wait_ge(left_ready, w.at("left"))
                for j, (o, n, c) in enumerate(blocks):
                    x = turn(ps[:, bank + o:bank + o + P], src[:, n, c * P:c * P + P])
                x.then_inc(result_ready, 1)

            pe.wait_ge(params_in, 16 * (len(ROWS) + 1))
            for t in range(5):
                x = turn(ps[:, t * P:t * P + ROW_N[t]], prow[0:ROW_N[t], t, :])
            x.then_inc(params_turned, 1)
            pe.wait_ge(operand, after("turn_params"))
            turn_tokens(1)
            column(first_of="x")
            column(KV0_BLOCK)
            column(KV1_BLOCK)
            saved()
            pe.wait_ge(left_ready, w.at("left"))
            for g in range(2):
                r = slice(64 * g, 64 * g + 64)
                for l in range(32):
                    mm(ps[r, PC:PC + NCMP], n_w[r, 0, l, :], n_win[r, 0, l, :], l == 0, l == 31)
            for g in range(2):
                r = slice(64 * g, 64 * g + 64)
                for l in range(32):
                    x = mm(ps[0:NCMP, PC + 512 + 512 * g:PC + 576 + 512 * g], n_win[r, 1, l, :], n_w[r, 1, l, :],
                           l == 0, l == 31)
            x.then_inc(result_ready, 1)
            pe.wait_ge(left_ready, w.at("left"))
            for g in range(2):
                r = slice(64 * g, 64 * g + 64)
                for qt in range(NT):
                    for br in range(3):
                        n = NCMP if br == 0 else P * (qt + 1)
                        keys = n_kc[r, 0:NCMP] if br == 0 else n_kv[r, br + 1, 0:n]
                        for j in range(4):
                            x = mm(ps[:, PC + j * T:PC + j * T + n], n_q[r, j, qt * P:qt * P + P], keys, True, True)
                        x.then_inc(result_ready, 1)
                        fill(behind_sparse, 3)
                        pe.wait_ge(left_ready, w.at("left"))
                        turn_probs(n_s, 4, n)
                        for j in range(4):
                            o = ps[64 * (j % 2):64 * (j % 2) + 64, PO + (j // 2) * P:PO + (j // 2) * P + P]
                            for kt in range(-(-n // P)):
                                kn = min(n, P)
                                v = n_vc[0:NCMP, g, :] if br == 0 else n_v[:, br - 1, kt, 64 * g:64 * g + 64]
                                x = mm(o, v, n_pt[0:kn, kt, j * P:j * P + P], br == 0 and j < 2, br == 2 and kt == qt)
                    x.then_inc(result_ready, 1)
            for l in range(-1, 7):
                fill(behind_sparse, 4 if l < 0 else 3)
                pe.wait_ge(left_ready, w.at("left"))
                for h in range(4):
                    for n in range(NT):
                        c = h * T + n * P
                        kk = g_k[:, h, n * P:n * P + P] if l < 0 else g_kh[:, c:c + P]
                        qq = g_q[:, h, n * P:n * P + P] if l < 0 else g_qh[:, c:c + P]
                        x = mm(ps[:, PC + c:PC + c + P], kk, qq, True, True)
                x.then_inc(result_ready, 1)
            fill(behind_sparse, 3)
            pe.wait_ge(left_ready, w.at("left"))
            for h in range(4):
                x = mm(ps[:, PC + h * P:PC + h * P + P], g_kh[:, h * T:h * T + P], g_qh[:, h * T + P:h * T + T], True, True)
            x.then_inc(result_ready, 1)
            fill(behind_sparse, 2)
            pe.wait_ge(left_ready, w.at("left"))
            for n in range(NT):
                for h in range(4):
                    o = ps[:, PC + n * 512 + h * P:PC + n * 512 + h * P + P]
                    x = mm(o, g_a[:, h, n, :], g_v[:, n, h * P:h * P + P], h == 0, n == 0)
                    if n:
                        x = mm(o, g_p[:, h * P:h * P + P], g_v[:, 0, h * P:h * P + P], False, True)
            x.then_inc(result_ready, 1)
            fill(behind_sparse, 3)
            turn_rows(g_t[:, :].rearrange("p (n c) -> p n c", n=NT), [(c * T + n * P, n, c) for c in range(4) for n in range(NT)])
            fill(behind_sparse, 3)
            pe.wait_ge(left_ready, w.at("left"))
            for g in range(4):
                x = mm(ps[:, PC + g * T:PC + g * T + T], p_w[:, g, :], p_b[:, g, :], g % 2 == 0, True)
            x.then_inc(result_ready, 1)
            fill(behind_sparse, 4)
            pe.wait_ge(left_ready, w.at("left"))
            for g in range(4):
                x = turn(ps[:, PC + g * P:PC + g * P + P], s_w[:, g, :])
            x.then_inc(result_ready, 1)
            fill(behind_sparse, 1)
            pe.wait_ge(left_ready, w.at("left"))
            for n in range(NT):
                for g in range(4):
                    o = n * 512 + g * P
                    x = mm(ps[:, PC + o:PC + o + P], s_wt[:, g, :], s_v[:, n, g * P:g * P + P], g == 0, True)
            x.then_inc(result_ready, 1)
            fill(behind_sparse, 2)
            turn_rows(s_o, [(c * T + n * P, n, c) for c in range(4) for n in range(NT)])
            while w.n["unit"] < behind_sparse.end:
                fill(behind_sparse, 4)
            pe.wait_ge(piece_ready, pieces("branches"))
            with pe.Fori(0, 4) as i, w.loop(i, 0, 4, {"unit": 4, "block": 4}):
                for cb in range(NB):
                    column(units=1, hi=alt_h, lo=alt_l, dyn=i * CB)

            def square(hi, lo, first_of):
                with pe.Fori(0, 2) as i, w.loop(i, 0, 2, {"unit": 8, "block": 2}):
                    column(hi=hi, lo=lo, first_of=first_of)
                    column(hi=hi, lo=lo)

            def ffn(conv, first_of):
                per = {"unit": 8, "conv": 1, "silu": 1, "used": 1}
                with pe.Fori(0, FB) as i, w.loop(i, 0, FB, per):
                    if conv:
                        pe.wait_ge(conv_done, w.now("conv") + 1)
                    else:
                        pe.wait_ge(silu_done, w.now("silu"))
                    w.at("conv")
                    w.at("silu")
                    products(F_BLOCK, 4, act_h, act_l, 0, first_of=first_of)
                    pe.wait_ge(silu_used, w.at("used"))
                    products(F_BLOCK, 4, act_h, act_l, 1024)
                w.at("used")

                def piece(fresh, last, parity):
                    pe.wait_ge(hidden_ready, w.at("hidden"))
                    for cb in range(NB):
                        products(F_BLOCK, 1, f_h[:, parity], f_l[:, parity], cb * 1024, fresh=fresh, last=last)

                piece(True, False, 0)
                with pe.Fori(0, FB // 2 - 1) as i, w.loop(i, 0, FB // 2 - 1, {"unit": 8, "hidden": 2}):
                    piece(False, False, 1)
                    piece(False, False, 0)
                piece(False, False, 1)
                piece(False, True, 0)

            assert w.n["block"] % 2 == 0
            square(alt_h, alt_l, "mixed")
            norm()
            pe.wait_ge(piece_ready, pieces("x1"))
            turn_tokens(2)
            norm()
            column(hi=alt_h, lo=alt_l, first_of="memory")
            column(T_BLOCK, hi=alt_h, lo=alt_l)
            column()
            saved()
            for qt in range(NT):
                for j in range(4):
                    x = mm(ps[:, PC + j * T:PC + j * T + T], x_q[:, j, qt * P:qt * P + P], x_k[:, j, :], True, True)
                x.then_inc(result_ready, 1)
                pe.wait_ge(left_ready, w.at("left"))
                turn_probs(x_s, 4, T)
                for j in range(4):
                    for kt in range(NT):
                        x = mm(ps[:, PO + j * P:PO + j * P + P], x_v[:, kt, j * P:j * P + P],
                               x_pt[:, kt, j * P:j * P + P], j + kt == 0, kt == 1)
                x.then_inc(result_ready, 1)
            pe.wait_ge(operand, after("xa"))
            for cb in range(NB):
                column(units=1, hi=alt_h, lo=alt_l)
            norm()
            ffn(True, "x2")
            norm()
            pe.wait_ge(small_in, 16 * SMALL["bias"])
            for h in range(8):
                x = mm(ps[:, h * 512:h * 512 + SKEW], b_rel[:, h:h + 1].to_broadcast([REL, P]), b_hot[:, :], True, True)
            x.then_inc(result_ready, 1)
            pe.wait_ge(operand, after("bias"))
            column(GATE_BLOCK, first_of="x3")
            pe.wait_ge(left_ready, w.at("left"))
            mm(ps[:, PC:PC + 4], tri, l_lf[:, 0, :], True, True)
            mm(ps[:, PC + 4:PC + 8], tri, l_lf[:, 1, :], False, False)
            mm(ps[:, PC + 4:PC + 8], ones, l_lf[:, 0, :], False, True).then_inc(result_ready, 1)
            pe.wait_ge(operand, after("gates2"))
            column()
            column()
            column(T_BLOCK)
            column(T_BLOCK)
            for g in range(2):
                q, k, v, _ = l_in[g]
                fill(behind_lstm, LSTM_FILL[g][0])
                pe.wait_ge(left_ready, w.at("left"))
                for qt in range(NT):
                    n = P * (qt + 1)
                    for j in range(2):
                        for kt in range(qt + 1):
                            mm(ps[:, PC + j * T + kt * P:PC + j * T + kt * P + P],
                               l_i[:, kt, 2 * g + j:2 * g + j + 1].to_broadcast([P, P]), ident, True, True)
                    for j in range(2):
                        for c in range(2):
                            x = mm(ps[:, PC + 512 + j * T:PC + 512 + j * T + n], q[:, 2 * j + c, qt * P:qt * P + P],
                                   k[:, 2 * j + c, 0:n], c == 0 and j == 0, c == 1)
                    x.then_inc(result_ready, 1)
                    fill(behind_lstm, LSTM_FILL[g][1 + 2 * qt])
                    pe.wait_ge(left_ready, w.at("left"))
                    turn_probs(l_s, 2, n)
                    for j in range(2):
                        for kt in range(qt + 1):
                            x = mm(ps[:, PO + j * T:PO + j * T + T], l_pt[:, kt, j * P:j * P + P],
                                   v[:, kt, j * T:j * T + T], j + kt == 0, kt == qt)
                    x.then_inc(result_ready, 1)
                    fill(behind_lstm, LSTM_FILL[g][2 + 2 * qt])
                    turn_rows(l_h[:, :].unsqueeze(1), [(c * P, 0, c) for c in range(4)], PT_)
            for g in range(2):
                q, k, v = d_in[g]
                if g == 0:
                    fill(behind_lstm, 4)
                pe.wait_ge(left_ready, w.at("left"))
                for qt in range(NT):
                    n = P * (qt + 1)
                    for j in range(4):
                        x = mm(ps[:, PC + j * T:PC + j * T + n], q[:, j, qt * P:qt * P + P], k[:, j, 0:n], True, True)
                    x.then_inc(result_ready, 1)
                    if g == 0:
                        fill(behind_lstm, 4)
                    pe.wait_ge(left_ready, w.at("left"))
                    turn_probs(d_s, 4, n)
                    for j in range(4):
                        for kt in range(qt + 1):
                            x = mm(ps[:, PO + j * P:PO + j * P + P], v[:, kt, j * P:j * P + P],
                                   d_pt[:, kt, j * P:j * P + P], j + kt == 0, kt == qt)
                    x.then_inc(result_ready, 1)
            square(alt_h, alt_l, "mixed2")
            norm()
            pe.wait_ge(piece_ready, pieces("x4"))
            turn_tokens(3)
            per = {"unit": 24, "block": 6, "left": 2, "turned": 2}
            with pe.Fori(0, 2) as i, w.loop(i, 0, 2, per):
                for h in range(2):
                    column(hi=alt_h, lo=alt_l, first_of="mem2" if h == 0 else None)
                    column(T_BLOCK, hi=alt_h, lo=alt_l)
                    column()
                    saved()
                    for qt in range(NT):
                        for c in range(4):
                            x = mm(ps[:, PC + qt * T:PC + qt * T + T], x_q[:, c, qt * P:qt * P + P], x_k[:, c, :],
                                   c + qt == 0, c == 3)
                    x.then_inc(result_ready, 1)
                    pe.wait_ge(left_ready, w.at("left"))
                    pe.wait_ge(turned_saved, w.now("turned"))
                    w.at("turned")
                    for kt in range(NT):
                        for qt in range(NT):
                            x = turn(ps[:, PT_ + kt * T + qt * P:PT_ + kt * T + qt * P + P],
                                     x_s[:, qt, kt * P:kt * P + P])
                    x.then_inc(turned, 1)
                    pe.wait_ge(turned_saved, w.now("turned"))
                    for c in range(4):
                        for kt in range(NT):
                            x = mm(ps[:, PC + c * T:PC + c * T + T], x_v[:, kt, c * P:c * P + P],
                                   x_pt[:, 0, kt * T:kt * T + T], (c % 2) + kt == 0, kt == 1)
                    x.then_inc(result_ready, 1)
            square(alt_h, alt_l, "xb")
            norm()
            ffn(False, "x5")
            norm()
            pe.wait_ge(operand, after("y"))
            for c in range(DC):
                for h in range(NT):
                    x = turn(ps[:, h * D + c * P:h * D + c * P + P], res[:, c, h * P:h * P + P])
            x.then_inc(tokens_turned, 1)
            assert w.n["unit"] == UNITS

        @block.vector
        def _(dve):
            w = Walk()
            told = [0]

            def link(ins):
                ins.then_inc(dve_step, 1)
                dve.wait_ge(dve_step, w.at("step"))

            def tell(name, ins):
                told[0] += 1
                assert after(name) == told[0], name
                ins.then_inc(operand, 1)
                dve.wait_ge(operand, told[0])

            def to_act(ins):
                ins.then_inc(shifted, 1)
                dve.wait_ge(mapped, w.at("mapped"))

            def to_pe(ins):
                ins.then_inc(left_ready, 1)
                dve.wait_ge(left_ready, w.at("left"))

            def from_pe():
                dve.wait_ge(result_ready, w.at("result"))

            def copy(dst, src):
                return dve.tensor_copy(dst, src)

            def tt(dst, x, y, op):
                return dve.tensor_tensor(dst, x, y, op)

            def split(hi, lo, src, name=None, piece=False):
                link(copy(hi, src))
                x = tt(lo, src, hi.bitcast(F32), ALU.subtract)
                if piece:
                    x.then_inc(piece_ready, 1)
                    dve.wait_ge(piece_ready, w.at("piece"))
                elif name:
                    tell(name, x)
                else:
                    link(x)

            def split_pieces(name, hi, lo, src):
                for q in range(4):
                    split(hi[:, 4 * q:4 * q + 4, :], lo[:, 4 * q:4 * q + 4, :], src(q), piece=True)
                assert w.n["piece"] == pieces(name)

            def arrived(units):
                dve.wait_ge(unit_done, w.at("unit", units))
                b = w.at("block")
                return pair(w.n["block"] - 1)

            def kept(ins):
                ins.then_inc(block_saved, 1)
                dve.wait_ge(block_saved, w.now("block"))

            def four(x):
                return x.rearrange("p (s t) -> p s t", s=4)

            def two(x):
                return x.rearrange("p (n c) -> p n c", n=NT)

            at_unit = [behind_sparse.first]
            stored = [0]

            def catch_up(shadow):
                while stored[0] < shadow.complete(at_unit[0]) and shadow.blocks[stored[0]][1] is not None:
                    kind, dst = shadow.blocks[stored[0]]
                    x = arrived(4)
                    kept(copy(dst[:, :, :], four(x) if kind == "F" else two(x)))
                    stored[0] += 1

            def fill(shadow, k):
                catch_up(shadow)
                at_unit[0] = shadow.upto(at_unit[0], k)

            def turned_tokens(count, hi, lo, name):
                dve.wait_ge(tokens_turned, count)
                split_pieces(name, hi, lo, lambda q: four(ps[:, q * 1024:q * 1024 + 1024]))

            def softmax(s, heads, n, gate=None, floor=False, weight=None):
                m, r = st[:, 0:heads], st[:, 16:16 + heads]
                link(dve.tensor_reduce(m, s, AX, ALU.max))
                if floor:
                    link(dve.tensor_scalar(m, m, NEG, None, ALU.max))
                to_act(tt(s, s, wide(m, n), ALU.subtract))
                if weight is not None:
                    link(tt(s, s, weight, ALU.mult))
                link(dve.tensor_reduce(r, s, AX, ALU.add))
                if floor:
                    link(dve.tensor_scalar(r, r, 1e-30, None, ALU.max))
                link(dve.reciprocal(r, r))
                if gate is not None:
                    link(tt(r, r, gate, ALU.mult))
                to_pe(tt(s, s, wide(r, n), ALU.mult))

            def chunks_summed(dst, x):
                return dve.tensor_reduce(dst, x.rearrange("p c t -> p t c"), AX, ALU.add)

            def statistics(cb):
                r = res[:, 4 * cb:4 * cb + 4, :]
                if cb == 0:
                    link(chunks_summed(ln_a[:, :], r))
                    link(dve.tensor_scalar(ln_a[:, :], ln_a[:, :], 1.0 / CB, None, ALU.mult))
                tt(r, r, over(ln_a[:, :], 4), ALU.subtract).then_inc(centred, 1)
                dve.wait_ge(centred, w.at("centred"))
                if cb == 0:
                    link(chunks_summed(ln_s1[:, :], r))
                else:
                    link(chunks_summed(ln_t[:, :], r))
                    link(tt(ln_s1[:, :], ln_s1[:, :], ln_t[:, :], ALU.add))
                dve.wait_ge(squares_done, w.at("squares"))
                if cb == 0:
                    link(chunks_summed(ln_s2[:, :], ln_sq[:, :, :]))
                else:
                    link(chunks_summed(ln_t[:, :], ln_sq[:, :, :]))
                    link(tt(ln_s2[:, :], ln_s2[:, :], ln_t[:, :], ALU.add))

            def residual(x, cb, keep):
                sl = slice(4 * cb, 4 * cb + 4)
                link(dve.scalar_tensor_tensor(res[:, sl, :], act_h[:, sl, :].bitcast(F32), ALPHA, x, ALU.mult, ALU.add))
                keep(dve.scalar_tensor_tensor(res[:, sl, :], act_l[:, sl, :].bitcast(F32), ALPHA, res[:, sl, :],
                                              ALU.mult, ALU.add))
                statistics(cb)

            def norm(which, hi, lo, name):
                a, s1, s2, t, c, rstd = (x[:, :] for x in (ln_a, ln_s1, ln_s2, ln_t, ln_c, ln_rstd))
                to_pe(dve.scalar_tensor_tensor(t, a, float(DC), s1, ALU.mult, ALU.add))
                link(tt(rstd, s1, s1, ALU.mult))
                link(dve.scalar_tensor_tensor(s2, rstd, -1.0 / DC, s2, ALU.mult, ALU.add))
                from_pe()
                link(tt(c, ps[:, PC:PC + T], a, ALU.subtract))
                link(dve.scalar_tensor_tensor(rstd, s1, 1.0 / DC, c, ALU.mult, ALU.subtract))
                link(tt(rstd, rstd, rstd, ALU.mult))
                to_pe(dve.scalar_tensor_tensor(s2, rstd, float(DC), s2, ALU.mult, ALU.add))
                from_pe()
                to_act(dve.tensor_scalar(rstd, ps[:, PC:PC + T], EPS, None, ALU.add))
                link(dve.reciprocal(rstd, rstd))
                for q in range(4):
                    r = res[:, 4 * q:4 * q + 4, :]
                    link(tt(r, r, over(c, 4), ALU.subtract))
                    link(tt(r, r, over(rstd, 4), ALU.mult))
                    for c4 in range(4 * q, 4 * q + 4):
                        x = dve.tensor_scalar(res[:, c4, :], res[:, c4, :], col(f"ln_g{which}", c4), col(f"ln_b{which}", c4),
                                              ALU.mult, ALU.add)
                        if name == "y" and c4 == DC - 1:
                            tell(name, x)
                        elif c4 % 4 == 3:
                            link(x)
                        else:
                            x.then_inc(dve_step, 1)
                            w.at("step")
                    if name != "y":
                        split(hi[:, 4 * q:4 * q + 4, :], lo[:, 4 * q:4 * q + 4, :], r, piece=True)
                if name != "y":
                    assert w.n["piece"] == pieces(name)

            dve.wait_ge(params_turned, 1)
            for t in range(5):
                x = copy(pcol[:, t, 0:ROW_N[t]], ps[:, t * P:t * P + ROW_N[t]])
                tell("turn_params", x) if t == 4 else link(x)
            turned_tokens(1, act_h, act_l, "x")

            kept(dve.tensor_scalar(n_q[:, :, :], four(arrived(4)), 0.125, None, ALU.mult))
            x = arrived(4)
            link(copy(n_kv[:, 0:3, :], x[:, 0:768].rearrange("p (s t) -> p s t", s=3)))
            kept(copy(n_v[:, 0, :, :], two(x[:, 768:1024])))
            x = arrived(4)
            link(copy(n_kv[:, 3, :], x[:, 0:256]))
            link(copy(n_v[:, 1, :, :], two(x[:, 256:512])))
            kept(copy(n_gate[:, :, :], x[:, 512:640].rearrange("p (n c) -> p n c", n=2)[:, :, 0:24]))
            to_act(copy(n_gate[:, :, :], n_gate[:, :, :]))
            dve.wait_ge(small_in, 16 * SMALL["nsa"])
            for kv in range(2):
                for half in range(2):
                    src = n_kv[:, kv, 16 * half:16 * half + 240].rearrange("p (c l) -> p l c", l=16)
                    x = tt(n_win[:, kv, 16 * half:16 * half + 16, :], src,
                           n_pos[:, kv, 16 * half:16 * half + 16].unsqueeze(2).to_broadcast([P, 16, NCMP]), ALU.add)
                    to_pe(x) if kv + half == 2 else link(x)
            from_pe()
            link(copy(n_kc[:, 0:NCMP], ps[:, PC:PC + NCMP]))
            to_pe(copy(n_vc[0:NCMP, :, :], ps[0:NCMP, PC + 512:PC + 1536].rearrange("p (g e) -> p g e", g=2)[:, :, 0:64]))
            for g in range(2):
                for qt in range(NT):
                    for br in range(3):
                        n = NCMP if br == 0 else P * (qt + 1)
                        dist = n_tab[:, 2 * P + 16 * qt:2 * P + 16 * qt + n] if br == 0 else n_tab[:, 2 * P - n:2 * P]
                        fill(behind_sparse, 3)
                        from_pe()
                        for j in range(4):
                            slope = 2.0 ** -(4 * g + j + 1)
                            link(dve.scalar_tensor_tensor(n_s[:, j, 0:n], dist, -slope, ps[:, PC + j * T:PC + j * T + n],
                                                          ALU.mult, ALU.add))
                        o = 12 * g + br
                        softmax(n_s[:, :, 0:n], 4, n, gate=n_gate[:, qt, o:o + 10:3], floor=br == 0)
                    from_pe()
                    o = two(ps[:, PO:PO + 256])
                    x = copy(mixed_in[:, 2 * g:2 * g + 2, qt * P:qt * P + P], o)
                    tell("nsa", x) if g + qt == 2 else link(x)

            catch_up(behind_sparse)
            assert stored[0] == FIRST_GATE - 3
            lb, e = col("lb", 0, 4), st[:, 0:4]
            to_act(tt(e, lb, lb, ALU.subtract))
            link(dve.reciprocal(st[:, 4:8], e))
            link(tt(e, e, st[:, 4:8], ALU.mult))
            link(tt(st[:, 8:12], e, e, ALU.subtract))
            link(dve.tensor_scalar(st[:, 12:16], st[:, 8:12], -1.0, 1.0, ALU.mult, ALU.add))
            to_act(copy(g_k[:, :, :], g_k[:, :, :]))
            for h in range(4):
                link(dve.tensor_scalar(g_k[:, h, :], g_k[:, h, :], st[:, 12 + h:13 + h], st[:, 8 + h:9 + h],
                                       ALU.mult, ALU.add))
            to_act(dve.tensor_scalar(g_k[:, :, :], g_k[:, :, :], 1e-6, None, ALU.max))
            link(dve.tensor_scalar(g_k[:, :, :], g_k[:, :, :], -1.0, 1.0, ALU.mult, ALU.add))
            link(copy(g_qh[:, :], g_q[:, :, :].rearrange("p h t -> p (h t)")))
            to_pe(copy(g_kh[:, :], g_k[:, :, :].rearrange("p h t -> p (h t)")))
            q = g_q[:, :, :].rearrange("p h t -> p (h t)")
            k = g_k[:, :, :].rearrange("p h t -> p (h t)")
            acc = g_a[:, :, :, :].rearrange("p h n t -> p (h n) t")
            blocks8 = ps[:, PC:PC + 1024].rearrange("p (b t) -> p b t", b=8)
            dve.wait_ge(small_in, 16 * SMALL["hgrn"])
            from_pe()
            link(tt(acc, blocks8, over(ident, 8), ALU.mult))
            for l in range(8):
                h = 1 << l

                def halves(x):
                    return x.rearrange("p (m two h) -> p m two h", two=2, h=h)

                pv, ev = halves(g_p[:, :]), halves(g_t[:, :])
                last = pv[:, :, 0, h - 1:h].to_broadcast([P, 512 // h, h])
                to_act(tt(ev[:, :, 0, :], last, pv[:, :, 0, :], ALU.subtract))
                link(tt(halves(g_qh[:, :])[:, :, 1, :], halves(q)[:, :, 1, :], ev[:, :, 1, :], ALU.mult))
                to_pe(tt(halves(g_kh[:, :])[:, :, 0, :], halves(k)[:, :, 0, :], ev[:, :, 0, :], ALU.mult))
                if l < 7:
                    link(tt(pv[:, :, 1, :], pv[:, :, 1, :], last, ALU.add))
                    from_pe()
                    t8 = g_t[:, :].rearrange("p (b t) -> p b t", b=8)
                    link(tt(t8, blocks8, over(g_mask[:, l, :], 8), ALU.mult))
                    link(tt(acc, acc, t8, ALU.add))
                else:
                    from_pe()
                    to_pe(copy(g_p[:, 0:512], ps[:, PC:PC + 512]))
            from_pe()
            x8 = g_t[:, :].rearrange("p (b t) -> p b t", b=8)
            to_act(copy(st[:, 16:17], st[:, 12:13]))
            link(dve.tensor_reduce(st[:, 0:8], x8, AX, ALU.add))
            to_act(dve.tensor_scalar(st[:, 0:8], st[:, 0:8], 1.0 / P, EPS, ALU.mult, ALU.add))
            link(dve.reciprocal(st[:, 0:8], st[:, 0:8]))
            link(tt(x8, blocks8, wide(st[:, 0:8], P), ALU.mult))
            o2 = two(g_t[:, :])
            to_act(tt(o2, o2, over(g_norm[:, :], NT), ALU.mult))
            to_pe(tt(o2, o2, g_g[:, :, :], ALU.mult))
            from_pe()
            split(alt_h[:, 0:4, :], alt_l[:, 0:4, :], mixed_in[:, 0:4, :], piece=True)
            split(alt_h[:, 4:8, :], alt_l[:, 4:8, :], four(ps[:, PC:PC + 1024]), piece=True)

            src = p_c
            for g in range(4):
                h = 1 << g
                dst = (p_a, p_b)[g % 2]
                link(tt(dst[:, g:4, h:T], src[:, g:4, h:T], src[:, g:4, 0:T - h], ALU.add))
                link(copy(dst[:, g:4, 0:h], src[:, g:4, 0:h]))
                src = dst
            link(copy(p_b[:, 0, :], p_a[:, 0, :]))
            link(copy(p_b[:, 2, :], p_a[:, 2, :]))
            dve.wait_ge(small_in, 16 * SMALL["pool"])
            link(tt(p_b[:, :, :], p_b[:, :, :], p_inv[:, :, :], ALU.mult))
            to_pe(tt(p_b[:, :, :], p_b[:, :, :], p_c[:, :, :], ALU.subtract))
            from_pe()
            for g in range(4):
                link(dve.tensor_scalar(p_a[:, g, :], ps[:, PC + g * T:PC + g * T + T], col("pool_scale", g), None, ALU.mult))
            split(alt_h[:, 8:12, :], alt_l[:, 8:12, :], p_a[:, :, :], piece=True)

            dve.wait_ge(small_in, 16 * SMALL["sgu"])
            to_act(copy(st[:, 16:17], s_v[:, 0, 0:1]))
            to_act(copy(st[:, 16:17], s_v[:, 0, 0:1]))
            for n in range(NT):
                link(dve.bn_stats(st[:, 64 + 6 * n:70 + 6 * n], s_v[:, n, :]))
                link(dve.bn_aggr(st[:, 40 + 2 * n:42 + 2 * n], st[:, 64 + 6 * n:70 + 6 * n]))
            to_act(dve.tensor_scalar(st[:, 32:34], st[:, 41:44:2], EPS, None, ALU.add))
            link(dve.reciprocal(st[:, 32:34], st[:, 32:34]))
            for n in range(NT):
                link(dve.tensor_scalar(s_v[:, n, :], s_v[:, n, :], st[:, 40 + 2 * n:41 + 2 * n], st[:, 32 + n:33 + n],
                                       ALU.subtract, ALU.mult))
            link(tt(s_v[:, :, :], s_v[:, :, :], over(s_g[:, :], NT), ALU.mult))
            to_pe(tt(s_v[:, :, :], s_v[:, :, :], over(s_b[:, :], NT), ALU.add))
            from_pe()
            to_pe(tt(s_wt[:, :, :], four(ps[:, PC:PC + 512]), over(tri, 4), ALU.mult))
            from_pe()
            vs = two(ps[:, PC:PC + 1024])
            for g in range(4):
                c = slice(g * P, g * P + P)
                x = dve.scalar_tensor_tensor(s_o[:, :, c], vs[:, :, c], col("sg_b", g), s_u[:, :, c], ALU.add, ALU.mult)
                to_pe(x) if g == 3 else link(x)
            from_pe()
            split(alt_h[:, 12:16, :], alt_l[:, 12:16, :], four(ps[:, PC:PC + 1024]), piece=True)

            dve.wait_ge(gate_spilled, 16 * 4 * NB)
            dve.sem_inc(block_saved, 4 * NB)
            w.at("block", 4 * NB)
            w.at("unit", BASE["merge"] - BASE["gates"])
            dve.sem_inc(merge_added, 2)
            w.at("added", 2)
            link(dve.memset(res[:, :, :], 0.0))
            with dve.Fori(0, 4) as i, w.loop(i, 0, 4, {"unit": 4, "block": 4, "added": 4, "gates0": 32, "gates1": 32}):
                for cb in range(NB):
                    x = four(arrived(1))
                    dve.wait_ge(gate_loaded[cb % 2], w.at(f"gates{cb % 2}", 16))
                    kept(tt(m_t[:, :, :], x, four(m_g[:, cb % 2, :]), ALU.mult))
                    sl = slice(4 * cb, 4 * cb + 4)
                    tt(res[:, sl, :], res[:, sl, :], m_t[:, :, :], ALU.add).then_inc(merge_added, 1)
                    dve.wait_ge(merge_added, w.at("added"))
            split_pieces("mixed", alt_h, alt_l, lambda q: res[:, 4 * q:4 * q + 4, :])

            def residuals(units):
                for cb in range(NB):
                    residual(four(arrived(units)), cb, kept)

            def ffn(conv):
                for s in (conv_done, silu_used) if conv else (silu_used,):
                    dve.sem_inc(s, 1)
                w.at("conv")
                w.at("used")
                per = {"unit": 8, "silu": 1, "used": 1}
                if conv:
                    per |= {"conv": 1, "step": 7}
                with dve.Fori(0, FB) as i, w.loop(i, 0, FB, per):
                    w.at("unit", 8)
                    u = w.now("unit")
                    if conv:
                        dve.wait_ge(unit_done, u - 4)
                        gate = four(ps[:, 0:1024])

                        def tap(name):
                            t, r = ROW_AT[name]
                            return pcol[:, t, bass.ds(i * 4 + r, 4)]

                        link(tt(f_a[:, :, :], gate, wide(tap("cw2"), T), ALU.mult))
                        for j, s in ((1, 1), (0, 2)):
                            link(tt(f_b[:, :, 0:T - s], gate[:, :, 0:T - s], wide(tap(f"cw{j}"), T - s), ALU.mult))
                            link(tt(f_a[:, :, s:T], f_a[:, :, s:T], f_b[:, :, 0:T - s], ALU.add))
                        link(copy(st[:, 16:17], ident[:, 0:1]))
                        link(copy(st[:, 16:17], ident[:, 0:1]))
                        tt(f_a[:, :, :], f_a[:, :, :], wide(tap("cb"), T), ALU.add).then_inc(conv_done, 1)
                        dve.wait_ge(conv_done, w.at("conv"))
                    dve.wait_ge(unit_done, u)
                    dve.wait_ge(silu_done, w.at("silu"))
                    dve.tensor_tensor(hid[:, bass.ds(i * 4, 4), :], f_a[:, :, :], four(ps[:, 1024:2048]),
                                      ALU.mult).then_inc(silu_used, 1)
                    dve.wait_ge(silu_used, w.at("used"))

                def piece(k, parity, first):
                    w.at("unit", 4)
                    if not first:
                        dve.wait_ge(unit_done, w.now("unit") - 8)
                    src = hid[:, k, :] if isinstance(k, slice) else hid[:, bass.ds(k, 4), :]
                    dve.tensor_copy(f_h[:, parity], src).then_inc(dve_step, 1)
                    dve.wait_ge(dve_step, w.at("step"))
                    dve.tensor_tensor(f_l[:, parity], src, f_h[:, parity].bitcast(F32), ALU.subtract).then_inc(hidden_ready, 1)
                    w.at("hidden")

                piece(slice(0, 4), 0, True)
                piece(slice(4, 8), 1, True)
                with dve.Fori(0, 4) as i, w.loop(i, 0, 4, {"unit": 8, "hidden": 2, "step": 2}):
                    piece(i * 8 + 8, 0, False)
                    piece(i * 8 + 12, 1, False)
                piece(slice(40, 44), 0, False)
                dve.wait_ge(hidden_ready, w.now("hidden"))
                for cb in range(NB):
                    dve.wait_ge(unit_done, w.now("unit") - 3 + cb)
                    residual(four(ps[:, cb * 1024:cb * 1024 + 1024]), cb, link)

            residuals(4)
            norm(0, act_h, act_l, "x1")
            dve.wait_ge(tokens_turned, 2)
            for q in range(4):
                x = copy(res[:, 4 * q:4 * q + 4, :], four(ps[:, q * 1024:q * 1024 + 1024]))
                tell("mem_tokens", x) if q == 3 else link(x)
            for q in range(4):
                statistics(q)
            norm(1, alt_h, alt_l, "memory")
            kept(dve.tensor_scalar(x_k[:, :, :], four(arrived(4)), 128 ** -0.5, None, ALU.mult))
            kept(copy(x_v[:, :, :], two(arrived(4))))
            kept(copy(x_q[:, :, :], four(arrived(4))))
            for qt in range(NT):
                from_pe()
                link(copy(x_s[:, :, :], four(ps[:, PC:PC + 1024])))
                softmax(x_s[:, :, :], 4, T)
                from_pe()
                at = (slice(None), slice(0, 4), slice(qt * P, qt * P + P))
                split(alt_h[at], alt_l[at], four(ps[:, PO:PO + 512]), "xa" if qt else None)
            residuals(1)
            norm(2, act_h, act_l, "x2")
            ffn(True)
            norm(3, act_h, act_l, "x3")

            from_pe()
            for h in range(8):
                x = copy(b_vec[:, h, :], ps[:, h * 512:h * 512 + SKEW])
                tell("bias", x) if h == 7 else link(x)
            x = arrived(4)
            dve.wait_ge(small_in, 16 * SMALL["gates2"])
            kept(tt(l_gate[:, :, :], x[:, 0:128].rearrange("p (n c) -> p n c", n=2)[:, :, 0:8], over(l_gb[:, :], NT), ALU.add))
            f = l_gate[:, :, 4:8]
            link(dve.tensor_scalar(l_e[:, :, :], f, -1.0, None, ALU.mult))
            to_act(tt(l_e[:, :, :], l_e[:, :, :], f, ALU.min))
            to_act(dve.tensor_scalar(l_e[:, :, :], l_e[:, :, :], 1.0, None, ALU.add))
            link(dve.tensor_scalar(l_lf[:, :, :], f, 0.0, None, ALU.min))
            to_pe(tt(l_lf[:, :, :], l_lf[:, :, :], l_e[:, :, :], ALU.subtract))
            from_pe()
            link(copy(l_cum[:, :, :], ps[:, PC:PC + 8].rearrange("p (n h) -> p n h", n=2)))
            tell("gates2", tt(l_i[:, :, :], l_gate[:, :, 0:4], l_cum[:, :, :], ALU.subtract))
            for dst in l_in[0]:
                kept(copy(dst[:, :, :], (four if dst.shape[1] == 4 else two)(arrived(4))))
            at_unit[0], stored[0] = behind_lstm.first, 0
            for g in range(2):
                q, k, _, o = l_in[g]
                dve.wait_ge(small_in, 16 * SMALL[f"ml{g}"])
                fill(behind_lstm, LSTM_FILL[g][0])
                for part, x in enumerate((q, k)):
                    r = part * 8 + 4 * g

                    def tap(j):
                        return col(f"c2w{j}", r, 4)

                    link(tt(l_a[:, :, :], x[:, :, :], wide(tap(3), T), ALU.mult))
                    for j, s in ((2, 1), (1, 2), (0, 3)):
                        link(tt(l_b[:, :, 0:T - s], x[:, :, 0:T - s], wide(tap(j), T - s), ALU.mult))
                        link(tt(l_a[:, :, s:T], l_a[:, :, s:T], l_b[:, :, 0:T - s], ALU.add))
                    to_act(tt(l_a[:, :, :], l_a[:, :, :], wide(col("cb2", r, 4), T), ALU.add))
                to_act(copy(st[:, 16:17], ident[:, 0:1]))
                to_pe(dve.tensor_scalar(k[:, :, :], k[:, :, :], 1.0 / 16, None, ALU.mult))
                for qt in range(NT):
                    n = P * (qt + 1)
                    fill(behind_lstm, LSTM_FILL[g][1 + 2 * qt])
                    from_pe()
                    for j in range(2):
                        link(dve.scalar_tensor_tensor(l_s[:, j, 0:n], ps[:, PC + j * T:PC + j * T + n],
                                                      l_cum[:, qt, 2 * g + j:2 * g + j + 1], l_tab[:, 2 * P - n:2 * P],
                                                      ALU.add, ALU.add))
                    m = st[:, 0:2]
                    link(dve.tensor_reduce(m, l_s[:, :, 0:n], AX, ALU.max))
                    link(tt(m, m, l_cum[:, qt, 2 * g:2 * g + 2], ALU.max))
                    link(dve.tensor_scalar(st[:, 8:10], m, -1.0, None, ALU.mult))
                    to_act(tt(l_s[:, :, 0:n], l_s[:, :, 0:n], wide(m, n), ALU.subtract))
                    qk = ps[:, PC + 512:PC + 1024].rearrange("p (j t) -> p j t", j=2)[:, :, 0:n]
                    link(tt(l_s[:, :, 0:n], l_s[:, :, 0:n], qk, ALU.mult))
                    link(dve.tensor_reduce(st[:, 4:6], l_s[:, :, 0:n], AX, ALU.add))
                    link(dve.tensor_scalar(st[:, 6:8], st[:, 4:6], -1.0, None, ALU.mult))
                    link(tt(st[:, 4:6], st[:, 4:6], st[:, 6:8], ALU.max))
                    link(tt(st[:, 4:6], st[:, 4:6], st[:, 8:10], ALU.max))
                    link(dve.reciprocal(st[:, 4:6], st[:, 4:6]))
                    to_pe(tt(l_s[:, :, 0:n], l_s[:, :, 0:n], wide(st[:, 4:6], n), ALU.mult))
                    fill(behind_lstm, LSTM_FILL[g][2 + 2 * qt])
                    from_pe()
                    link(copy(l_h[:, :], ps[:, PO:PO + 512]))
                    for j in range(2):
                        link(dve.bn_stats(st[:, 64 + 6 * j:70 + 6 * j], l_h[:, j * T:j * T + T]))
                        link(dve.bn_aggr(st[:, 40 + 2 * j:42 + 2 * j], st[:, 64 + 6 * j:70 + 6 * j]))
                    to_act(dve.tensor_scalar(st[:, 32:34], st[:, 41:44:2], EPS, None, ALU.add))
                    link(dve.reciprocal(st[:, 32:34], st[:, 32:34]))
                    for j in range(2):
                        link(dve.tensor_scalar(l_h[:, j * T:j * T + T], l_h[:, j * T:j * T + T], st[:, 40 + 2 * j:41 + 2 * j],
                                               st[:, 32 + j:33 + j], ALU.subtract, ALU.mult))
                    link(tt(l_h[:, :], l_h[:, :], l_norm[:, :], ALU.mult))
                    to_pe(tt(l_h[:, :], l_h[:, :], o[:, qt, :], ALU.mult))
                    from_pe()
                    x = copy(mixed_in[:, 4 * g:4 * g + 4, qt * P:qt * P + P], four(ps[:, PT_:PT_ + 512]))
                    tell(f"ml{g}", x) if qt else link(x)
                catch_up(behind_lstm)
            for g in range(2):
                q, k, v = d_in[g]
                if g == 0:
                    fill(behind_lstm, 4)
                else:
                    catch_up(behind_lstm)
                to_pe(dve.tensor_scalar(q[:, :, :], q[:, :, :], 128 ** -0.5, None, ALU.mult))
                dve.wait_ge(small_in, 16 * SMALL[f"di{g}"])
                link(tt(d_bias[:, :, :], d_bias[:, :, :], over(d_tab[:, 1, :], 4), ALU.add))
                for qt in range(NT):
                    n = P * (qt + 1)
                    if g == 0:
                        fill(behind_lstm, 4)
                    from_pe()
                    link(tt(d_s[:, :, 0:n], four(ps[:, PC:PC + 1024])[:, :, 0:n], d_bias[:, :, T - n:T], ALU.add))
                    softmax(d_s[:, :, 0:n], 4, n, weight=over(d_tab[:, 0, T - n:T], 4))
                    from_pe()
                    x = copy(mixed_in[:, 8 + 4 * g:12 + 4 * g, qt * P:qt * P + P], four(ps[:, PO:PO + 512]))
                    tell("di0", x) if qt and not g else link(x)
            split_pieces("mixed2", alt_h, alt_l, lambda q: mixed_in[:, 4 * q:4 * q + 4, :])
            residuals(4)
            norm(4, act_h, act_l, "x4")
            turned_tokens(3, alt_h, alt_l, "mem2")
            per = {"unit": 24, "block": 6, "step": 12, "result": 4, "mapped": 2, "left": 2}
            with dve.Fori(0, 2) as i, w.loop(i, 0, 2, per):
                for h in range(2):
                    kept(dve.tensor_scalar(x_k[:, :, :], four(arrived(4)), 512 ** -0.5, None, ALU.mult))
                    kept(copy(x_v[:, :, :], two(arrived(4))))
                    kept(copy(x_q[:, :, :], four(arrived(4))))
                    from_pe()
                    link(copy(x_s[:, 0:2, :], two(ps[:, PC:PC + 512])))
                    softmax(x_s[:, 0:2, :], 2, T)
                    from_pe()
                    link(copy(res[:, bass.ds(i * 8 + h * 4, 4), :], four(ps[:, PC:PC + 1024])))
                    link(copy(st[:, 16:17], ident[:, 0:1]))
            split_pieces("xb", alt_h, alt_l, lambda q: res[:, 4 * q:4 * q + 4, :])
            residuals(4)
            norm(5, act_h, act_l, "x5")
            ffn(False)
            norm(6, None, None, "y")
            dve.wait_ge(tokens_turned, 4)
            for q in range(4):
                h, c = q // 2, (q % 2) * 1024
                x = copy(outt[:, h, c:c + 1024], ps[:, q * 1024:q * 1024 + 1024])
                tell("end", x) if q == 3 else link(x)
            assert w.n["unit"] == UNITS


def kernel(**inputs):
    import concourse.bacc as bacc
    from concourse.bass_utils import run_bass_kernel_spmd

    nc = bacc.Bacc("TRN2", target_bir_lowering=False, num_devices=1)
    arrays, aps = {}, {}
    for name, value in inputs.items():
        v = np.ascontiguousarray(value)
        arrays[f"in_{name}"] = v
        aps[name] = nc.dram_tensor(f"in_{name}", v.shape, mybir.dt.from_np(v.dtype), kind="ExternalInput").ap()
    _, table = shape_tables()
    arrays["shape_tables"] = table
    tables = nc.dram_tensor("shape_tables", table.shape, F32, kind="ExternalInput").ap()
    out = nc.dram_tensor("out_x", (1, T, D), F32, kind="ExternalOutput").ap()
    two_blocks(nc, aps, tables, out)
    r = run_bass_kernel_spmd(nc, [arrays], core_ids=[0])
    return r.results[0]["out_x"]
```

```python
from contextlib import ExitStack, contextmanager

import numpy as np
import concourse.bass as bass
from concourse import mybir

F32 = mybir.dt.float32
F32R = mybir.dt.float32r
ALU = mybir.AluOpType
ACT = mybir.ActivationFunctionType
AX = mybir.AxisListType.X

P = 128
T = 256
NT = T // P
D = 2048
DC = D // P
CB = 4
UNIT = CB * P
SLOTS = 4
NB = D // UNIT
FF = 5632
FC = FF // P
FB = FF // UNIT
ALPHA = 2.0 ** 0.25
EPS = 1e-5
NEG = -1e30
FAR = 1e35
MIX = 512
C_Q, C_KV, C_HG, C_POOL, C_SG, C_MERGE = 0, 512, 1304, 3352, 3864, 4888
C2_GATE, C2_DQ = 4096, 4104
NCMP = 15
REL = 32
SKEW = 384

STAGES = [("nsa_q", 4), ("nsa_kv", 8), ("xmem", 8), ("hgrn", 16), ("pool", 4), ("sgu", 8), ("gates", 64), ("merge", 16),
          ("mix_out", 16), ("xq", 4), ("xo", 4), ("ffn_in", 8 * FB), ("ffn_out", 4 * FB),
          ("gates2", 4), ("mlstm", 16), ("mlstm1", 16), ("dilated", 24), ("out2", 16), ("x2", 48), ("xo2", 16),
          ("ffn2_in", 8 * FB), ("ffn2_out", 4 * FB)]
BASE, _n = {}, 0
for _name, _u in STAGES:
    BASE[_name] = _n
    _n += _u
UNITS = _n

FIRST_GATE = 12
LSTM_FILL = [(4, 3, 3, 3, 3), (4, 2, 2, 2, 2)]

F_BLOCK = [("F", s * P, P, 0, s * T) for s in range(CB)]
T_BLOCK = [("T", 0, UNIT, h, h * UNIT) for h in range(NT)]
KV0_BLOCK = [("F", 0, P, 0, 0), ("F", 128, P, 0, 256), ("F", 256, P, 0, 512),
             ("T", 384, P, 0, 768), ("T", 384, P, 1, 896)]
KV1_BLOCK = [("F", 0, P, 0, 0), ("T", 128, P, 0, 256), ("T", 128, P, 1, 384),
             ("T", 256, 24, 0, 512), ("T", 256, 24, 1, 576)]
GATE_BLOCK = [("T", 0, 8, 0, 0), ("T", 0, 8, 1, 64)]

ROWS = [(0, f"ln_g{i}", DC) for i in range(7)] + [(1, f"ln_b{i}", DC) for i in range(7)] + [
    (1, "lb", 4), (1, "pool_scale", 4), (1, "sg_b", 4),
    (2, "cw0", FC), (2, "cw1", FC), (2, "cb2", DC),
    (3, "cw2", FC), (3, "cb", FC),
    (4, "c2w0", DC), (4, "c2w1", DC), (4, "c2w2", DC), (4, "c2w3", DC)]
ROW_AT, ROW_N = {}, [0] * 5
for _t, _name, _r in ROWS:
    ROW_AT[_name] = (_t, ROW_N[_t])
    ROW_N[_t] += _r


def shape_tables():
    p = np.arange(P)[:, None]
    u = np.arange(2 * P)[None, :]
    dist = P + p - u
    ident = np.eye(P)
    mean = np.full((P, P), 1.0 / D)
    tri = (p <= np.arange(P)[None, :]) * 1.0
    ones = np.ones((P, P))
    core = np.concatenate([ident, mean, tri, ones], 1)
    alibi = np.where(dist >= 0, dist, FAR)
    end = 16 * np.arange(16) + 31
    cmp_d = [np.where(t0 + p - end >= 0, t0 + p - end, FAR) for t0 in (0, P)]
    nsa = np.concatenate([alibi] + cmp_d, 1)
    level = []
    s, t = np.arange(P)[:, None], np.arange(P)[None, :]
    for l in range(7):
        h = 1 << l
        level.append((s // (2 * h) == t // (2 * h)) & (s % (2 * h) < h) & (t % (2 * h) >= h))
    level = np.concatenate(level, 1) * 1.0
    cnt = np.concatenate([1.0 / np.minimum(np.arange(T) + 1, w) for w in (2, 4, 8, 16)])
    cnt = np.broadcast_to(cnt, (P, 4 * T))
    mult = ((dist >= 0) & (dist <= 128)) * 1.0 + ((dist >= 0) & (dist % 4 == 0)) + ((dist >= 0) & (dist % 16 == 0))
    dil = np.concatenate([mult, np.where(mult > 0, 0.0, NEG)], 1)
    causal = np.where(dist >= 0, 0.0, NEG)
    d = np.maximum(255 - np.arange(SKEW), 0)
    big = np.maximum(d, 1).astype(np.float32)
    lg = 16 + (np.log(big / 16) / np.float32(np.log(2048 / 16)) * 16).astype(np.int32)
    bucket = np.where(d < 16, d, np.minimum(lg, REL - 1))
    hot = np.zeros((P, SKEW))
    hot[:REL] = (np.arange(REL)[:, None] == bucket[None, :])
    parts = {"core": core, "nsa": nsa, "level": level, "cnt": cnt, "dil": dil, "causal": causal, "hot": hot}
    at, n = {}, 0
    for k, v in parts.items():
        at[k] = (n, n + v.shape[1])
        n += v.shape[1]
    return at, np.concatenate(list(parts.values()), 1).astype(np.float32)


class Walk:

    def __init__(self):
        self.n, self.off = {}, {}

    def at(self, key, k=1):
        self.n[key] = self.n.get(key, 0) + k
        return self.n[key] + self.off.get(key, 0)

    def now(self, key):
        return self.n.get(key, 0) + self.off.get(key, 0)

    @contextmanager
    def loop(self, i, first, times, per):
        begin = dict(self.n)
        self.off = {k: (i - first) * v for k, v in per.items()}
        yield
        for k in set(self.n) | set(per):
            assert self.n.get(k, 0) - begin.get(k, 0) == per.get(k, 0), (k, self.n.get(k, 0) - begin.get(k, 0))
            self.n[k] = begin.get(k, 0) + per.get(k, 0) * times
        self.off = {}


class Shadow:

    def __init__(self, first, end, blocks):
        self.first, self.end, self.blocks = BASE[first], BASE[end], blocks
        assert self.end - self.first == CB * len(blocks)

    def upto(self, unit, k):
        assert k <= SLOTS
        return min(unit + k, self.end)

    def complete(self, unit):
        return (unit - self.first) // CB


def two_blocks(nc, a, tables, out):
    tab_at, _ = shape_tables()
    ctx = ExitStack()
    with ctx:
        def place(name, at, shape, dt=F32):
            n = int(np.prod(shape[1:])) * 4
            assert at + n <= 229344, (name, at + n)
            return nc.alloc_sbuf_tensor_at(name, shape, dt, offset=at)

        def sem(name):
            return ctx.enter_context(nc.semaphore(name))

        KB = 1024
        W0 = 16512
        wraw = place("wraw", W0, [P, SLOTS, CB, UNIT])
        whi = place("whi", W0 + 32 * KB, [P, SLOTS, CB, UNIT], F32R)
        wlo = place("wlo", W0 + 64 * KB, [P, SLOTS, CB, UNIT], F32R)
        A0 = W0 + 96 * KB
        act_h = place("act_h", A0, [P, DC, T], F32R)
        act_l = place("act_l", A0 + 16 * KB, [P, DC, T], F32R)
        kept_x = place("kept_x", A0 + 16 * KB, [P, DC, T])
        X0 = A0 + 32 * KB
        alt_h = place("alt_h", X0, [P, DC, T], F32R)
        alt_l = place("alt_l", X0 + 16 * KB, [P, DC, T], F32R)
        hid = place("hid", X0, [P, FC, T])
        Z0 = X0 + 32 * KB
        res = place("res", Z0, [P, DC, T])
        tok = place("tok", Z0, [P, NT, D])
        Y0 = Z0 + 16 * KB
        core = place("core", Y0, [P, 4 * P])
        pcol = place("pcol", Y0 + 2 * KB, [P, 5, P])
        Y1 = Y0 + 2 * KB + 5 * P * 4
        ident, mean_w, tri, ones = (core[:, P * j:P * j + P] for j in range(4))
        prow = place("prow", Y1, [P, 5, P])
        outt = place("outt", X0, [P, NT, D])

        mtok2 = place("mtok2", Y1, [P, NT, D])
        mtok = place("mtok", X0 + 16 * KB, [P, NT, D])
        ln_a = place("ln_a", Y1 + 16 * KB, [P, T])
        ln_s1 = place("ln_s1", Y1 + 17 * KB, [P, T])
        ln_s2 = place("ln_s2", Y1 + 18 * KB, [P, T])
        ln_t = place("ln_t", Y1 + 19 * KB, [P, T])
        ln_c = place("ln_c", Y1 + 20 * KB, [P, T])
        ln_rstd = place("ln_rstd", Y1 + 21 * KB, [P, T])
        ln_sq = place("ln_sq", Y1 + 22 * KB, [P, CB, T])
        n_q = place("n_q", Y1, [P, 4, T])
        n_kv = place("n_kv", Y1 + 4 * KB, [P, 4, T])
        n_v = place("n_v", Y1 + 8 * KB, [P, 2, NT, P])
        n_s = place("n_s", Y1 + 10 * KB, [P, 4, T])
        n_pt = place("n_pt", Y1 + 14 * KB, [P, NT, 4 * P])
        n_win = place("n_win", Y1 + 18 * KB, [P, 2, 32, NCMP])
        n_tab = place("n_tab", Y1 + 22 * KB, [P, 2 * P + 32])
        n_gate = place("n_gate", Y1 + 24 * KB, [P, NT, 24])
        n_kc = place("n_kc", Y1 + 24 * KB + 256, [P, 16])
        n_vc = place("n_vc", Y1 + 24 * KB + 512, [16, 2, 64])
        n_pos = place("n_pos", Y1 + 25 * KB, [P, 2, 32])
        st = place("st", Y1 + 27 * KB - 256, [P, 128])
        m_k = place("m_k", Y1 + 10 * KB, [P, 4, T])
        m_v = place("m_v", Y1 + 14 * KB, [P, NT, MIX])
        n_w = place("n_w", Z0, [P, 2, 32, 64])
        mixed_in = place("mixed_in", X0 + 16 * KB, [P, DC, T])
        g_out = place("g_out", Z0 + 12 * KB, [P, 4 * T])
        g_q = place("g_q", X0, [P, 4, T])
        g_k = place("g_k", X0 + 4 * KB, [P, 4, T])
        g_v = place("g_v", X0 + 8 * KB, [P, NT, MIX])
        g_g = place("g_g", X0 + 12 * KB, [P, NT, MIX])
        g_p = place("g_p", Y1 + 16 * KB, [P, 4 * T])
        g_mask = place("g_mask", Y1 + 20 * KB, [P, 7, P])
        g_norm = place("g_norm", Y1 + 24 * KB, [P, MIX])
        g_qh = place("g_qh", Y1, [P, 4 * T])
        g_kh = place("g_kh", Y1 + 4 * KB, [P, 4 * T])
        g_a = place("g_a", Y1 + 8 * KB, [P, 4, NT, P])
        g_t = place("g_t", Y1 + 12 * KB, [P, 4 * T])
        p_c = place("p_c", Z0, [P, 4, T])
        p_inv = place("p_inv", Y1, [P, 4, T])
        p_w = place("p_w", Y1 + 4 * KB, [P, 4, P])
        p_a = place("p_a", Y1 + 6 * KB, [P, 4, T])
        p_b = place("p_b", Y1 + 10 * KB, [P, 4, T])
        s_u = place("s_u", Z0 + 4 * KB, [P, NT, MIX])
        s_v = place("s_v", Z0 + 8 * KB, [P, NT, MIX])
        s_w = place("s_w", Y1 + 14 * KB, [P, 4, P])
        s_wt = place("s_wt", Y1 + 16 * KB, [P, 4, P])
        s_g = place("s_g", Y1 + 18 * KB, [P, MIX])
        s_b = place("s_b", Y1 + 20 * KB, [P, MIX])
        s_o = place("s_o", Y1 + 22 * KB, [P, NT, MIX])
        m_g = place("m_g", Y1, [P, 2, 4 * T])
        m_t = place("m_t", Y1 + 8 * KB, [P, 4, T])
        x_q = place("x_q", Y1, [P, 4, T])
        x_k = place("x_k", Y1 + 4 * KB, [P, 4, T])
        x_v = place("x_v", Y1 + 8 * KB, [P, NT, MIX])
        x_s = place("x_s", Y1 + 12 * KB, [P, 4, T])
        x_pt = place("x_pt", Y1 + 16 * KB, [P, NT, 4 * P])
        d_in = [[place(f"d{x}{g}", at + 4 * j * KB, [P, 4, T] if x != "v" else [P, NT, MIX]) for j, x in enumerate("qkv")]
                for g, at in ((0, X0), (1, Z0))]
        d_s = place("d_s", Y1, [P, 4, T])
        d_pt = place("d_pt", Y1 + 4 * KB, [P, NT, 4 * P])
        d_bias = place("d_bias", Y1 + 8 * KB, [P, 4, T])
        d_tab = place("d_tab", Y1 + 12 * KB, [P, 2, T])
        f_h = place("f_h", Y1, [P, 2, CB, T], F32R)
        f_l = place("f_l", Y1 + 8 * KB, [P, 2, CB, T], F32R)
        f_a = place("f_a", Y1 + 16 * KB, [P, CB, T])
        f_b = place("f_b", Y1 + 20 * KB, [P, CB, T])
        l_in = [[place(f"l{x}{g}", at + 4 * j * KB, [P, 4, T] if x in "qk" else [P, NT, MIX]) for j, x in enumerate("qkvo")]
                for g, at in ((0, X0), (1, Z0))]
        l_norm = place("l_norm", Y1 + 16 * KB, [P, MIX])
        l_tab = place("l_tab", Y1 + 18 * KB, [P, 2 * P])
        l_s = place("l_s", Y1 + 19 * KB, [P, 2, T])
        l_gate = place("l_gate", Y1 + 21 * KB, [P, NT, 8])
        l_gb = place("l_gb", Y1 + 21 * KB + 128, [P, 8])
        l_lf = place("l_lf", Y1 + 21 * KB + 256, [P, NT, 4])
        l_cum = place("l_cum", Y1 + 21 * KB + 512, [P, NT, 4])
        l_i = place("l_i", Y1 + 21 * KB + 640, [P, NT, 4])
        l_e = place("l_e", Y1 + 21 * KB + 768, [P, NT, 4])
        l_a = place("l_a", Y1, [P, 4, T])
        l_b = place("l_b", Y1 + 4 * KB, [P, 4, T])
        l_pt = place("l_pt", Y1 + 8 * KB, [P, NT, 2 * P])
        l_h = place("l_h", Y1 + 10 * KB, [P, MIX])
        b_vec = place("b_vec", X0, [P, 8, SKEW])
        b_hot = place("b_hot", Y1 + 16 * KB, [REL, SKEW])
        b_rel = place("b_rel", Y1 + 18 * KB, [REL, 8])

        ps = ctx.enter_context(nc.psum_tensor("ps", [P, 8 * 512], F32))
        PC = 2048
        PT_ = 3072
        PO = 3584
        kv_dram = nc.dram_tensor("kv_dram", [2, P, 4 * T], F32)
        gate_dram = nc.dram_tensor("gate_dram", [4, NB, P, 4 * T], F32)
        bias_dram = nc.dram_tensor("bias_dram", [8, P, SKEW], F32)

        loaded = [sem(f"loaded{j}") for j in range(SLOTS)]
        hi_done = sem("hi_done")
        lo_done = sem("lo_done")
        unit_done = sem("unit_done")
        block_saved = sem("block_saved")
        tokens_in = sem("tokens_in")
        memory_in = sem("memory_in")
        kv_out = sem("kv_out")
        kv_in = sem("kv_in")
        tokens_turned = sem("tokens_turned")
        operand = sem("operand")
        params_in = sem("params_in")
        params_turned = sem("params_turned")
        small_in = sem("small_in")
        dve_step = sem("dve_step")
        centred = sem("centred")
        squares_done = sem("squares_done")
        piece_ready = sem("piece_ready")
        result_ready = sem("result_ready")
        shifted = sem("shifted")
        mapped = sem("mapped")
        left_ready = sem("left_ready")
        turned = sem("turned")
        turned_saved = sem("turned_saved")
        gate_done = sem("gate_done")
        gate_spilled = sem("gate_spilled")
        gate_loaded = [sem(f"gate_loaded{j}") for j in range(2)]
        conv_done = sem("conv_done")
        silu_done = sem("silu_done")
        silu_used = sem("silu_used")
        merge_added = sem("merge_added")
        hidden_ready = sem("hidden_ready")
        bias_out = sem("bias_out")
        answer_ready = sem("answer_ready")
        out_done = sem("out_done")

        OPERANDS = ["turn_params", "bias", "memory_half", "nsa", "xa", "gates2", "ml0", "ml1", "di0"]
        WHOLE = ["x", "memory", "branches", "mixed", "x1", "x2", "x3", "mixed2", "mem2", "x4", "xb", "x5", "y"]
        SMALL = {"bias": 2, "nsa": 7, "hgrn": 9, "pool": 14, "sgu": 14, "gates2": 16, "ml0": 17, "ml1": 18, "di0": 20, "di1": 21}

        def after(name):
            return OPERANDS.index(name) + 1

        def pieces(name, n=4):
            return 4 * WHOLE.index(name) + n

        def col(name, c=0, n=1):
            t, r = ROW_AT[name]
            return pcol[:, t, r + c:r + c + n]

        def wide(ap, n):
            return ap.unsqueeze(2).to_broadcast([ap.shape[0], ap.shape[1], n])

        def over(ap, n):
            return ap.unsqueeze(1).to_broadcast([ap.shape[0], n, ap.shape[1]])

        def pair(b):
            return ps[:, (b % 2) * 1024:(b % 2) * 1024 + 1024]

        def tab(name):
            x, y = tab_at[name]
            return tables[:, x:y]

        def rows(w, r0, c0, cols=UNIT):
            return w[r0:r0 + UNIT, c0:c0 + cols].rearrange("(k p) n -> p k n", p=P)

        win, win2 = a["w_in"][0], a["w_in_2"][0]
        wb = a["w_branch"][0]
        gains = [a["ln_mix_g"][0], a["mem_ln_g"], a["ln_x_g"][0], a["ln_ffn_g"][0]] + [a["ln_g_2"][0, j] for j in range(3)]
        biases = [a["ln_mix_b"][0], a["mem_ln_b"], a["ln_x_b"][0], a["ln_ffn_b"][0]] + [a["ln_b_2"][0, j] for j in range(3)]
        prow_src = {f"ln_g{j}": gains[j] for j in range(7)} | {f"ln_b{j}": biases[j] for j in range(7)}
        prow_src |= {"lb": a["hgrn_lb_logits"][0], "pool_scale": a["pool_scale"][0], "cb": a["ffn_conv_b"][0],
                     "cb2": a["conv_b_2"][0]}
        prow_src |= {f"cw{j}": a["ffn_conv_w"][0, j] for j in range(3)} | {f"c2w{j}": a["conv_w_2"][0, j] for j in range(4)}
        behind_sparse = Shadow("hgrn", "merge", [("F", g_q), ("F", g_k), ("T", g_v), ("T", g_g), ("F", p_c),
                                                 ("T", s_u), ("T", s_v)] + [("F", None)] * (4 * NB))
        behind_lstm = Shadow("mlstm1", "out2", [*zip("FFTT", l_in[1]), *zip("FFT", d_in[0]), *zip("FFT", d_in[1])])
        block = ctx.enter_context(nc.Block())

        @block.sync
        def _(sp):
            w = Walk()

            def load(src, cols=UNIT, perm=False):
                g = w.at("unit")
                slot = (w.n["unit"] - 1) % SLOTS
                if w.n["unit"] > SLOTS:
                    sp.wait_ge(lo_done, g - SLOTS)
                if perm:
                    for j in range(4):
                        for h in range(2):
                            sp.dma_start(wraw[:, slot, :, j * P + h * 64:j * P + h * 64 + 64],
                                         src[:, :, h * 256 + j * 64:h * 256 + j * 64 + 64]).then_inc(loaded[slot], 16)
                else:
                    sp.dma_start(wraw[:, slot, :, 0:cols], src).then_inc(loaded[slot], 16)

            def column(mat, c0, cols=UNIT, k=D, r0=0):
                for u in range(k // UNIT):
                    load(rows(mat, r0 + u * UNIT, c0, cols), cols)

            sp.dma_start(tok[:, :, :], a["x"][0].rearrange("(n p) d -> p n d", p=P)).then_inc(tokens_in, 16)
            sp.wait_ge(params_in, 16 * (len(ROWS) + 1))
            for u in range(4):
                load(rows(win, u * UNIT, C_Q), perm=True)
            sp.dma_start(mtok[:, :, :], a["mem"][0].rearrange("(n p) d -> p n d", p=P)).then_inc(memory_in, 16)
            column(win, C_KV)
            column(win, C_KV + UNIT, 280)
            column(a["xattn_k"][0], 0)
            column(a["xattn_v"][0], 0)
            for j in range(4):
                column(win, C_HG + j * MIX)
            column(win, C_POOL)
            column(win, C_SG)
            column(win, C_SG + MIX)
            for n in range(4):
                for cb in range(NB):
                    column(win, C_MERGE + n * D + cb * UNIT)
            with sp.Fori(0, 4) as i, w.loop(i, 0, 4, {"unit": 4}):
                for cb in range(NB):
                    load(wb[i, :, cb * UNIT:(cb + 1) * UNIT].rearrange("(k p) n -> p k n", p=P))

            def square(mat):
                with sp.Fori(0, NB // 2) as i, w.loop(i, 0, NB // 2, {"unit": 8}):
                    for cb in range(2):
                        for u in range(4):
                            load(mat[u * UNIT:(u + 1) * UNIT, bass.ds(i * 2 * UNIT + cb * UNIT, UNIT)]
                                 .rearrange("(k p) n -> p k n", p=P))

            def ffn(gate, gate_c, up, up_c, down):
                with sp.Fori(0, FB) as i, w.loop(i, 0, FB, {"unit": 8}):
                    for mat, c0 in ((gate, gate_c), (up, up_c)):
                        for u in range(4):
                            load(mat[u * UNIT:(u + 1) * UNIT, bass.ds(i * UNIT + c0, UNIT)]
                                 .rearrange("(k p) n -> p k n", p=P))
                with sp.Fori(0, FB) as i, w.loop(i, 0, FB, {"unit": 4}):
                    for cb in range(NB):
                        load(down[bass.ds(i * UNIT, UNIT), cb * UNIT:(cb + 1) * UNIT]
                             .rearrange("(k p) n -> p k n", p=P))

            square(a["w_mix_out"][0])
            column(a["xattn_q"][0], 0)
            for cb in range(NB):
                column(a["xattn_o"][0], cb * UNIT, k=UNIT)
            ffn(a["ffn_in"][0], 0, a["ffn_in"][0], FF, a["ffn_out"][0])
            column(win2, C2_GATE, 8)
            for g in range(2):
                for c0 in (0, 1024, 2048, 3072):
                    column(win2, c0 + g * UNIT)
            for g in range(2):
                for c0 in (0, 1024, 2048):
                    column(win2, C2_DQ + c0 + g * UNIT)
            for units in ((0, 1, 2), (3,)):
                for cb in range(2):
                    for u in units:
                        load(rows(a["w_out_2"][0], u * UNIT, cb * UNIT))
            column(a["w_out_2"][0], 2 * UNIT)
            sp.wait_ge(piece_ready, pieces("mixed2"))
            sp.dma_start(mtok2[:, :, :], a["mem_2"][0].rearrange("(n p) d -> p n d", p=P)).then_inc(tokens_in, 16)
            column(a["w_out_2"][0], 3 * UNIT)
            column(a["xk_2"][0], 0)
            column(a["xv_2"][0], 0)
            column(a["xq_2"][0], 0)
            with sp.Fori(1, 4) as i, w.loop(i, 1, 3, {"unit": 12}):
                for mat in (a["xk_2"][0], a["xv_2"][0], a["xq_2"][0]):
                    for u in range(4):
                        load(mat[u * UNIT:(u + 1) * UNIT, bass.ds(i * UNIT, UNIT)]
                             .rearrange("(k p) n -> p k n", p=P))
            square(a["xo_2"][0])
            ffn(a["w1_2"][0], 0, a["w3_2"][0], 0, a["w2_2"][0])
            assert w.n["unit"] == UNITS
            for q in range(4):
                c = slice(q * UNIT, (q + 1) * UNIT)
                sp.wait_ge(answer_ready, q + 1)
                sp.dma_start(out[0].rearrange("(n p) d -> p n d", p=P)[:, :, c], outt[:, :, c]).then_inc(out_done, 16)
            sp.wait_ge(out_done, 16 * 4)

        @block.gpsimd
        def _(pool):
            with pool.Fori(0, UNITS // SLOTS) as i:
                for slot in range(SLOTS):
                    pool.wait_ge(hi_done, i * SLOTS + (slot + 1))
                    pool.tensor_tensor(wlo[:, slot], wraw[:, slot], whi[:, slot].bitcast(F32),
                                       ALU.subtract).then_inc(lo_done, 1)

        @block.scalar
        def _(act):
            w = Walk()

            def hi(n, first_load=16):
                for _ in range(n):
                    g = w.at("unit")
                    slot = (w.n["unit"] - 1) % SLOTS
                    act.wait_ge(loaded[slot], w.at(f"slot{slot}", first_load))
                    if w.n["unit"] > SLOTS:
                        act.wait_ge(unit_done, g - SLOTS)
                    act.activation(whi[:, slot], wraw[:, slot], ACT.Copy).then_inc(hi_done, 1)

            def small(dst, src):
                act.dma_start(dst, src).then_inc(small_in, 16)

            def mapping(*ins):
                act.wait_ge(shifted, w.at("shifted"))
                for n, (dst, src, fn) in enumerate(ins):
                    x = act.activation(dst, src, fn)
                    if n == len(ins) - 1:
                        x.then_inc(mapped, 1)

            def save_turned(dst, src):
                act.wait_ge(turned, w.at("turned"))
                act.activation(dst, src, ACT.Copy).then_inc(turned_saved, 1)

            def square(cb):
                act.wait_ge(centred, w.at("centred"))
                act.activation(ln_sq[:, :, :], res[:, 4 * cb:4 * cb + 4, :], ACT.Square).then_inc(squares_done, 1)

            def norm(ahead=0, units=4, more=None, late=0):
                for cb in range(4):
                    hi(more[cb] if more else ahead if cb == 3 else units)
                    square(cb)
                hi(late)
                mapping((ln_rstd[:, :], ln_rstd[:, :], ACT.Sqrt))

            at_unit = [behind_sparse.first]
            gates = [0]

            def fill(shadow, k):
                hi(min(at_unit[0] + SLOTS, shadow.end) - w.n["unit"])
                while shadow is behind_sparse and gates[0] < (at_unit[0] - BASE["gates"]) // CB:
                    save_gates()
                at_unit[0] = shadow.upto(at_unit[0], k)

            def save_gates():
                n = gates[0]
                if n:
                    act.wait_ge(gate_spilled, 16 * n)
                act.wait_ge(unit_done, BASE["gates"] + CB * (n + 1))
                act.activation(g_out[:, :], pair(FIRST_GATE + n), ACT.Sigmoid).then_inc(gate_done, 1)
                act.wait_ge(gate_done, n + 1)
                act.dma_start(gate_dram[n // NB, n % NB], g_out[:, :]).then_inc(gate_spilled, 16)
                gates[0] += 1

            for t, name, r in ROWS:
                at = ROW_AT[name][1]
                src = a["sg_b"][0] if name == "sg_b" else prow_src[name].rearrange("(c p) -> c p", p=P)
                act.dma_start(prow[at:at + r, t, :], src).then_inc(params_in, 16)
            act.dma_start(core[:, :], tab("core")).then_inc(params_in, 16)
            small(b_hot[:, :], tab("hot")[0:REL, :])
            small(b_rel[:, :], a["rel_bias_2"])
            hi(4, 128)
            act.wait_ge(operand, after("bias"))
            act.dma_start(bias_dram.ap().rearrange("h p n -> p h n"), b_vec[:, :, :]).then_inc(bias_out, 16)
            hi(4)
            act.wait_ge(bias_out, 16)
            square(0)
            square(1)
            hi(4)
            square(2)
            square(3)
            mapping((ln_rstd[:, :], ln_rstd[:, :], ACT.Sqrt))
            act.wait_ge(piece_ready, pieces("memory"))
            small(n_tab[:, :], tab("nsa"))
            for g in range(2):
                small(n_w[64 * g:64 * g + 64], a["nsa_cmp_w"][0].rearrange("v l d e -> d v l e"))
                with nc.allow_non_contiguous_dma("small"):
                    small(n_pos[64 * g:64 * g + 64], a["nsa_cmp_pos"][0].rearrange("v l d -> d v l"))
            hi(4)
            mapping((n_gate[:, :, :], n_gate[:, :, :], ACT.Sigmoid))
            hi(4)
            for j, x in enumerate((m_k, m_v)):
                act.wait_ge(block_saved, 4 + j)
                act.dma_start(kv_dram[j], x[:, :, :].rearrange("p a b -> p (a b)")).then_inc(kv_out, 16)
            fill(behind_sparse, 2)
            for g in range(2):
                for qt in range(NT):
                    for br in range(3):
                        n = NCMP if br == 0 else P * (qt + 1)
                        fill(behind_sparse, 3)
                        mapping((n_s[:, :, 0:n], n_s[:, :, 0:n], ACT.Exp))
                        for kt in range(1 if br == 0 else qt + 1):
                            kn = NCMP if br == 0 else P
                            save_turned(n_pt[0:kn, kt, :], ps[0:kn, PT_:PT_ + 512])
            act.wait_ge(operand, after("nsa"))
            small(g_mask[:, :, :], tab("level").rearrange("p (l n) -> p l n", l=7))
            small(g_norm[:, :], a["hgrn_norm_g"][0].partition_broadcast(P))
            mapping((st[:, 0:4], st[:, 0:4], ACT.Exp))
            fill(behind_sparse, 4)
            mapping((g_k[:, :, :], g_k[:, :, :], ACT.Sigmoid))
            mapping((g_p[:, :], g_k[:, :, :].rearrange("p h t -> p (h t)"), ACT.Ln))
            for l in range(8):
                h = 1 << l
                fill(behind_sparse, 3)
                v = g_p[:, :].rearrange("p (m two h) -> p m two h", two=2, h=h)
                e = g_t[:, :].rearrange("p (m two h) -> p m two h", two=2, h=h)
                mapping((e[:, :, 0, :], e[:, :, 0, :], ACT.Exp), (e[:, :, 1, :], v[:, :, 1, :], ACT.Exp))
            fill(behind_sparse, 2)
            fill(behind_sparse, 3)
            mapping((g_t[:, :], ps[:, PC:PC + 1024], ACT.Square))
            mapping((st[:, 0:8], st[:, 0:8], ACT.Sqrt))
            mapping((g_g[:, :, :], g_g[:, :, :], ACT.Silu))
            fill(behind_sparse, 4)
            act.wait_ge(piece_ready, pieces("branches", 2))
            small(p_inv[:, :, :], tab("cnt").rearrange("p (g t) -> p g t", g=4))
            small(p_w[:, :, :], a["pool_w"][0].rearrange("g c d -> c g d"))
            small(s_w[:, :, :], a["sg_w"][0].rearrange("g q p -> q g p"))
            small(s_g[:, :], a["sg_ln_g"][0].partition_broadcast(P))
            small(s_b[:, :], a["sg_ln_b"][0].partition_broadcast(P))
            fill(behind_sparse, 4)
            mapping((s_u[:, :, :], s_u[:, :, :], ACT.Gelu_apprx_tanh))
            mapping((s_v[:, :, :], s_v[:, :, :], ACT.Gelu_apprx_tanh))
            mapping((st[:, 32:34], st[:, 32:34], ACT.Sqrt))
            fill(behind_sparse, 3)
            fill(behind_sparse, 4)
            while at_unit[0] < behind_sparse.end:
                fill(behind_sparse, 4)
            while gates[0] < 4 * NB:
                save_gates()
            act.wait_ge(piece_ready, pieces("branches"))
            hi(2)
            with act.Fori(0, 4) as i, w.loop(i, 0, 4, {"unit": 4, "added": 4, **{f"slot{s}": 16 for s in range(4)}}):
                for cb in range(NB):
                    hi(1)
                    act.wait_ge(merge_added, w.at("added"))
                    act.dma_start(m_g[:, cb % 2, :], gate_dram.ap()[bass.ds(i, 1), cb].rearrange("o p n -> (o p) n")
                                  ).then_inc(gate_loaded[cb % 2], 16)
                    if cb == 0:
                        act.wait_ge(gate_spilled, 16 * 4 * NB)

            def ffn(name, conv, ahead):
                per = {"unit": 8, "silu": 1, **{f"slot{s}": 32 for s in range(4)}}
                with act.Fori(0, FB) as i, w.loop(i, 0, FB, per):
                    hi(6)
                    n = w.at("silu")
                    if conv:
                        act.wait_ge(conv_done, n + 1)
                        act.activation(f_a[:, :, :], f_a[:, :, :], ACT.Silu).then_inc(silu_done, 1)
                    else:
                        act.wait_ge(unit_done, BASE[name] + 8 * i + 4)
                        act.wait_ge(silu_used, n + 1)
                        act.activation(f_a[:, :, :], pair(0).rearrange("p (s t) -> p s t", s=4),
                                       ACT.Silu).then_inc(silu_done, 1)
                    hi(2)
                with act.Fori(0, FB - 1) as i, w.loop(i, 0, FB - 1, {"unit": 4, **{f"slot{s}": 16 for s in range(4)}}):
                    hi(4)
                norm(ahead, 0)

            hi(2)
            act.wait_ge(piece_ready, pieces("mixed"))
            act.wait_ge(kv_out, 32)
            for j, x in enumerate((x_k, x_v)):
                act.dma_start(x[:, :, :].rearrange("p a b -> p (a b)"), kv_dram[j]).then_inc(kv_in, 16)
            norm(4)
            hi(4)
            for qt in range(NT):
                mapping((x_s[:, :, :], x_s[:, :, :], ACT.Exp))
                for kt in range(NT):
                    save_turned(x_pt[:, kt, :], ps[:, PT_:PT_ + 512])
            norm(4, 0)
            ffn("ffn_in", True, 4)
            act.wait_ge(piece_ready, pieces("x3"))
            small(l_gb[:, :], a["gate_b_2"][0].partition_broadcast(P))
            small(l_tab[:, :], tab("causal"))
            hi(8)
            mapping((l_e[:, :, :], l_e[:, :, :], ACT.Exp))
            mapping((l_e[:, :, :], l_e[:, :, :], ACT.Ln))
            at_unit[0] = behind_lstm.first
            for g in range(2):
                if g:
                    act.wait_ge(operand, after("ml0"))
                small(l_norm[:, :], a["mh_g_2"][0, g * MIX:(g + 1) * MIX].partition_broadcast(P))
                if g == 0:
                    hi(12)
                q, k, _, o = l_in[g]
                fill(behind_lstm, LSTM_FILL[g][0])
                mapping((q[:, :, :], l_a[:, :, :], ACT.Silu))
                mapping((k[:, :, :], l_a[:, :, :], ACT.Silu))
                mapping((o[:, :, :], o[:, :, :], ACT.Sigmoid))
                for qt in range(NT):
                    n = P * (qt + 1)
                    fill(behind_lstm, LSTM_FILL[g][1 + 2 * qt])
                    mapping((l_s[:, :, 0:n], l_s[:, :, 0:n], ACT.Exp), (st[:, 8:10], st[:, 8:10], ACT.Exp))
                    for kt in range(qt + 1):
                        save_turned(l_pt[:, kt, :], ps[:, PT_:PT_ + 256])
                    fill(behind_lstm, LSTM_FILL[g][2 + 2 * qt])
                    mapping((st[:, 32:34], st[:, 32:34], ACT.Sqrt))
            for g in range(2):
                act.wait_ge(operand, after(f"ml1" if g == 0 else "di0"))
                if g == 0:
                    small(d_tab[:, :, :], tab("dil").rearrange("p (a n) -> p a n", a=2))
                skew = bass.AP(bias_dram, 4 * g * P * SKEW + P - 1, [[SKEW - 1, P], [P * SKEW, 4], [1, T]])
                small(d_bias[:, :, :], skew)
                if g == 0:
                    fill(behind_lstm, 4)
                for qt in range(NT):
                    n = P * (qt + 1)
                    if g == 0:
                        fill(behind_lstm, 4)
                    else:
                        hi(3 if qt else 4)
                    mapping((d_s[:, :, 0:n], d_s[:, :, 0:n], ACT.Exp))
                    for kt in range(qt + 1):
                        save_turned(d_pt[:, kt, :], ps[:, PT_:PT_ + 512])
            hi(1)
            norm(more=(4, 4, 0, 4), late=2)
            hi(6)
            for head in range(4):
                hi(4)
                mapping((x_s[:, 0:2, :], x_s[:, 0:2, :], ACT.Exp))
                save_turned(x_pt[:, 0, :], ps[:, PT_:PT_ + 512])
                if head < 3:
                    hi(8)
            norm(4)
            ffn("ffn2_in", False, 0)
            for q in range(4):
                act.wait_ge(tokens_turned, 5 + q)
                act.activation(outt[:, :, q * UNIT:(q + 1) * UNIT], ps[:, q * 1024:(q + 1) * 1024]
                               .rearrange("p (n c) -> p n c", n=NT), ACT.Copy).then_inc(answer_ready, 1)
            assert w.n["unit"] == UNITS

        @block.tensor
        def _(pe):
            w = Walk()

            def products(parts, units, hi, lo, bank, chunk=0, fresh=True, last=True, dyn=None, first_of=None,
                         begin=0):
                for u in range(begin, units):
                    if first_of:
                        pe.wait_ge(piece_ready, pieces(first_of, u + 1))
                    pe.wait_ge(lo_done, w.at("unit"))
                    slot = (w.n["unit"] - 1) % SLOTS
                    for k in range(CB):
                        begun = set()
                        for kind, c, width, h, at in parts:
                            first = fresh and u == 0 and k == 0 and at // 512 not in begun
                            begun.add(at // 512)
                            stop = last and u == units - 1 and k == CB - 1
                            kc = chunk + u * CB + k
                            for n, (wt, op) in enumerate(((whi, hi), (whi, lo), (wlo, hi))):
                                wk = wt[:, slot, k, c:c + (P if kind == "F" else width)]
                                if kind == "F":
                                    x = op[:, kc, :] if dyn is None else op[:, dyn + k, :]
                                    o = ps[:, bank + at:bank + at + T]
                                    ins = pe.matmul(o, wk, x, start=first and n == 0, stop=stop and n == 2,
                                                    skip_group_check=True)
                                else:
                                    x = op[:, kc, h * P:h * P + P]
                                    o = ps[:, bank + at:bank + at + width]
                                    ins = pe.matmul(o, x, wk, start=first and n == 0, stop=stop and n == 2,
                                                    skip_group_check=True)
                    ins.then_inc(unit_done, 1)

            def column(parts=F_BLOCK, units=4, hi=act_h, lo=act_l, first_of=None, dyn=None, last=True):
                b = w.at("block")
                if w.n["block"] > 2:
                    pe.wait_ge(block_saved, b - 2)
                products(parts, units, hi, lo, ((w.n["block"] - 1) % 2) * 1024, first_of=first_of, dyn=dyn,
                         last=last)

            def fill(shadow, k):
                for unit in range(w.n["unit"], shadow.upto(w.n["unit"], k)):
                    n, u = divmod(unit - shadow.first, CB)
                    kind, place = shadow.blocks[n]
                    if u == 0:
                        b = w.at("block")
                        if b - 2 <= FIRST_GATE or shadow is not behind_sparse:
                            pe.wait_ge(block_saved, b - 2)
                        else:
                            pe.wait_ge(gate_done, b - 2 - FIRST_GATE)
                    products(F_BLOCK if kind == "F" else T_BLOCK, u + 1, act_h, act_l, ((w.n["block"] - 1) % 2) * 1024,
                             begin=u, last=u == CB - 1)

            def saved():
                pe.wait_ge(block_saved, w.now("block"))

            def mm(o, left, right, start, stop):
                return pe.matmul(o, left, right, start=start, stop=stop, skip_group_check=True)

            def turn(o, src, n=P):
                k = src.shape[0]
                return pe.matmul(o, src, ident[0:k, 0:k], start=True, stop=True, is_transpose=True, skip_group_check=True)

            def turn_tokens(count, tok=tok):
                pe.wait_ge(tokens_in, 16 * count)
                for c in range(DC):
                    for h in range(NT):
                        x = turn(ps[:, c * T + h * P:c * T + h * P + P], tok[:, h, c * P:c * P + P])
                x.then_inc(tokens_turned, 1)

            def turn_memory(half):
                for c in range(DC // 2):
                    for h in range(NT):
                        o = 2048 + c * T + h * P
                        x = turn(ps[:, o:o + P], mtok[:, h, (half * DC // 2 + c) * P:(half * DC // 2 + c) * P + P])
                x.then_inc(tokens_turned, 1)

            def mean_of(x):
                pe.wait_ge(left_ready, w.at("left"))
                mm(ps[:, PC:PC + T], mean_w, x[:, :], True, True).then_inc(result_ready, 1)

            def norm():
                mean_of(ln_t)
                mean_of(ln_s2)

            def turn_probs(s, heads, keys):
                for kt in range(-(-keys // P)):
                    kn = min(keys, P)
                    if w.n.get("turned", 0):
                        pe.wait_ge(turned_saved, w.now("turned"))
                    w.at("turned")
                    for j in range(heads):
                        x = turn(ps[0:kn, PT_ + j * P:PT_ + j * P + P], s[:, j, kt * P:kt * P + kn])
                    x.then_inc(turned, 1)
                pe.wait_ge(turned_saved, w.now("turned"))

            def turn_rows(src, blocks, bank=PC):
                pe.wait_ge(left_ready, w.at("left"))
                for j, (o, n, c) in enumerate(blocks):
                    x = turn(ps[:, bank + o:bank + o + P], src[:, n, c * P:c * P + P])
                x.then_inc(result_ready, 1)

            pe.wait_ge(params_in, 16 * (len(ROWS) + 1))
            for t in range(5):
                x = turn(ps[:, t * P:t * P + ROW_N[t]], prow[0:ROW_N[t], t, :])
            x.then_inc(params_turned, 1)
            pe.wait_ge(operand, after("turn_params"))
            pe.wait_ge(small_in, 16 * SMALL["bias"])
            for h in range(8):
                x = mm(ps[:, h * 512:h * 512 + SKEW], b_rel[:, h:h + 1].to_broadcast([REL, P]), b_hot[:, :], True, True)
            x.then_inc(result_ready, 1)
            pe.wait_ge(operand, after("bias"))
            turn_tokens(1)
            column(first_of="x")
            pe.wait_ge(memory_in, 16)
            turn_memory(0)
            column(KV0_BLOCK)
            pe.wait_ge(operand, after("memory_half"))
            turn_memory(1)
            column(KV1_BLOCK, units=2, last=False)
            norm()
            products(KV1_BLOCK, 4, act_h, act_l, 0, begin=2)
            column(hi=alt_h, lo=alt_l, first_of="memory")
            column(T_BLOCK, hi=alt_h, lo=alt_l)
            saved()
            pe.wait_ge(left_ready, w.at("left"))
            for g in range(2):
                r = slice(64 * g, 64 * g + 64)
                for l in range(32):
                    mm(ps[r, PC:PC + NCMP], n_w[r, 0, l, :], n_win[r, 0, l, :], l == 0, l == 31)
            for g in range(2):
                r = slice(64 * g, 64 * g + 64)
                for l in range(32):
                    x = mm(ps[0:NCMP, PC + 512 + 512 * g:PC + 576 + 512 * g], n_win[r, 1, l, :], n_w[r, 1, l, :],
                           l == 0, l == 31)
            x.then_inc(result_ready, 1)
            fill(behind_sparse, 2)
            pe.wait_ge(left_ready, w.at("left"))
            for g in range(2):
                r = slice(64 * g, 64 * g + 64)
                for qt in range(NT):
                    for br in range(3):
                        n = NCMP if br == 0 else P * (qt + 1)
                        keys = n_kc[r, 0:NCMP] if br == 0 else n_kv[r, br + 1, 0:n]
                        for j in range(4):
                            x = mm(ps[:, PC + j * T:PC + j * T + n], n_q[r, j, qt * P:qt * P + P], keys, True, True)
                        x.then_inc(result_ready, 1)
                        fill(behind_sparse, 3)
                        pe.wait_ge(left_ready, w.at("left"))
                        turn_probs(n_s, 4, n)
                        for j in range(4):
                            o = ps[64 * (j % 2):64 * (j % 2) + 64, PO + (j // 2) * P:PO + (j // 2) * P + P]
                            for kt in range(-(-n // P)):
                                kn = min(n, P)
                                v = n_vc[0:NCMP, g, :] if br == 0 else n_v[:, br - 1, kt, 64 * g:64 * g + 64]
                                x = mm(o, v, n_pt[0:kn, kt, j * P:j * P + P], br == 0 and j < 2, br == 2 and kt == qt)
                    x.then_inc(result_ready, 1)
            for l in range(-1, 7):
                fill(behind_sparse, 4 if l < 0 else 3)
                pe.wait_ge(left_ready, w.at("left"))
                for h in range(4):
                    for n in range(NT):
                        c = h * T + n * P
                        kk = g_k[:, h, n * P:n * P + P] if l < 0 else g_kh[:, c:c + P]
                        qq = g_q[:, h, n * P:n * P + P] if l < 0 else g_qh[:, c:c + P]
                        x = mm(ps[:, PC + c:PC + c + P], kk, qq, True, True)
                x.then_inc(result_ready, 1)
            fill(behind_sparse, 3)
            pe.wait_ge(left_ready, w.at("left"))
            for h in range(4):
                x = mm(ps[:, PC + h * P:PC + h * P + P], g_kh[:, h * T:h * T + P], g_qh[:, h * T + P:h * T + T], True, True)
            x.then_inc(result_ready, 1)
            fill(behind_sparse, 2)
            pe.wait_ge(left_ready, w.at("left"))
            for n in range(NT):
                for h in range(4):
                    o = ps[:, PC + n * 512 + h * P:PC + n * 512 + h * P + P]
                    x = mm(o, g_a[:, h, n, :], g_v[:, n, h * P:h * P + P], h == 0, n == 0)
                    if n:
                        x = mm(o, g_p[:, h * P:h * P + P], g_v[:, 0, h * P:h * P + P], False, True)
            x.then_inc(result_ready, 1)
            fill(behind_sparse, 3)
            turn_rows(g_t[:, :].rearrange("p (n c) -> p n c", n=NT), [(c * T + n * P, n, c) for c in range(4) for n in range(NT)])
            fill(behind_sparse, 4)
            pe.wait_ge(left_ready, w.at("left"))
            for g in range(4):
                x = mm(ps[:, PC + g * T:PC + g * T + T], p_w[:, g, :], p_b[:, g, :], g % 2 == 0, True)
            x.then_inc(result_ready, 1)
            fill(behind_sparse, 4)
            pe.wait_ge(left_ready, w.at("left"))
            for g in range(4):
                x = turn(ps[:, PC + g * P:PC + g * P + P], s_w[:, g, :])
            x.then_inc(result_ready, 1)
            fill(behind_sparse, 3)
            pe.wait_ge(left_ready, w.at("left"))
            for n in range(NT):
                for g in range(4):
                    o = n * 512 + g * P
                    x = mm(ps[:, PC + o:PC + o + P], s_wt[:, g, :], s_v[:, n, g * P:g * P + P], g == 0, True)
            x.then_inc(result_ready, 1)
            fill(behind_sparse, 4)
            turn_rows(s_o, [(c * T + n * P, n, c) for c in range(4) for n in range(NT)])
            while w.n["unit"] < behind_sparse.end:
                fill(behind_sparse, 4)
            pe.wait_ge(piece_ready, pieces("branches"))
            with pe.Fori(0, 4) as i, w.loop(i, 0, 4, {"unit": 4, "block": 4}):
                for cb in range(NB):
                    column(units=1, hi=alt_h, lo=alt_l, dyn=i * CB)

            def square(hi, lo, first_of):
                with pe.Fori(0, 2) as i, w.loop(i, 0, 2, {"unit": 8, "block": 2}):
                    column(hi=hi, lo=lo, first_of=first_of)
                    column(hi=hi, lo=lo)

            def ffn(conv, first_of):
                per = {"unit": 8, "conv": 1, "silu": 1, "used": 1}
                with pe.Fori(0, FB) as i, w.loop(i, 0, FB, per):
                    if conv:
                        pe.wait_ge(conv_done, w.now("conv") + 1)
                    else:
                        pe.wait_ge(silu_done, w.now("silu"))
                    w.at("conv")
                    w.at("silu")
                    products(F_BLOCK, 4, act_h, act_l, 0, first_of=first_of)
                    pe.wait_ge(silu_used, w.at("used"))
                    products(F_BLOCK, 4, act_h, act_l, 1024)
                w.at("used")

                def piece(fresh, last, parity):
                    pe.wait_ge(hidden_ready, w.at("hidden"))
                    for cb in range(NB):
                        products(F_BLOCK, 1, f_h[:, parity], f_l[:, parity], cb * 1024, fresh=fresh, last=last)

                piece(True, False, 0)
                with pe.Fori(0, FB // 2 - 1) as i, w.loop(i, 0, FB // 2 - 1, {"unit": 8, "hidden": 2}):
                    piece(False, False, 1)
                    piece(False, False, 0)
                piece(False, False, 1)
                piece(False, True, 0)

            assert w.n["block"] % 2 == 0
            square(alt_h, alt_l, "mixed")
            norm()
            column(first_of="x1")
            saved()
            pe.wait_ge(kv_in, 32)
            for qt in range(NT):
                for j in range(4):
                    x = mm(ps[:, PC + j * T:PC + j * T + T], x_q[:, j, qt * P:qt * P + P], x_k[:, j, :], True, True)
                x.then_inc(result_ready, 1)
                pe.wait_ge(left_ready, w.at("left"))
                turn_probs(x_s, 4, T)
                for j in range(4):
                    for kt in range(NT):
                        x = mm(ps[:, PO + j * P:PO + j * P + P], x_v[:, kt, j * P:j * P + P],
                               x_pt[:, kt, j * P:j * P + P], j + kt == 0, kt == 1)
                x.then_inc(result_ready, 1)
            pe.wait_ge(operand, after("xa"))
            for cb in range(NB):
                column(units=1, hi=alt_h, lo=alt_l)
            norm()
            ffn(True, "x2")
            norm()
            column(GATE_BLOCK, first_of="x3")
            column()
            pe.wait_ge(left_ready, w.at("left"))
            mm(ps[:, PC:PC + 4], tri, l_lf[:, 0, :], True, True)
            mm(ps[:, PC + 4:PC + 8], tri, l_lf[:, 1, :], False, False)
            mm(ps[:, PC + 4:PC + 8], ones, l_lf[:, 0, :], False, True).then_inc(result_ready, 1)
            column()
            column(T_BLOCK)
            column(T_BLOCK)
            for g in range(2):
                q, k, v, _ = l_in[g]
                fill(behind_lstm, LSTM_FILL[g][0])
                pe.wait_ge(left_ready, w.at("left"))
                for qt in range(NT):
                    n = P * (qt + 1)
                    for j in range(2):
                        for kt in range(qt + 1):
                            mm(ps[:, PC + j * T + kt * P:PC + j * T + kt * P + P],
                               l_i[:, kt, 2 * g + j:2 * g + j + 1].to_broadcast([P, P]), ident, True, True)
                    for j in range(2):
                        for c in range(2):
                            x = mm(ps[:, PC + 512 + j * T:PC + 512 + j * T + n], q[:, 2 * j + c, qt * P:qt * P + P],
                                   k[:, 2 * j + c, 0:n], c == 0 and j == 0, c == 1)
                    x.then_inc(result_ready, 1)
                    fill(behind_lstm, LSTM_FILL[g][1 + 2 * qt])
                    pe.wait_ge(left_ready, w.at("left"))
                    turn_probs(l_s, 2, n)
                    for j in range(2):
                        for kt in range(qt + 1):
                            x = mm(ps[:, PO + j * T:PO + j * T + T], l_pt[:, kt, j * P:j * P + P],
                                   v[:, kt, j * T:j * T + T], j + kt == 0, kt == qt)
                    x.then_inc(result_ready, 1)
                    fill(behind_lstm, LSTM_FILL[g][2 + 2 * qt])
                    turn_rows(l_h[:, :].unsqueeze(1), [(c * P, 0, c) for c in range(4)], PT_)
            for g in range(2):
                q, k, v = d_in[g]
                if g == 0:
                    fill(behind_lstm, 4)
                pe.wait_ge(left_ready, w.at("left"))
                for qt in range(NT):
                    n = P * (qt + 1)
                    for j in range(4):
                        x = mm(ps[:, PC + j * T:PC + j * T + n], q[:, j, qt * P:qt * P + P], k[:, j, 0:n], True, True)
                    x.then_inc(result_ready, 1)
                    if g == 0:
                        fill(behind_lstm, 4)
                    else:
                        assert w.n["block"] % 2 == qt
                        column(units=3, hi=alt_h, lo=alt_l, first_of="mixed2", last=False)
                    pe.wait_ge(left_ready, w.at("left"))
                    turn_probs(d_s, 4, n)
                    for j in range(4):
                        for kt in range(qt + 1):
                            x = mm(ps[:, PO + j * P:PO + j * P + P], v[:, kt, j * P:j * P + P],
                                   d_pt[:, kt, j * P:j * P + P], j + kt == 0, kt == qt)
                    x.then_inc(result_ready, 1)
            for cb in range(2):
                products(F_BLOCK, 4, alt_h, alt_l, cb * 1024, begin=3, first_of="mixed2")
            for cb in range(2, NB):
                column(hi=alt_h, lo=alt_l)
            saved()
            turn_tokens(2, mtok2)
            pe_bank = (w.n["block"] % 2) * 1024
            column(units=2, hi=alt_h, lo=alt_l, first_of="mem2", last=False)
            mean_of(ln_t)
            products(F_BLOCK, 3, alt_h, alt_l, pe_bank, begin=2, last=False, first_of="mem2")
            mean_of(ln_s2)
            products(F_BLOCK, 4, alt_h, alt_l, pe_bank, begin=3, first_of="mem2")
            column(T_BLOCK, hi=alt_h, lo=alt_l)
            column(first_of="x4")
            for head in range(4):
                saved()
                for qt in range(NT):
                    for c in range(4):
                        x = mm(ps[:, PC + qt * T:PC + qt * T + T], x_q[:, c, qt * P:qt * P + P], x_k[:, c, :],
                               c + qt == 0, c == 3)
                x.then_inc(result_ready, 1)
                if head < 3:
                    column(hi=alt_h, lo=alt_l)
                pe.wait_ge(left_ready, w.at("left"))
                pe.wait_ge(turned_saved, w.now("turned"))
                w.at("turned")
                for kt in range(NT):
                    for qt in range(NT):
                        x = turn(ps[:, PT_ + kt * T + qt * P:PT_ + kt * T + qt * P + P], x_s[:, qt, kt * P:kt * P + P])
                x.then_inc(turned, 1)
                pe.wait_ge(turned_saved, w.now("turned"))
                for c in range(4):
                    for kt in range(NT):
                        x = mm(ps[:, PC + c * T:PC + c * T + T], x_v[:, kt, c * P:c * P + P],
                               x_pt[:, 0, kt * T:kt * T + T], (c % 2) + kt == 0, kt == 1)
                x.then_inc(result_ready, 1)
                if head < 3:
                    column(T_BLOCK, hi=alt_h, lo=alt_l)
                    column()
            square(alt_h, alt_l, "xb")
            norm()
            ffn(False, "x5")
            norm()
            for q in range(4):
                pe.wait_ge(piece_ready, pieces("y", q + 1))
                for h in range(NT):
                    for c in range(CB):
                        o = q * 1024 + h * UNIT + c * P
                        x = turn(ps[:, o:o + P], res[:, CB * q + c, h * P:h * P + P])
                x.then_inc(tokens_turned, 1)
            assert w.n["unit"] == UNITS

        @block.vector
        def _(dve):
            w = Walk()
            told = [0]

            def link(ins):
                ins.then_inc(dve_step, 1)
                dve.wait_ge(dve_step, w.at("step"))

            def tell(name, ins):
                told[0] += 1
                assert after(name) == told[0], name
                ins.then_inc(operand, 1)
                dve.wait_ge(operand, told[0])

            def to_act(ins):
                ins.then_inc(shifted, 1)
                dve.wait_ge(mapped, w.at("mapped"))

            def to_pe(ins):
                ins.then_inc(left_ready, 1)
                dve.wait_ge(left_ready, w.at("left"))

            def from_pe():
                dve.wait_ge(result_ready, w.at("result"))

            def copy(dst, src):
                return dve.tensor_copy(dst, src)

            def tt(dst, x, y, op):
                return dve.tensor_tensor(dst, x, y, op)

            def split(hi, lo, src, name=None, piece=False):
                link(copy(hi, src))
                x = tt(lo, src, hi.bitcast(F32), ALU.subtract)
                if piece:
                    x.then_inc(piece_ready, 1)
                    dve.wait_ge(piece_ready, w.at("piece"))
                elif name:
                    tell(name, x)
                else:
                    link(x)

            def split_pieces(name, hi, lo, src):
                for q in range(4):
                    split(hi[:, 4 * q:4 * q + 4, :], lo[:, 4 * q:4 * q + 4, :], src(q), piece=True)
                assert w.n["piece"] == pieces(name)

            def arrived(units):
                dve.wait_ge(unit_done, w.at("unit", units))
                b = w.at("block")
                return pair(w.n["block"] - 1)

            def kept(ins):
                ins.then_inc(block_saved, 1)
                dve.wait_ge(block_saved, w.now("block"))

            def four(x):
                return x.rearrange("p (s t) -> p s t", s=4)

            def two(x):
                return x.rearrange("p (n c) -> p n c", n=NT)

            at_unit = [behind_sparse.first]
            stored = [0]

            def catch_up(shadow):
                while stored[0] < shadow.complete(at_unit[0]) and shadow.blocks[stored[0]][1] is not None:
                    kind, dst = shadow.blocks[stored[0]]
                    x = arrived(4)
                    kept(copy(dst[:, :, :], four(x) if kind == "F" else two(x)))
                    stored[0] += 1

            def fill(shadow, k):
                catch_up(shadow)
                at_unit[0] = shadow.upto(at_unit[0], k)

            def turned_tokens(count, hi, lo, name):
                dve.wait_ge(tokens_turned, count)
                split_pieces(name, hi, lo, lambda q: four(ps[:, q * 1024:q * 1024 + 1024]))

            def softmax(s, heads, n, gate=None, floor=False, weight=None, src=None):
                src = s if src is None else src
                m, r = st[:, 0:heads], st[:, 16:16 + heads]
                link(dve.tensor_reduce(m, src, AX, ALU.max))
                if floor:
                    link(dve.tensor_scalar(m, m, NEG, None, ALU.max))
                to_act(tt(s, src, wide(m, n), ALU.subtract))
                if weight is not None:
                    link(tt(s, s, weight, ALU.mult))
                link(dve.tensor_reduce(r, s, AX, ALU.add))
                if floor:
                    link(dve.tensor_scalar(r, r, 1e-30, None, ALU.max))
                link(dve.reciprocal(r, r))
                if gate is not None:
                    link(tt(r, r, gate, ALU.mult))
                to_pe(tt(s, s, wide(r, n), ALU.mult))

            def chunks_summed(dst, x):
                return dve.tensor_reduce(dst, x.rearrange("p c t -> p t c"), AX, ALU.add)

            def statistics(cb, is_centred=False):
                a, s1, s2, t, c, rstd = (x[:, :] for x in (ln_a, ln_s1, ln_s2, ln_t, ln_c, ln_rstd))
                r = res[:, 4 * cb:4 * cb + 4, :]
                if cb == 0:
                    link(chunks_summed(a, r))
                    link(dve.tensor_scalar(a, a, 1.0 / CB, None, ALU.mult))
                if not is_centred:
                    tt(r, r, over(a, 4), ALU.subtract).then_inc(centred, 1)
                    dve.wait_ge(centred, w.at("centred"))
                if cb == 0:
                    link(chunks_summed(s1, r))
                else:
                    link(chunks_summed(t, r))
                    link(tt(s1, s1, t, ALU.add))
                if cb == NB - 1:
                    to_pe(dve.scalar_tensor_tensor(t, a, float(DC), s1, ALU.mult, ALU.add))
                    link(tt(rstd, s1, s1, ALU.mult))
                    link(dve.scalar_tensor_tensor(s2, rstd, -1.0 / DC, s2, ALU.mult, ALU.add))
                    from_pe()
                    link(tt(c, ps[:, PC:PC + T], a, ALU.subtract))
                    link(dve.scalar_tensor_tensor(rstd, s1, 1.0 / DC, c, ALU.mult, ALU.subtract))
                    link(tt(rstd, rstd, rstd, ALU.mult))
                    link(dve.scalar_tensor_tensor(s2, rstd, float(DC), s2, ALU.mult, ALU.add))
                dve.wait_ge(squares_done, w.at("squares"))
                if cb == 0:
                    link(chunks_summed(s2, ln_sq[:, :, :]))
                elif cb < NB - 1:
                    link(chunks_summed(t, ln_sq[:, :, :]))
                    link(tt(s2, s2, t, ALU.add))
                else:
                    link(chunks_summed(a, ln_sq[:, :, :]))
                    to_pe(tt(s2, s2, a, ALU.add))

            def prepare(cb):
                sl = slice(4 * cb, 4 * cb + 4)
                link(dve.tensor_scalar(res[:, sl, :], act_h[:, sl, :].bitcast(F32), ALPHA, None, ALU.mult))
                link(dve.scalar_tensor_tensor(res[:, sl, :], act_l[:, sl, :].bitcast(F32), ALPHA, res[:, sl, :],
                                              ALU.mult, ALU.add))

            def residuals(units, prepared=False, before_last=None):
                for cb in range(NB):
                    r = res[:, 4 * cb:4 * cb + 4, :]
                    if not prepared:
                        prepare(cb)
                    if cb and units[cb] > 1:
                        link(tt(r, r, over(ln_a[:, :], 4), ALU.subtract))
                    x = tt(r, r, four(arrived(units[cb])), ALU.add)
                    if cb and units[cb] > 1:
                        x.then_inc(centred, 1)
                        dve.wait_ge(centred, w.at("centred"))
                        dve.sem_inc(block_saved, 1)
                    else:
                        kept(x)
                    if cb == NB - 1 and before_last:
                        before_last()
                    statistics(cb, cb > 0 and units[cb] > 1)

            def norm(which, hi, lo, name):
                c, rstd = ln_c[:, :], ln_rstd[:, :]

                def less_mean(q):
                    r = res[:, 4 * q:4 * q + 4, :]
                    link(tt(r, r, over(c, 4), ALU.subtract))

                less_mean(0)
                from_pe()
                dve.tensor_scalar(rstd, ps[:, PC:PC + T], EPS, None, ALU.add).then_inc(shifted, 1)
                less_mean(1)
                dve.wait_ge(mapped, w.at("mapped"))
                link(dve.reciprocal(rstd, rstd))
                for q in range(4):
                    r = res[:, 4 * q:4 * q + 4, :]
                    if q > 1:
                        less_mean(q)
                    link(tt(r, r, over(rstd, 4), ALU.mult))
                    for c4 in range(4 * q, 4 * q + 4):
                        x = dve.tensor_scalar(res[:, c4, :], res[:, c4, :], col(f"ln_g{which}", c4), col(f"ln_b{which}", c4),
                                              ALU.mult, ALU.add)
                        if name == "y" and c4 % 4 == 3:
                            x.then_inc(piece_ready, 1)
                            w.at("piece")
                        elif c4 % 4 == 3:
                            link(x)
                        else:
                            x.then_inc(dve_step, 1)
                            w.at("step")
                    if name != "y":
                        split(hi[:, 4 * q:4 * q + 4, :], lo[:, 4 * q:4 * q + 4, :], r, piece=True)
                assert w.n["piece"] == pieces(name)

            dve.wait_ge(params_turned, 1)
            for t in range(5):
                x = copy(pcol[:, t, 0:ROW_N[t]], ps[:, t * P:t * P + ROW_N[t]])
                tell("turn_params", x) if t == 4 else link(x)
            from_pe()
            for h in range(8):
                x = copy(b_vec[:, h, :], ps[:, h * 512:h * 512 + SKEW])
                tell("bias", x) if h == 7 else link(x)
            turned_tokens(1, act_h, act_l, "x")

            kept(dve.tensor_scalar(n_q[:, :, :], four(arrived(4)), 0.125, None, ALU.mult))
            for half in range(2):
                dve.wait_ge(tokens_turned, 2 + half)
                x = copy(res[:, 8 * half:8 * half + 8, :], ps[:, 2048:4096].rearrange("p (s t) -> p s t", s=8))
                tell("memory_half", x) if half == 0 else link(x)
                statistics(2 * half)
                statistics(2 * half + 1)
            norm(1, alt_h, alt_l, "memory")
            x = arrived(4)
            link(copy(n_kv[:, 0:3, :], x[:, 0:768].rearrange("p (s t) -> p s t", s=3)))
            kept(copy(n_v[:, 0, :, :], two(x[:, 768:1024])))
            x = arrived(4)
            link(copy(n_kv[:, 3, :], x[:, 0:256]))
            link(copy(n_v[:, 1, :, :], two(x[:, 256:512])))
            kept(copy(n_gate[:, :, :], x[:, 512:640].rearrange("p (n c) -> p n c", n=2)[:, :, 0:24]))
            to_act(copy(n_gate[:, :, :], n_gate[:, :, :]))
            dve.wait_ge(small_in, 16 * SMALL["nsa"])
            for kv in range(2):
                for half in range(2):
                    src = n_kv[:, kv, 16 * half:16 * half + 240].rearrange("p (c l) -> p l c", l=16)
                    x = tt(n_win[:, kv, 16 * half:16 * half + 16, :], src,
                           n_pos[:, kv, 16 * half:16 * half + 16].unsqueeze(2).to_broadcast([P, 16, NCMP]), ALU.add)
                    to_pe(x) if kv + half == 2 else link(x)
            kept(dve.tensor_scalar(m_k[:, :, :], four(arrived(4)), 128 ** -0.5, None, ALU.mult))
            kept(copy(m_v[:, :, :], two(arrived(4))))
            fill(behind_sparse, 2)
            from_pe()
            link(copy(n_kc[:, 0:NCMP], ps[:, PC:PC + NCMP]))
            to_pe(copy(n_vc[0:NCMP, :, :], ps[0:NCMP, PC + 512:PC + 1536].rearrange("p (g e) -> p g e", g=2)[:, :, 0:64]))
            dve.wait_ge(kv_out, 32)
            for g in range(2):
                for qt in range(NT):
                    for br in range(3):
                        n = NCMP if br == 0 else P * (qt + 1)
                        dist = n_tab[:, 2 * P + 16 * qt:2 * P + 16 * qt + n] if br == 0 else n_tab[:, 2 * P - n:2 * P]
                        fill(behind_sparse, 3)
                        from_pe()
                        for j in range(4):
                            slope = 2.0 ** -(4 * g + j + 1)
                            link(dve.scalar_tensor_tensor(n_s[:, j, 0:n], dist, -slope, ps[:, PC + j * T:PC + j * T + n],
                                                          ALU.mult, ALU.add))
                        o = 12 * g + br
                        softmax(n_s[:, :, 0:n], 4, n, gate=n_gate[:, qt, o:o + 10:3], floor=br == 0)
                    from_pe()
                    o = two(ps[:, PO:PO + 256])
                    x = copy(mixed_in[:, 2 * g:2 * g + 2, qt * P:qt * P + P], o)
                    tell("nsa", x) if g + qt == 2 else link(x)

            catch_up(behind_sparse)
            assert stored[0] == FIRST_GATE - 5
            lb, e = col("lb", 0, 4), st[:, 0:4]
            to_act(tt(e, lb, lb, ALU.subtract))
            link(dve.reciprocal(st[:, 4:8], e))
            link(tt(e, e, st[:, 4:8], ALU.mult))
            link(tt(st[:, 8:12], e, e, ALU.subtract))
            link(dve.tensor_scalar(st[:, 12:16], st[:, 8:12], -1.0, 1.0, ALU.mult, ALU.add))
            to_act(copy(g_k[:, :, :], g_k[:, :, :]))
            for h in range(4):
                link(dve.tensor_scalar(g_k[:, h, :], g_k[:, h, :], st[:, 12 + h:13 + h], st[:, 8 + h:9 + h],
                                       ALU.mult, ALU.add))
            to_act(dve.tensor_scalar(g_k[:, :, :], g_k[:, :, :], 1e-6, None, ALU.max))
            link(dve.tensor_scalar(g_k[:, :, :], g_k[:, :, :], -1.0, 1.0, ALU.mult, ALU.add))
            link(copy(g_qh[:, :], g_q[:, :, :].rearrange("p h t -> p (h t)")))
            to_pe(copy(g_kh[:, :], g_k[:, :, :].rearrange("p h t -> p (h t)")))
            q = g_q[:, :, :].rearrange("p h t -> p (h t)")
            k = g_k[:, :, :].rearrange("p h t -> p (h t)")
            acc = g_a[:, :, :, :].rearrange("p h n t -> p (h n) t")
            blocks8 = ps[:, PC:PC + 1024].rearrange("p (b t) -> p b t", b=8)
            dve.wait_ge(small_in, 16 * SMALL["hgrn"])
            from_pe()
            link(tt(acc, blocks8, over(ident, 8), ALU.mult))
            for l in range(8):
                h = 1 << l

                def halves(x):
                    return x.rearrange("p (m two h) -> p m two h", two=2, h=h)

                pv, ev = halves(g_p[:, :]), halves(g_t[:, :])
                last = pv[:, :, 0, h - 1:h].to_broadcast([P, 512 // h, h])
                to_act(tt(ev[:, :, 0, :], last, pv[:, :, 0, :], ALU.subtract))
                link(tt(halves(g_qh[:, :])[:, :, 1, :], halves(q)[:, :, 1, :], ev[:, :, 1, :], ALU.mult))
                to_pe(tt(halves(g_kh[:, :])[:, :, 0, :], halves(k)[:, :, 0, :], ev[:, :, 0, :], ALU.mult))
                if l < 7:
                    link(tt(pv[:, :, 1, :], pv[:, :, 1, :], last, ALU.add))
                    from_pe()
                    t8 = g_t[:, :].rearrange("p (b t) -> p b t", b=8)
                    link(tt(t8, blocks8, over(g_mask[:, l, :], 8), ALU.mult))
                    link(tt(acc, acc, t8, ALU.add))
                else:
                    from_pe()
                    to_pe(copy(g_p[:, 0:512], ps[:, PC:PC + 512]))
            from_pe()
            x8 = g_t[:, :].rearrange("p (b t) -> p b t", b=8)
            to_act(copy(st[:, 16:17], st[:, 12:13]))
            link(dve.tensor_reduce(st[:, 0:8], x8, AX, ALU.add))
            to_act(dve.tensor_scalar(st[:, 0:8], st[:, 0:8], 1.0 / P, EPS, ALU.mult, ALU.add))
            link(dve.reciprocal(st[:, 0:8], st[:, 0:8]))
            link(tt(x8, blocks8, wide(st[:, 0:8], P), ALU.mult))
            o2 = two(g_t[:, :])
            to_act(tt(o2, o2, over(g_norm[:, :], NT), ALU.mult))
            to_pe(tt(o2, o2, g_g[:, :, :], ALU.mult))
            from_pe()
            split(alt_h[:, 0:4, :], alt_l[:, 0:4, :], mixed_in[:, 0:4, :], piece=True)
            split(alt_h[:, 4:8, :], alt_l[:, 4:8, :], four(ps[:, PC:PC + 1024]), piece=True)

            src = p_c
            for g in range(4):
                h = 1 << g
                dst = (p_a, p_b)[g % 2]
                link(tt(dst[:, g:4, h:T], src[:, g:4, h:T], src[:, g:4, 0:T - h], ALU.add))
                link(copy(dst[:, g:4, 0:h], src[:, g:4, 0:h]))
                src = dst
            link(copy(p_b[:, 0, :], p_a[:, 0, :]))
            link(copy(p_b[:, 2, :], p_a[:, 2, :]))
            dve.wait_ge(small_in, 16 * SMALL["pool"])
            link(tt(p_b[:, :, :], p_b[:, :, :], p_inv[:, :, :], ALU.mult))
            to_pe(tt(p_b[:, :, :], p_b[:, :, :], p_c[:, :, :], ALU.subtract))
            from_pe()
            for g in range(4):
                link(dve.tensor_scalar(p_a[:, g, :], ps[:, PC + g * T:PC + g * T + T], col("pool_scale", g), None, ALU.mult))
            split(alt_h[:, 8:12, :], alt_l[:, 8:12, :], p_a[:, :, :], piece=True)

            dve.wait_ge(small_in, 16 * SMALL["sgu"])
            to_act(copy(st[:, 16:17], s_v[:, 0, 0:1]))
            to_act(copy(st[:, 16:17], s_v[:, 0, 0:1]))
            for n in range(NT):
                link(dve.bn_stats(st[:, 64 + 6 * n:70 + 6 * n], s_v[:, n, :]))
                link(dve.bn_aggr(st[:, 40 + 2 * n:42 + 2 * n], st[:, 64 + 6 * n:70 + 6 * n]))
            to_act(dve.tensor_scalar(st[:, 32:34], st[:, 41:44:2], EPS, None, ALU.add))
            link(dve.reciprocal(st[:, 32:34], st[:, 32:34]))
            for n in range(NT):
                link(dve.tensor_scalar(s_v[:, n, :], s_v[:, n, :], st[:, 40 + 2 * n:41 + 2 * n], st[:, 32 + n:33 + n],
                                       ALU.subtract, ALU.mult))
            link(tt(s_v[:, :, :], s_v[:, :, :], over(s_g[:, :], NT), ALU.mult))
            to_pe(tt(s_v[:, :, :], s_v[:, :, :], over(s_b[:, :], NT), ALU.add))
            from_pe()
            to_pe(tt(s_wt[:, :, :], four(ps[:, PC:PC + 512]), over(tri, 4), ALU.mult))
            from_pe()
            vs = two(ps[:, PC:PC + 1024])
            for g in range(4):
                c = slice(g * P, g * P + P)
                x = dve.scalar_tensor_tensor(s_o[:, :, c], vs[:, :, c], col("sg_b", g), s_u[:, :, c], ALU.add, ALU.mult)
                to_pe(x) if g == 3 else link(x)
            from_pe()
            split(alt_h[:, 12:16, :], alt_l[:, 12:16, :], four(ps[:, PC:PC + 1024]), piece=True)

            dve.wait_ge(gate_done, 4 * NB)
            dve.sem_inc(block_saved, 4 * NB)
            w.at("block", 4 * NB)
            w.at("unit", BASE["merge"] - BASE["gates"])
            dve.sem_inc(merge_added, 2)
            w.at("added", 2)
            dve.wait_ge(gate_spilled, 16 * 4 * NB)
            link(dve.memset(res[:, :, :], 0.0))
            with dve.Fori(0, 4) as i, w.loop(i, 0, 4, {"unit": 4, "block": 4, "added": 4, "gates0": 32, "gates1": 32}):
                for cb in range(NB):
                    x = four(arrived(1))
                    dve.wait_ge(gate_loaded[cb % 2], w.at(f"gates{cb % 2}", 16))
                    kept(tt(m_t[:, :, :], x, four(m_g[:, cb % 2, :]), ALU.mult))
                    sl = slice(4 * cb, 4 * cb + 4)
                    tt(res[:, sl, :], res[:, sl, :], m_t[:, :, :], ALU.add).then_inc(merge_added, 1)
                    dve.wait_ge(merge_added, w.at("added"))
            split_pieces("mixed", alt_h, alt_l, lambda q: res[:, 4 * q:4 * q + 4, :])

            def ffn(conv):
                dve.sem_inc(silu_used, 1)
                w.at("conv")
                w.at("used")
                per = {"unit": 8, "silu": 1, "used": 1}
                if conv:
                    per |= {"conv": 1, "step": 7}
                with dve.Fori(0, FB) as i, w.loop(i, 0, FB, per):
                    w.at("unit", 8)
                    u = w.now("unit")
                    if conv:
                        dve.wait_ge(unit_done, u - 4)
                        gate = four(ps[:, 0:1024])

                        def tap(name):
                            t, r = ROW_AT[name]
                            return pcol[:, t, bass.ds(i * 4 + r, 4)]

                        link(tt(f_a[:, :, :], gate, wide(tap("cw2"), T), ALU.mult))
                        for j, s in ((1, 1), (0, 2)):
                            link(tt(f_b[:, :, 0:T - s], gate[:, :, 0:T - s], wide(tap(f"cw{j}"), T - s), ALU.mult))
                            link(tt(f_a[:, :, s:T], f_a[:, :, s:T], f_b[:, :, 0:T - s], ALU.add))
                        link(copy(st[:, 16:17], ident[:, 0:1]))
                        link(copy(st[:, 16:17], ident[:, 0:1]))
                        tt(f_a[:, :, :], f_a[:, :, :], wide(tap("cb"), T), ALU.add).then_inc(conv_done, 1)
                        dve.wait_ge(conv_done, w.at("conv"))
                    dve.wait_ge(unit_done, u)
                    dve.wait_ge(silu_done, w.at("silu"))
                    dve.tensor_tensor(hid[:, bass.ds(i * 4, 4), :], f_a[:, :, :], four(ps[:, 1024:2048]),
                                      ALU.mult).then_inc(silu_used, 1)
                    dve.wait_ge(silu_used, w.at("used"))

                def piece(k, parity, first):
                    w.at("unit", 4)
                    if not first:
                        dve.wait_ge(unit_done, w.now("unit") - 8)
                    src = hid[:, k, :] if isinstance(k, slice) else hid[:, bass.ds(k, 4), :]
                    dve.tensor_copy(f_h[:, parity], src).then_inc(dve_step, 1)
                    dve.wait_ge(dve_step, w.at("step"))
                    dve.tensor_tensor(f_l[:, parity], src, f_h[:, parity].bitcast(F32), ALU.subtract).then_inc(hidden_ready, 1)
                    w.at("hidden")

                piece(slice(0, 4), 0, True)
                piece(slice(4, 8), 1, True)
                with dve.Fori(0, 4) as i, w.loop(i, 0, 4, {"unit": 8, "hidden": 2, "step": 2}):
                    piece(i * 8 + 8, 0, False)
                    piece(i * 8 + 12, 1, False)
                piece(slice(40, 44), 0, False)
                dve.wait_ge(hidden_ready, w.now("hidden"))
                for sl in (slice(4 * q, 4 * q + 4) for q in range(NB)):
                    x = kept_x[:, sl, :]
                    link(tt(x, act_l[:, sl, :].bitcast(F32), act_h[:, sl, :].bitcast(F32), ALU.add))
                    link(dve.tensor_scalar(x, x, ALPHA, None, ALU.mult))
                for cb in range(NB):
                    dve.wait_ge(unit_done, w.now("unit") - 3 + cb)
                    sl = slice(4 * cb, 4 * cb + 4)
                    link(tt(res[:, sl, :], kept_x[:, sl, :], four(ps[:, cb * 1024:cb * 1024 + 1024]), ALU.add))
                    statistics(cb)

            residuals((4, 4, 4, 4))
            norm(0, act_h, act_l, "x1")
            for cb in range(NB):
                prepare(cb)
            kept(copy(x_q[:, :, :], four(arrived(4))))
            for qt in range(NT):
                from_pe()
                softmax(x_s[:, :, :], 4, T, src=four(ps[:, PC:PC + 1024]))
                from_pe()
                at = (slice(None), slice(0, 4), slice(qt * P, qt * P + P))
                split(alt_h[at], alt_l[at], four(ps[:, PO:PO + 512]), "xa" if qt else None)
            residuals((1, 1, 1, 1), True)
            dve.sem_inc(conv_done, 1)
            norm(2, act_h, act_l, "x2")
            ffn(True)
            norm(3, act_h, act_l, "x3")

            x = arrived(4)
            dve.wait_ge(small_in, 16 * SMALL["gates2"])
            kept(tt(l_gate[:, :, :], x[:, 0:128].rearrange("p (n c) -> p n c", n=2)[:, :, 0:8], over(l_gb[:, :], NT), ALU.add))
            f = l_gate[:, :, 4:8]
            link(dve.tensor_scalar(l_e[:, :, :], f, -1.0, None, ALU.mult))
            to_act(tt(l_e[:, :, :], l_e[:, :, :], f, ALU.min))
            to_act(dve.tensor_scalar(l_e[:, :, :], l_e[:, :, :], 1.0, None, ALU.add))
            link(dve.tensor_scalar(l_lf[:, :, :], f, 0.0, None, ALU.min))
            to_pe(tt(l_lf[:, :, :], l_lf[:, :, :], l_e[:, :, :], ALU.subtract))
            from_pe()
            link(copy(l_cum[:, :, :], ps[:, PC:PC + 8].rearrange("p (n h) -> p n h", n=2)))
            tell("gates2", tt(l_i[:, :, :], l_gate[:, :, 0:4], l_cum[:, :, :], ALU.subtract))
            for dst in l_in[0]:
                kept(copy(dst[:, :, :], (four if dst.shape[1] == 4 else two)(arrived(4))))
            at_unit[0], stored[0] = behind_lstm.first, 0
            for g in range(2):
                q, k, _, o = l_in[g]
                dve.wait_ge(small_in, 16 * SMALL[f"ml{g}"])
                fill(behind_lstm, LSTM_FILL[g][0])
                for part, x in enumerate((q, k)):
                    r = part * 8 + 4 * g

                    def tap(j):
                        return col(f"c2w{j}", r, 4)

                    link(tt(l_a[:, :, :], x[:, :, :], wide(tap(3), T), ALU.mult))
                    for j, s in ((2, 1), (1, 2), (0, 3)):
                        link(tt(l_b[:, :, 0:T - s], x[:, :, 0:T - s], wide(tap(j), T - s), ALU.mult))
                        link(tt(l_a[:, :, s:T], l_a[:, :, s:T], l_b[:, :, 0:T - s], ALU.add))
                    to_act(tt(l_a[:, :, :], l_a[:, :, :], wide(col("cb2", r, 4), T), ALU.add))
                to_act(copy(st[:, 16:17], ident[:, 0:1]))
                to_pe(dve.tensor_scalar(k[:, :, :], k[:, :, :], 1.0 / 16, None, ALU.mult))
                for qt in range(NT):
                    n = P * (qt + 1)
                    fill(behind_lstm, LSTM_FILL[g][1 + 2 * qt])
                    from_pe()
                    for j in range(2):
                        link(dve.scalar_tensor_tensor(l_s[:, j, 0:n], ps[:, PC + j * T:PC + j * T + n],
                                                      l_cum[:, qt, 2 * g + j:2 * g + j + 1], l_tab[:, 2 * P - n:2 * P],
                                                      ALU.add, ALU.add))
                    m = st[:, 0:2]
                    link(dve.tensor_reduce(m, l_s[:, :, 0:n], AX, ALU.max))
                    link(tt(m, m, l_cum[:, qt, 2 * g:2 * g + 2], ALU.max))
                    link(dve.tensor_scalar(st[:, 8:10], m, -1.0, None, ALU.mult))
                    to_act(tt(l_s[:, :, 0:n], l_s[:, :, 0:n], wide(m, n), ALU.subtract))
                    qk = ps[:, PC + 512:PC + 1024].rearrange("p (j t) -> p j t", j=2)[:, :, 0:n]
                    link(tt(l_s[:, :, 0:n], l_s[:, :, 0:n], qk, ALU.mult))
                    link(dve.tensor_reduce(st[:, 4:6], l_s[:, :, 0:n], AX, ALU.add))
                    link(dve.tensor_scalar(st[:, 6:8], st[:, 4:6], -1.0, None, ALU.mult))
                    link(tt(st[:, 4:6], st[:, 4:6], st[:, 6:8], ALU.max))
                    link(tt(st[:, 4:6], st[:, 4:6], st[:, 8:10], ALU.max))
                    link(dve.reciprocal(st[:, 4:6], st[:, 4:6]))
                    to_pe(tt(l_s[:, :, 0:n], l_s[:, :, 0:n], wide(st[:, 4:6], n), ALU.mult))
                    fill(behind_lstm, LSTM_FILL[g][2 + 2 * qt])
                    from_pe()
                    link(copy(l_h[:, :], ps[:, PO:PO + 512]))
                    for j in range(2):
                        link(dve.bn_stats(st[:, 64 + 6 * j:70 + 6 * j], l_h[:, j * T:j * T + T]))
                        link(dve.bn_aggr(st[:, 40 + 2 * j:42 + 2 * j], st[:, 64 + 6 * j:70 + 6 * j]))
                    to_act(dve.tensor_scalar(st[:, 32:34], st[:, 41:44:2], EPS, None, ALU.add))
                    link(dve.reciprocal(st[:, 32:34], st[:, 32:34]))
                    for j in range(2):
                        link(dve.tensor_scalar(l_h[:, j * T:j * T + T], l_h[:, j * T:j * T + T], st[:, 40 + 2 * j:41 + 2 * j],
                                               st[:, 32 + j:33 + j], ALU.subtract, ALU.mult))
                    link(tt(l_h[:, :], l_h[:, :], l_norm[:, :], ALU.mult))
                    to_pe(tt(l_h[:, :], l_h[:, :], o[:, qt, :], ALU.mult))
                    from_pe()
                    x = copy(mixed_in[:, 4 * g:4 * g + 4, qt * P:qt * P + P], four(ps[:, PT_:PT_ + 512]))
                    tell(f"ml{g}", x) if qt else link(x)
                catch_up(behind_lstm)
            for g in range(2):
                q, k, v = d_in[g]
                if g == 0:
                    fill(behind_lstm, 4)
                else:
                    catch_up(behind_lstm)
                to_pe(dve.tensor_scalar(q[:, :, :], q[:, :, :], 128 ** -0.5, None, ALU.mult))
                if g == 1:
                    for x in range(3):
                        c = slice(4 * x, 4 * x + 4)
                        split(alt_h[:, c, :], alt_l[:, c, :], mixed_in[:, c, :], piece=True)
                dve.wait_ge(small_in, 16 * SMALL[f"di{g}"])
                link(tt(d_bias[:, :, :], d_bias[:, :, :], over(d_tab[:, 1, :], 4), ALU.add))
                for qt in range(NT):
                    n = P * (qt + 1)
                    if g == 0:
                        fill(behind_lstm, 4)
                    from_pe()
                    link(tt(d_s[:, :, 0:n], four(ps[:, PC:PC + 1024])[:, :, 0:n], d_bias[:, :, T - n:T], ALU.add))
                    softmax(d_s[:, :, 0:n], 4, n, weight=over(d_tab[:, 0, T - n:T], 4))
                    from_pe()
                    x = copy(mixed_in[:, 8 + 4 * g:12 + 4 * g, qt * P:qt * P + P], four(ps[:, PO:PO + 512]))
                    tell("di0", x) if qt and not g else link(x)
            split(alt_h[:, 12:16, :], alt_l[:, 12:16, :], mixed_in[:, 12:16, :], piece=True)
            assert w.n["piece"] == pieces("mixed2")
            residuals((7, 1, 4, 4), before_last=lambda: turned_tokens(4, alt_h, alt_l, "mem2"))
            norm(4, act_h, act_l, "x4")
            def keys():
                kept(dve.tensor_scalar(x_k[:, :, :], four(arrived(4)), 512 ** -0.5, None, ALU.mult))

            def values_queries():
                kept(copy(x_v[:, :, :], two(arrived(4))))
                kept(copy(x_q[:, :, :], four(arrived(4))))

            def xb_piece(h):
                c = slice(4 * h, 4 * h + 4)
                split(alt_h[:, c, :], alt_l[:, c, :], res[:, c, :], piece=True)

            keys()
            values_queries()
            for head in range(4):
                from_pe()
                softmax(x_s[:, 0:2, :], 2, T, src=two(ps[:, PC:PC + 512]))
                if head < 3:
                    keys()
                else:
                    for h in range(3):
                        xb_piece(h)
                from_pe()
                link(copy(res[:, 4 * head:4 * head + 4, :], four(ps[:, PC:PC + 1024])))
                if head < 3:
                    values_queries()
            xb_piece(3)
            assert w.n["piece"] == pieces("xb")
            residuals((4, 4, 4, 4))
            norm(5, act_h, act_l, "x5")
            ffn(False)
            norm(6, None, None, "y")
            assert w.n["unit"] == UNITS


def kernel(**inputs):
    import concourse.bacc as bacc
    from concourse.bass_utils import run_bass_kernel_spmd

    nc = bacc.Bacc("TRN2", target_bir_lowering=False, num_devices=1)
    arrays, aps = {}, {}
    for name, value in inputs.items():
        v = np.ascontiguousarray(value)
        arrays[f"in_{name}"] = v
        aps[name] = nc.dram_tensor(f"in_{name}", v.shape, mybir.dt.from_np(v.dtype), kind="ExternalInput").ap()
    _, table = shape_tables()
    arrays["shape_tables"] = table
    tables = nc.dram_tensor("shape_tables", table.shape, F32, kind="ExternalInput").ap()
    out = nc.dram_tensor("out_x", (1, T, D), F32, kind="ExternalOutput").ap()
    two_blocks(nc, aps, tables, out)
    r = run_bass_kernel_spmd(nc, [arrays], core_ids=[0])
    return r.results[0]["out_x"]
```
